# Optimizing a Trainium2 kernel written in Bass

```python
import math
import jax, jax.numpy as jnp
from jax import lax
import numpy as np

D_MODEL = 1024
BATCH = 1
SEQ = 2048
DEPTH = 1

HEAD_DIM = 64
N_Q_HEADS = 16
N_KV_HEADS = 4
GROUP = N_Q_HEADS // N_KV_HEADS
ATTN_WIDTH = N_Q_HEADS * HEAD_DIM
KV_WIDTH = N_KV_HEADS * HEAD_DIM
WINDOW = 128
BLOCK = 128
ROT_DIM = HEAD_DIM // 4
ROPE_THETA = 500000.0
NEG_INF = -1e30
LRU_WIDTH = 1024
LRU_BLOCKS = 16
LRU_BLOCK_W = LRU_WIDTH // LRU_BLOCKS
CONV_W = 4
LRU_C = 8.0
MIX_WIDTH = ATTN_WIDTH + LRU_WIDTH
IN_DIM = ATTN_WIDTH + 2 * KV_WIDTH + ATTN_WIDTH + 2 * LRU_WIDTH
SPLITS = tuple(np.cumsum([ATTN_WIDTH, KV_WIDTH, KV_WIDTH, ATTN_WIDTH, LRU_WIDTH]).tolist())
EPS = 1e-6

kernel_name = "hymba_swa_sink_rglru_hybrid"

def rmsnorm(x, g):
    xf = x.astype(jnp.float32)
    y = xf * lax.rsqrt(jnp.mean(xf * xf, axis=-1, keepdims=True) + EPS)
    return (y * g.astype(jnp.float32)).astype(x.dtype)

def partial_rope(t, cos, sin):
    half = ROT_DIM // 2
    t1 = t[..., :half].astype(jnp.float32)
    t2 = t[..., half:ROT_DIM].astype(jnp.float32)
    rot = jnp.concatenate([t1 * cos - t2 * sin, t2 * cos + t1 * sin], axis=-1)
    return jnp.concatenate([rot.astype(t.dtype), t[..., ROT_DIM:]], axis=-1)

def swa_sink_attention(q, k, v, sinks):
    b, s = q.shape[0], q.shape[1]
    nb = s // BLOCK
    qb = q.reshape(b, nb, BLOCK, N_KV_HEADS, GROUP, HEAD_DIM)

    def with_prev(t):
        tb = t.reshape(b, nb, BLOCK, N_KV_HEADS, HEAD_DIM)
        prev = jnp.pad(tb, ((0, 0), (1, 0), (0, 0), (0, 0), (0, 0)))[:, :-1]
        return jnp.concatenate([prev, tb], axis=2)

    kc, vc = with_prev(k), with_prev(v)
    scores = jnp.einsum('bnqhgd,bnkhd->bnhgqk', qb, kc,
                        preferred_element_type=jnp.float32) * (HEAD_DIM ** -0.5)
    qi = jnp.arange(BLOCK)[:, None]
    kj = jnp.arange(2 * BLOCK)[None, :]
    diff = qi + BLOCK - kj
    band = (diff >= 0) & (diff < WINDOW)
    blk = jnp.arange(nb)[:, None, None]
    valid = band[None] & ((blk > 0) | (kj >= BLOCK)[None])
    scores = jnp.where(valid[None, :, None, None], scores, NEG_INF)
    sink = sinks.astype(jnp.float32).reshape(N_KV_HEADS, GROUP)[None, None, :, :, None, None]
    m = jnp.maximum(jnp.max(scores, axis=-1, keepdims=True), sink)
    p = jnp.exp(scores - m)
    denom = jnp.sum(p, axis=-1, keepdims=True) + jnp.exp(sink - m)
    o = jnp.einsum('bnhgqk,bnkhd->bnqhgd', p / denom, vc.astype(jnp.float32))
    return o.reshape(b, s, ATTN_WIDTH).astype(q.dtype)

def causal_depthwise_conv(x, w, bias):
    s = x.shape[1]
    xp = jnp.pad(x, ((0, 0), (CONV_W - 1, 0), (0, 0)))
    y = bias[None, None, :]
    for tap in range(CONV_W):
        y = y + xp[:, tap:tap + s] * w[tap][None, None, :]
    return y

def rg_lru(x, w_r, b_r, w_i, b_i, lam):
    b, s, _ = x.shape
    xf = x.astype(jnp.float32)
    xb = xf.reshape(b, s, LRU_BLOCKS, LRU_BLOCK_W)
    r = jax.nn.sigmoid(jnp.einsum('bsnc,ncd->bsnd', xb, w_r.astype(jnp.float32)).reshape(b, s, LRU_WIDTH)
                       + b_r.astype(jnp.float32))
    i = jax.nn.sigmoid(jnp.einsum('bsnc,ncd->bsnd', xb, w_i.astype(jnp.float32)).reshape(b, s, LRU_WIDTH)
                       + b_i.astype(jnp.float32))
    log_a = -LRU_C * r * jax.nn.softplus(-lam.astype(jnp.float32))
    a = jnp.exp(log_a)
    u = jnp.sqrt(-jnp.expm1(2.0 * log_a)) * (i * xf)

    def combine(left, right):
        a1, b1 = left
        a2, b2 = right
        return a1 * a2, a2 * b1 + b2

    _, h = lax.associative_scan(combine, (a, u), axis=1)
    return h.astype(x.dtype)

def setup_inputs(seed: int = 0) -> dict:
    key = jax.random.key(seed)
    ks = jax.random.split(key, 16)
    f32 = jnp.float32
    x = jax.random.normal(ks[0], (BATCH, SEQ, D_MODEL), f32)
    ln_gain = 1.0 + 0.02 * jax.random.normal(ks[1], (DEPTH, D_MODEL), f32)
    w_in = jax.random.normal(ks[2], (DEPTH, D_MODEL, IN_DIM), f32) * D_MODEL ** -0.5
    sinks = 0.5 * jax.random.normal(ks[3], (DEPTH, N_Q_HEADS), f32)
    conv_w = jax.random.normal(ks[4], (DEPTH, CONV_W, LRU_WIDTH), f32) * CONV_W ** -0.5
    conv_b = 0.02 * jax.random.normal(ks[5], (DEPTH, LRU_WIDTH), f32)
    w_rgate = jax.random.normal(ks[6], (DEPTH, LRU_BLOCKS, LRU_BLOCK_W, LRU_BLOCK_W), f32) * LRU_BLOCK_W ** -0.5
    b_rgate = 0.02 * jax.random.normal(ks[7], (DEPTH, LRU_WIDTH), f32)
    w_igate = jax.random.normal(ks[8], (DEPTH, LRU_BLOCKS, LRU_BLOCK_W, LRU_BLOCK_W), f32) * LRU_BLOCK_W ** -0.5
    b_igate = 0.02 * jax.random.normal(ks[9], (DEPTH, LRU_WIDTH), f32)
    a0 = jax.random.uniform(ks[10], (DEPTH, LRU_WIDTH), f32, 0.9, 0.999)
    sig = a0 ** (1.0 / LRU_C)
    lru_lambda = jnp.log(sig) - jnp.log1p(-sig)
    attn_out_gain = 1.0 + 0.02 * jax.random.normal(ks[11], (DEPTH, ATTN_WIDTH), f32)
    lru_out_gain = 1.0 + 0.02 * jax.random.normal(ks[12], (DEPTH, LRU_WIDTH), f32)
    w_out = jax.random.normal(ks[13], (DEPTH, MIX_WIDTH, D_MODEL), f32) * MIX_WIDTH ** -0.5
    final_gain = 1.0 + 0.02 * jax.random.normal(ks[14], (D_MODEL,), f32)
    return {"x": x, "ln_gain": ln_gain, "w_in": w_in, "sinks": sinks,
            "conv_w": conv_w, "conv_b": conv_b, "w_rgate": w_rgate, "b_rgate": b_rgate,
            "w_igate": w_igate, "b_igate": b_igate, "lru_lambda": lru_lambda,
            "attn_out_gain": attn_out_gain, "lru_out_gain": lru_out_gain,
            "w_out": w_out, "final_gain": final_gain}

def reference(x, ln_gain, w_in, sinks, conv_w, conv_b, w_rgate, b_rgate, w_igate, b_igate,
              lru_lambda, attn_out_gain, lru_out_gain, w_out, final_gain):
    b, s, _ = x.shape
    pos = jnp.arange(s, dtype=jnp.float32)
    inv_freq = ROPE_THETA ** (-jnp.arange(0, ROT_DIM, 2, dtype=jnp.float32) / ROT_DIM)
    ang = pos[:, None] * inv_freq[None, :]
    cos = jnp.cos(ang)[None, :, None, :]
    sin = jnp.sin(ang)[None, :, None, :]
    for l in range(DEPTH):
        h = rmsnorm(x, ln_gain[l])
        z = jnp.einsum('bsd,de->bse', h, w_in[l])
        q, k, v, g_attn, x_lru, g_lru = jnp.split(z, SPLITS, axis=-1)
        q = partial_rope(q.reshape(b, s, N_Q_HEADS, HEAD_DIM), cos, sin)
        k = partial_rope(k.reshape(b, s, N_KV_HEADS, HEAD_DIM), cos, sin)
        v = v.reshape(b, s, N_KV_HEADS, HEAD_DIM)
        y_attn = swa_sink_attention(q, k, v, sinks[l])
        y_attn = rmsnorm(y_attn * jax.nn.silu(g_attn), attn_out_gain[l])
        u = causal_depthwise_conv(x_lru, conv_w[l], conv_b[l])
        y_lru = rg_lru(u, w_rgate[l], b_rgate[l], w_igate[l], b_igate[l], lru_lambda[l])
        y_lru = rmsnorm(y_lru * jax.nn.silu(g_lru), lru_out_gain[l])
        y = jnp.einsum('bse,ed->bsd', jnp.concatenate([y_attn, y_lru], axis=-1), w_out[l])
        x = x + y
    return rmsnorm(x, final_gain)


_drawn_inputs = setup_inputs


def setup_inputs(seed=0):
    import zlib

    import numpy as np

    out = dict(_drawn_inputs(seed))
    spreads = {}
    factors = {'sinks': 8.0,
     'b_rgate': 8.0,
     'b_igate': 8.0,
     'attn_out_gain': 5.649,
     'lru_out_gain': 5.897,
     'final_gain': 2.871}
    for name, (base, spread) in spreads.items():
        noise = np.random.default_rng([zlib.crc32(name.encode()), seed]).standard_normal(out[name].shape)
        drawn = base * np.exp(spread * noise) if base else spread * noise
        out[name] = __import__('jax').numpy.asarray(drawn.astype(out[name].dtype))
    for name, factor in factors.items():
        out[name] = (out[name] * factor).astype(out[name].dtype)
    return out
```

```python
from contextlib import ExitStack

import numpy as np

import concourse.bass as bass
from concourse import mybir

F32 = mybir.dt.float32
F32R = mybir.dt.float32r
BF16 = mybir.dt.bfloat16
U8 = mybir.dt.uint8
ALU = mybir.AluOpType
ACT = mybir.ActivationFunctionType
AXX = mybir.AxisListType.X

P = 128
SEQ, D = 2048, 1024
KC = D // P
HD = 64
KV, GQ = 4, 4
BLK = 128
ROT = HD // 4
T = 512
NBLK = T // BLK
NQUART = SEQ // T
NITER = NQUART * KV
LRU_W = 1024
UNITS = LRU_W // P // KV
BW = 64
EPS = 1e-6
MIX = 2048
EC = MIX // P
NTOK = SEQ // P
CONV = 4
BIG = 3.0e38
NEG = -1.0e30

COL_Q, COL_K, COL_V = 0, 1024, 1024 + KV * HD
COL_GA = COL_V + KV * HD
COL_XL = COL_GA + 1024
COL_GL = COL_XL + LRU_W

XL0, GL0, XL1, GA0, GA1, GL1, KVG, Q0, Q1 = range(9)
NG = 9
WSLOTS = 3
(R_XL0, R_GL0, R_XL1, R_R0, R_I0, R_GA0, R_R1, R_I1, R_GA1, R_XT0, R_XT1, R_GL1, R_KV, R_Q0, R_Q1,
 R_VT) = range(16)
NR = 16
RING = 4
RING_OF_GROUP = [R_XL0, R_GL0, R_XL1, R_GA0, R_GA1, R_GL1, R_KV, R_Q0, R_Q1]
FREED_BY_DVE = [R_GL0, R_GA0, R_GA1, R_XT0, R_XT1, R_GL1]
FREED_BY_ACT = [r for r in range(NR) if r not in FREED_BY_DVE]

(C_W0, C_W1, C_W2, C_W3, C_CB, C_BR, C_BI, C_LAM, C_NEG4SP, C_POS4SP, C_T0, C_T1, C_T2) = range(13)
NPRM = 13


SWAP = [(i + ROT // 2) % ROT if i < ROT else i for i in range(32)]


class Signal:

    def __init__(self, ctx, nc, name, per, unit=1, lead=1, ahead=0):
        self.sem = ctx.enter_context(nc.semaphore(name))
        self.name, self.per, self.unit, self.lead, self.count = name, per, unit, lead, 0
        self.prime = (lead * per - ahead) * unit
        self.ahead = ahead

    def at(self, n, k):
        return self.sem, n * (self.per * self.unit) + (self.lead * self.per + k) * self.unit

    def one(self):
        self.count += 1
        return self.sem, self.unit

    def checked(self, bodies, beyond=0):
        assert self.count == bodies * self.per + self.ahead + beyond, (self.name, self.count, self.per)


def hymba_kernel(nc, x, ln_gain, w_in, sinks, conv_w, conv_b, w_rgate, b_rgate, w_igate, b_igate,
                 lru_lambda, attn_out_gain, lru_out_gain, w_out, final_gain,
                 rope_cos, rope_sin, first_cap, identity, out):
    y_dram = nc.dram_tensor("y_scratch", (EC, P, SEQ), F32, kind="Internal").ap()
    sq_dram = nc.dram_tensor("sq_scratch", (P, 2, SEQ), F32, kind="Internal").ap()

    with ExitStack() as top:
        ident = top.enter_context(nc.sbuf_tensor("ident", [P, P], F32))

        phase_a(nc, x, ln_gain, w_in, sinks, conv_w, conv_b, w_rgate, b_rgate, w_igate, b_igate,
                lru_lambda, rope_cos, rope_sin, first_cap, identity, y_dram, sq_dram, ident)
        phase_b(nc, x, attn_out_gain, lru_out_gain, w_out, final_gain, y_dram, sq_dram, out)


def phase_a(nc, x, ln_gain, w_in, sinks, conv_w, conv_b, w_rgate, b_rgate, w_igate, b_igate,
            lru_lambda, rope_cos, rope_sin, first_cap, identity, y_dram, sq_dram, ident):
    with ExitStack() as ctx:
        signals = []

        def sb(name, shape, dt=F32):
            return ctx.enter_context(nc.sbuf_tensor(name, shape, dt))

        def sem(name):
            return ctx.enter_context(nc.semaphore(name))

        def signal(name, per, unit=1, ahead=0):
            s = Signal(ctx, nc, name, per, unit, lead=2, ahead=ahead)
            signals.append(s)
            return s

        h_hi = sb("h_hi", [P, 2, KC, T], F32R)
        h_lo = sb("h_lo", [P, 2, KC, T], F32R)
        w_raw = sb("w_raw", [P, WSLOTS, KC, P])
        w_hi = sb("w_hi", [P, WSLOTS, KC, P], F32R)
        w_lo = sb("w_lo", [P, WSLOTS, KC, P], F32R)
        xb = sb("xb", [P, D])
        gain_row = sb("gain_row", [P, D])
        xs = sb("x_stat", [P, 4])
        acc = sb("acc", [P, 2, T])
        cosT = sb("cosT", [P, T])
        sinT = sb("sinT", [P, T])
        prev_mask = sb("prev_mask", [P, GQ, BLK], U8)
        cap = sb("cap", [P, 2, BLK])
        sink_all = sb("sink_all", [P, KV * GQ])
        prm = sb("prm", [P, LRU_W // P, NPRM])
        kraw = sb("kraw", [P, T])
        swp = sb("swp", [P, T])
        krot = sb("krot", [HD, BLK + T])
        k_hi = sb("k_hi", [P, BLK + T], F32R)
        k_lo = sb("k_lo", [P, BLK + T], F32R)
        kc_ol = sb("kc_ol", [P, KV, BLK])
        k_carry, o_low = kc_ol[0:HD], kc_ol[HD:]
        vraw = sb("vraw", [P, 1 + NBLK, HD])
        v_hl = sb("v_hl", [P, 1 + NBLK, 2 * HD], F32R)
        dvraw = sb("dvraw", [P, NBLK, HD])
        dv_hl = sb("dv_hl", [P, NBLK, 2 * HD], F32R)
        v_carry = sb("v_carry", [P, KV, HD])
        qraw = sb("qraw", [P, T])
        qrot = sb("qrot", [P, T])
        q_st = sb("q_st", [P, GQ, T], F32R)
        s_sb = sb("s_sb", [P, 2, GQ, BLK])
        smax = sb("smax", [P, 2, 4, GQ])
        sden = sb("sden", [P, 2, 4, GQ])
        p_hi = sb("p_hi", [P, GQ, BLK], F32R)
        p_lo = sb("p_lo", [P, GQ, BLK], F32R)
        p_hi_c = sb("p_hi_c", [P, GQ, BLK], F32R)
        p_lo_c = sb("p_lo_c", [P, GQ, BLK], F32R)
        o_sb = sb("o_sb", [P, 2, BLK])
        ya = sb("ya", [P, 2, T])
        sq = sb("sq", [P, T])
        xl = [sb(f"xl{u}", [P, CONV - 1 + T]) for u in range(UNITS)]
        cu = [sb(f"cu{u}", [P, T]) for u in range(UNITS)]
        u_hi = sb("u_hi", [P, T], F32R)
        u_lo = sb("u_lo", [P, T], F32R)
        ra = [sb(f"ra{u}", [P, T]) for u in range(UNITS)]
        a2 = sb("a2", [P, T])
        ri = [sb(f"ri{u}", [P, T]) for u in range(UNITS)]
        gl = [sb(f"gl{u}", [P, T]) for u in range(UNITS)]
        hs = [sb(f"hs{u}", [P, T]) for u in range(UNITS)]
        x_carry = sb("x_carry", [P, LRU_W // P, CONV - 1])
        h_carry = sb("h_carry", [P, LRU_W // P, 1])
        gw_raw = sb("gw_raw", [P, UNITS, 2, P])
        gw_hi = sb("gw_hi", [P, UNITS, 2, P], F32R)
        gw_lo = sb("gw_lo", [P, UNITS, 2, P], F32R)

        ring = ctx.enter_context(nc.psum_tensor("ring", [P, RING, T], F32))
        ps_s = ctx.enter_context(nc.psum_tensor("ps_s", [P, GQ, 2 * BLK], F32))
        ps_t = ctx.enter_context(nc.psum_tensor("ps_t", [P, GQ, BLK], F32))
        ps_v = ctx.enter_context(nc.psum_tensor("ps_v", [P, GQ, BLK], F32))

        primed = sem("primed")
        consts_in = sem("consts_in")
        zeroed = sem("zeroed")
        prm_step = sem("prm_step")
        prm_act = sem("prm_act")
        pro_x_in, pro_sq, pro_ms, pro_root, pro_rs, pro_norm, pro_T, pro_hi, pro_lo = (
            Signal(ctx, nc, "pro_" + s, k, u) for s, k, u in (
                ("x_in", 1, 16), ("sq", 1, 1), ("ms", 1, 1), ("root", 1, 1), ("rs", 1, 1),
                ("norm", 1, 1), ("T", 2, 1), ("hi", 2, 1), ("lo", 2, 1)))
        pro = [pro_x_in, pro_sq, pro_ms, pro_root, pro_rs, pro_norm, pro_T, pro_hi, pro_lo]
        table_in = sem("table_in")
        settled = sem("settled")

        w_in_dma = [signal(f"w_in_dma{s}", 4 if s == 0 else 3, 16, ahead=2 if s == 0 else 1)
                    for s in range(WSLOTS)]
        W_DMA_AT = {XL0: 1, GL0: 1, XL1: 1, GA0: 2, GA1: 2, GL1: 2, KVG: 4, Q0: 3, Q1: 3}
        w_high = signal("w_high", NG, ahead=3)
        w_low = signal("w_low", NG, ahead=3)
        ring_ready = signal("ring_ready", NR, ahead=4)
        ring_act = signal("ring_act", len(FREED_BY_ACT), ahead=4)
        ring_dve = signal("ring_dve", len(FREED_BY_DVE))
        x_in = signal("x_in", 1, 16)
        x_sq = signal("x_sq", 1)
        x_ms = signal("x_ms", 1)
        x_root = signal("x_root", 1)
        x_rs = signal("x_rs", 1)
        x_norm = signal("x_norm", 1)
        h_high = signal("h_high", 2)
        k_turn = signal("k_turn", 3, ahead=3)
        k_sin = signal("k_sin", 1, ahead=1)
        k_rot = signal("k_rot", 1, ahead=1)
        k_high = signal("k_high", 2, ahead=2)
        k_low = signal("k_low", 3, ahead=3)
        q_turn = signal("q_turn", 4, ahead=4)
        q_sin = signal("q_sin", 2, ahead=2)
        q_rot = signal("q_rot", 2, ahead=2)
        q_high = signal("q_high", 4, ahead=4)
        q_low = signal("q_low", 4, ahead=4)
        v_prev = signal("v_prev", 1, ahead=1)
        v_high = signal("v_high", 1, ahead=1)
        v_low = signal("v_low", 1, ahead=1)
        dv_raw = signal("dv_raw", 1, ahead=1)
        dv_high = signal("dv_high", 1, ahead=1)
        dv_low = signal("dv_low", 1, ahead=1)
        v_kept = signal("v_kept", 1, ahead=1)
        scores = signal("scores", NBLK)
        s_cur = signal("s_cur", NBLK)
        s_sel = signal("s_sel", NBLK)
        s_cap = signal("s_cap", 1)
        s_stat = signal("s_stat", 4 * NBLK)
        p_exp = signal("p_exp", NBLK * (GQ + 1))
        p_den = signal("p_den", 2 * NBLK)
        p_norm = signal("p_norm", NBLK)
        p_T = signal("p_T", NBLK)
        p_high = signal("p_high", NBLK)
        p_low = signal("p_low", NBLK)
        p_cur = signal("p_cur", 2 * NBLK)
        pv = signal("pv", NBLK)
        o_lowdone = signal("o_lowdone", NBLK)
        o_sum = signal("o_sum", 2 * NBLK)
        ga_tanh = signal("ga_tanh", 2)
        ya_done = signal("ya_done", NBLK)
        ya_out = signal("ya_out", 1, 16)
        sq_made = signal("sq_made", 4)
        sq_added = signal("sq_added", 4)
        xl_prev = signal("xl_prev", UNITS)
        xl_in = signal("xl_in", UNITS)
        u_conv = signal("u_conv", 3 * UNITS)
        xl_kept = signal("xl_kept", UNITS)
        u_high = signal("u_high", UNITS)
        u_low = signal("u_low", UNITS)
        gw_dma = signal("gw_dma", 4, 16)
        gw_high = signal("gw_high", 1)
        gw_low = signal("gw_low", 1)
        decay = signal("decay", 3 * UNITS)
        one_minus = signal("one_minus", UNITS)
        root = signal("root", UNITS)
        i_x = signal("i_x", UNITS)
        scan_in = signal("scan_in", UNITS)
        scanned = signal("scanned", UNITS)
        h_kept = signal("h_kept", UNITS)
        gl_tanh = signal("gl_tanh", UNITS)
        yl_done = signal("yl_done", UNITS)
        yl_out = [signal(f"yl_out{u}", 1, 16) for u in range(UNITS)]
        acc_out = sem("acc_out")
        acc_zero = sem("acc_zero")

        bank = lambda r: ring[:, r % RING, :]
        f = lambda ap: ap.bitcast(F32)

        def bank_free(n, r):
            before = (r - RING) % NR
            late = 0 if r >= RING else 1
            if before in FREED_BY_ACT:
                return ring_act.at(n, FREED_BY_ACT.index(before) + 1 - late * len(FREED_BY_ACT))
            return ring_dve.at(n, FREED_BY_DVE.index(before) + 1 - late * len(FREED_BY_DVE))

        def iterations(eng, body, quarter_start=None, quarter_end=None):
            with eng.Fori(0, NQUART // 2) as qp:
                for par in range(2):
                    if quarter_start:
                        quarter_start(qp, par)
                    eng.sem_inc(settled, 1)
                    with eng.Fori(0, KV - 1) as g:
                        body(qp * (2 * KV) + (g + par * KV), g, par, qp, g + 1, par)
                    eng.sem_inc(settled, 1)
                    body(qp * (2 * KV) + (KV - 1 + par * KV), KV - 1, par, qp, 0, 1 - par)
                    if quarter_end:
                        quarter_end(qp, par)
                        eng.sem_inc(settled, 1)

        N_CONST = 12
        block = ctx.enter_context(nc.Block())

        @block.sync
        def _(sp):
            chan = lambda v: v.rearrange("o (u p) -> p (o u)", p=P)
            sp.dma_start(ident[:, :], identity).then_inc(consts_in, 16)
            sp.dma_start(gain_row[:, :], ln_gain.broadcast_to([P, D])).then_inc(consts_in, 16)
            sp.dma_start(sink_all[:, :], sinks.broadcast_to([P, KV * GQ])).then_inc(consts_in, 16)
            with nc.allow_non_contiguous_dma(reason="per-channel parameters, a few KB once"):
                for i in range(CONV):
                    sp.dma_start(prm[:, :, C_W0 + i], conv_w[0, i:i + 1, :].rearrange(
                        "o (u p) -> p (o u)", p=P)).then_inc(consts_in, 16)
                for col, v in ((C_CB, conv_b), (C_BR, b_rgate), (C_BI, b_igate), (C_LAM, lru_lambda)):
                    sp.dma_start(prm[:, :, col], chan(v)).then_inc(consts_in, 16)
            sp.dma_start(cap[:, :, :], first_cap).then_inc(consts_in, 16)
            sp.wait_ge(primed, 1)
            sp.wait_ge(zeroed, 7)
            def load_group(n, i, col):
                sp.wait_ge(*w_low.at(n, i + 1 - WSLOTS))
                sp.dma_start(w_raw[:, i % WSLOTS, :, :],
                             w_in[0, :, bass.ds(col, P)].rearrange("(k p) c -> p k c", p=P)
                             ).then_inc(*w_in_dma[i % WSLOTS].one())

            def load_next(n, g):
                sp.wait_ge(*w_low.at(n, KVG + 1 - WSLOTS))
                for half, col in ((0, COL_K), (1, COL_V)):
                    sp.dma_start(w_raw[:, 0, :, half * HD:(half + 1) * HD],
                                 w_in[0, :, bass.ds(g * HD + col, HD)].rearrange("(k p) c -> p k c", p=P)
                                 ).then_inc(*w_in_dma[0].one())
                load_group(n, Q0, g * (2 * P) + COL_Q)
                load_group(n, Q1, g * (2 * P) + (COL_Q + P))

            def load_tables(col):
                sp.dma_start(cosT[:, :], rope_cos[:, bass.ds(col, T)]).then_inc(table_in, 16)
                sp.dma_start(sinT[:, :], rope_sin[:, bass.ds(col, T)]).then_inc(table_in, 16)

            load_next(-1, 0)
            load_tables(0)
            with sp.Fori(0, NBLK) as b:
                sp.wait_ge(*pro_T.at(b, 0))
                sp.dma_start(xb[:, :], x[0, bass.ds(b * P, P), :]).then_inc(*pro_x_in.one())
            sp.wait_ge(*pro_T.at(NBLK - 1, 2))

            def body(n, g, par, qp, following, nxt_par):
                load_group(n, XL0, g * (2 * P) + COL_XL)
                load_group(n, GL0, g * (2 * P) + COL_GL)
                sp.wait_ge(*ring_ready.at(n, R_XT1 + 1 - NR))
                first = (qp * (2 * KV) + (g + KV)) if par == 0 else (g + 2 * KV)
                sp.dma_start(xb[:, :], x[0, bass.ds(first * P, P), :]).then_inc(*x_in.one())
                load_group(n, XL1, g * (2 * P) + (COL_XL + P))
                sp.wait_ge(*gw_low.at(n, 0))
                for j, w in enumerate((w_rgate, w_igate)):
                    for half in range(2):
                        rows = slice(half * BW, (half + 1) * BW)
                        sp.dma_start(gw_raw[rows, :, j, rows],
                                     w[0, bass.ds(g * (2 * UNITS), 2 * UNITS), :, :].rearrange(
                                         "(u h) c d -> c h u d", h=2)[:, half, :, :]
                                     ).then_inc(*gw_dma.one())
                if nxt_par != par:
                    sp.wait_ge(*q_rot.at(n, 0))
                    load_tables((qp * 2 + 1) * T if par == 0 else 2 * T)
                load_group(n, GA0, g * (2 * P) + COL_GA)
                load_group(n, GA1, g * (2 * P) + (COL_GA + P))
                load_group(n, GL1, g * (2 * P) + (COL_GL + P))
                load_next(n, following)

            iterations(sp, body)
            for s in range(WSLOTS):
                sp.wait_ge(*w_low.at(NITER, s + 1 - WSLOTS))
                sp.sem_inc(w_in_dma[s].sem, w_in_dma[s].per * 16)

        @block.gpsimd
        def _(pool):
            for s in signals + pro:
                pool.sem_inc(s.sem, s.prime)
            pool.sem_inc(primed, 1)
            for ap in (k_carry, v_carry[:, :, :], x_carry[:, :, :], h_carry[:, :, :], gw_raw[:, :, :, :]):
                nc.gpsimd.memset(ap, 0.0).then_inc(zeroed, 1)

            nc.gpsimd.memset(acc[:, :, :], 0.0).then_inc(acc_zero, 1)
            pool.wait_ge(acc_zero, 1)
            pool.dma_start(sq_dram[:, :, 0:T], acc[:, :, :]).then_inc(acc_out, 16)

            def quarter_start(qp, par):
                q = qp * 2 + par
                pool.wait_ge(acc_out, q * 16 + 16)
                pool.sem_inc(settled, 1)
                nc.gpsimd.memset(acc[:, :, :], 0.0).then_inc(acc_zero, 1)
                pool.wait_ge(acc_zero, q + 2)

            def add_square(n, i, y, which, ready):
                pool.wait_ge(*ready)
                pool.wait_ge(*sq_added.at(n, i))
                nc.gpsimd.tensor_tensor(sq[:, :], y, y, ALU.mult).then_inc(*sq_made.one())
                pool.wait_ge(*sq_made.at(n, i + 1))
                nc.gpsimd.tensor_tensor(acc[:, which, :], acc[:, which, :], sq[:, :], ALU.add
                                        ).then_inc(*sq_added.one())

            def lru_tail(n, u):
                pool.wait_ge(*root.at(n, u + 1))
                pool.wait_ge(*i_x.at(n, u + 1))
                nc.gpsimd.tensor_tensor(ri[u][:, :], ri[u][:, :], hs[u][:, :], ALU.mult
                                        ).then_inc(*scan_in.one())

            def p_current(n, b):
                for k, (src, dst, ready) in enumerate(((p_hi, p_hi_c, p_high), (p_lo, p_lo_c, p_low))):
                    pool.wait_ge(*ready.at(n, b + 1))
                    if k == 0:
                        pool.wait_ge(*pv.at(n, b))
                    pool.sem_inc(settled, 1)
                    nc.gpsimd.affine_select(out=dst[:, :, :], in_=f(src[:, :, :]), compare_op=ALU.is_ge,
                                            fill=0.0, base=0, pattern=[[0, GQ], [1, BLK]],
                                            channel_multiplier=-1).then_inc(*p_cur.one())

            def sine_k(n):
                pool.wait_ge(*k_turn.at(n, 2))
                nc.gpsimd.tensor_tensor(swp[0:HD, :], swp[0:HD, :], sinT[0:HD, :], ALU.mult
                                        ).then_inc(*k_sin.one())

            def sine_q(n, j):
                pool.wait_ge(*q_turn.at(n, 2 * j + 2))
                nc.gpsimd.tensor_tensor(swp[:, :], swp[:, :], sinT[:, :], ALU.mult
                                        ).then_inc(*q_sin.one())

            def body(n, g, par, qp, following, nxt_par):
                lru_tail(n, 0)
                lru_tail(n, 1)
                lru_gate(n, 0)
                p_current(n, 0)
                p_current(n, 1)
                if nxt_par != par:
                    pool.wait_ge(table_in, (qp * 2 + par + 2) * 32)
                sine_k(n)
                p_current(n, 2)
                lru_gate(n, 1)
                sine_q(n, 0)
                p_current(n, 3)
                sine_q(n, 1)
                attention_squares(n)

            def attention_squares(n):
                pool.wait_ge(*ya_done.at(n, NBLK))
                for j in range(2):
                    add_square(n, 2 + j, ya[:, j, :], 0, ya_done.at(n, NBLK))

            def lru_gate(n, u):
                pool.wait_ge(*h_kept.at(n, u + 1))
                pool.wait_ge(*ring_dve.at(n, FREED_BY_DVE.index((R_GL0, R_GL1)[u]) + 1))
                nc.gpsimd.tensor_tensor(hs[u][:, :], hs[u][:, :], gl[u][:, :], ALU.mult
                                        ).then_inc(*yl_done.one())
                add_square(n, u, hs[u][:, :], 1, yl_done.at(n, u + 1))

            def quarter_end(qp, par):
                n0 = qp * (2 * KV) + (par + 1) * KV
                q = qp * 2 + par
                pool.wait_ge(*sq_added.at(n0, 0))
                pool.sem_inc(settled, 1)
                pool.dma_start(sq_dram[:, :, bass.ds(q * T, T)], acc[:, :, :]).then_inc(acc_out, 16)

            pool.wait_ge(table_in, 32)
            sine_k(-1)
            sine_q(-1, 0)
            sine_q(-1, 1)
            iterations(pool, body, quarter_start, quarter_end)
            pool.wait_ge(acc_out, NQUART * 16 + 16)

        @block.scalar
        def _(act):
            def split_w(n, i):
                m, i = (n, i) if i < NG else (n + 1, i - NG)
                s = i % WSLOTS
                act.wait_ge(*w_in_dma[s].at(m, W_DMA_AT[i]))
                prev = i - WSLOTS
                act.wait_ge(*ring_ready.at(m, RING_OF_GROUP[prev] + 1 - (NR if prev < 0 else 0)))
                nc.scalar.activation(w_hi[:, s, :, :], w_raw[:, s, :, :], ACT.Copy
                                     ).then_inc(*w_high.one())

            act.wait_ge(consts_in, N_CONST * 16)
            act.wait_ge(prm_step, 1)
            nc.scalar.activation(prm[:, :, C_T1], prm[:, :, C_T0], ACT.Exp).then_inc(prm_act, 1)
            act.wait_ge(prm_step, 2)
            nc.scalar.activation(prm[:, :, C_T2], prm[:, :, C_T0], ACT.Ln).then_inc(prm_act, 1)
            act.wait_ge(primed, 1)

            def square_x(n, xin, xsq, free):
                act.wait_ge(*xin)
                act.wait_ge(*free)
                nc.scalar.activation(a2[:, :].bitcast(BF16), xb[:, :], ACT.Square, accum_out=xs[:, 0:1]
                                     ).then_inc(*xsq.one())

            def root_x(n, xms, xroot):
                act.wait_ge(*xms)
                nc.scalar.activation(xs[:, 2:3], xs[:, 1:2], ACT.Sqrt).then_inc(*xroot.one())

            def high_x(dst, col, half, ps, ready, done):
                act.wait_ge(*ready)
                act.sem_inc(settled, 1)
                nc.scalar.activation(dst[:, half * 4:half * 4 + 4, bass.ds(col, P)],
                                     ps.rearrange("p (k t) -> p k t", k=4), ACT.Copy).then_inc(*done)

            for i in range(KVG, NG):
                split_w(-1, i)
            with act.Fori(0, NBLK) as b:
                square_x(b, pro_x_in.at(b, 1), pro_sq, pro_norm.at(b, 0))
                root_x(b, pro_ms.at(b, 1), pro_root)
                for half in range(2):
                    high_x(h_hi[:, 0], b * P, half, ring[:, half, :], pro_T.at(b, half + 1),
                           pro_hi.one())
            def take_kv(n):
                act.wait_ge(*ring_ready.at(n, R_KV + 1))
                act.wait_ge(*ring_ready.at(n, R_VT + 1 - NR))
                act.wait_ge(*k_rot.at(n, 0))
                nc.scalar.activation(kraw[:, :], bank(R_KV), ACT.Copy).then_inc(*ring_act.one())

            def take_q(n, j):
                act.wait_ge(*ring_ready.at(n, (R_Q0, R_Q1)[j] + 1))
                act.wait_ge(*q_turn.at(n, 2 * j))
                nc.scalar.activation(qraw[:, :], bank((R_Q0, R_Q1)[j]), ACT.Copy).then_inc(*ring_act.one())

            def high_k(n):
                act.wait_ge(*k_rot.at(n, 1))
                act.wait_ge(*scores.at(n, NBLK))
                for half in range(2):
                    nc.scalar.activation(k_hi[half * HD:(half + 1) * HD, :], krot[:, :], ACT.Copy
                                         ).then_inc(*k_high.one())

            def high_q(n, j):
                act.wait_ge(*q_rot.at(n, j + 1))
                act.wait_ge(*scores.at(n, NBLK))
                for half in range(2):
                    rows = slice(half * HD, (half + 1) * HD)
                    nc.scalar.activation(q_st[rows, 2 * j + half, :], qrot[rows, :], ACT.Copy
                                         ).then_inc(*q_high.one())

            def take_v(n):
                act.wait_ge(*ring_ready.at(n, R_VT + 1))
                act.wait_ge(*v_kept.at(n, 0))
                nc.scalar.activation(vraw[:, 1:, :], bank(R_VT).rearrange("p (b c) -> p b c", c=P)[:, :, HD:],
                                     ACT.Copy).then_inc(*ring_act.one())

            def high_v(n):
                act.wait_ge(*v_prev.at(n, 1))
                act.wait_ge(*ring_act.at(n, FREED_BY_ACT.index(R_VT) + 1))
                act.wait_ge(*pv.at(n, NBLK))
                nc.scalar.activation(v_hl[:, :, 0:HD], vraw[:, :, :], ACT.Copy).then_inc(*v_high.one())
                act.wait_ge(*dv_raw.at(n, 1))
                nc.scalar.activation(dv_hl[:, :, 0:HD], dvraw[:, :, :], ACT.Copy).then_inc(*dv_high.one())

            take_kv(-1)
            split_w(-1, NG + XL0)
            take_q(-1, 0)
            high_k(-1)
            split_w(-1, NG + GL0)
            take_q(-1, 1)
            high_q(-1, 0)
            split_w(-1, NG + XL1)
            take_v(-1)
            high_q(-1, 1)
            high_v(-1)

            def body(n, g, par, qp, following, nxt_par):
                def gate_a(j):
                    act.wait_ge(*ring_ready.at(n, (R_GA0, R_GA1)[j] + 1))
                    if j == 0:
                        act.wait_ge(*ya_out.at(n, 0))
                        act.wait_ge(*sq_made.at(n, 0))
                    nc.scalar.activation(ya[:, j, :], bank((R_GA0, R_GA1)[j]), ACT.Tanh, scale=0.5
                                         ).then_inc(*ga_tanh.one())

                def s_copy(b):
                    act.wait_ge(*scores.at(n, b + 1))
                    act.wait_ge(*p_T.at(n, b - 1))
                    nc.scalar.activation(s_sb[:, b % 2], ps_s[:, :, BLK:], ACT.Copy).then_inc(*s_cur.one())

                def s_exp(b):
                    act.wait_ge(*s_stat.at(n, 4 * b + 4))
                    for h in range(GQ):
                        nc.scalar.activation(s_sb[:, b % 2, h, :], s_sb[:, b % 2, h, :], ACT.Exp,
                                             bias=smax[:, b % 2, 2, h:h + 1], scale=HD ** -0.5,
                                             accum_out=sden[:, b % 2, 0, h:h + 1]).then_inc(*p_exp.one())
                    nc.scalar.activation(sden[:, b % 2, 1, :], smax[:, b % 2, 3, :], ACT.Exp
                                         ).then_inc(*p_exp.one())

                def high_p(b):
                    act.wait_ge(*p_T.at(n, b + 1))
                    act.wait_ge(*pv.at(n, b))
                    act.wait_ge(*p_cur.at(n, 2 * b))
                    nc.scalar.activation(p_hi[:, :, :], ps_t[:, :, :], ACT.Copy).then_inc(*p_high.one())

                def low_o(b):
                    act.wait_ge(*pv.at(n, b + 1))
                    act.wait_ge(*o_sum.at(n, 2 * b))
                    nc.scalar.activation(o_low, ps_v[HD:, :, :], ACT.Copy
                                         ).then_inc(*o_lowdone.one())

                def lru_in(u):
                    r = (R_XL0, R_XL1)[u]
                    G = g * UNITS + u
                    act.wait_ge(*ring_ready.at(n, r + 1))
                    act.wait_ge(*xl_kept.at(n, u + 1 - UNITS))
                    act.wait_ge(*i_x.at(n, u + 1 - UNITS))
                    nc.scalar.activation(xl[u][:, CONV - 1:], bank(r), ACT.Copy).then_inc(*xl_in.one())
                    act.sem_inc(settled, 1)
                    nc.scalar.activation(cu[u][:, :], bank(r), ACT.Identity,
                                         scale=prm[:, G, C_W3:C_W3 + 1], bias=prm[:, G, C_CB:C_CB + 1]
                                         ).then_inc(*ring_act.one())

                def high_u(u):
                    act.wait_ge(*u_conv.at(n, 3 * u + 3))
                    act.wait_ge(*ring_ready.at(n, R_I0 + 1 if u else R_I1 + 1 - NR))
                    nc.scalar.activation(u_hi[:, :], cu[u][:, :], ACT.Copy).then_inc(*u_high.one())

                def gate_l(u):
                    act.wait_ge(*ring_ready.at(n, (R_GL0, R_GL1)[u] + 1))
                    act.wait_ge(*yl_done.at(n, u + 1 - UNITS))
                    nc.scalar.activation(gl[u][:, :], bank((R_GL0, R_GL1)[u]), ACT.Tanh, scale=0.5
                                         ).then_inc(*gl_tanh.one())

                def decays(u):
                    G = g * UNITS + u
                    act.wait_ge(*ring_ready.at(n, (R_R0, R_R1)[u] + 1))
                    act.wait_ge(*scanned.at(n, u + 1 - UNITS))
                    act.sem_inc(settled, 1)
                    nc.scalar.activation(ra[u][:, :], bank((R_R0, R_R1)[u]), ACT.Tanh, scale=0.5,
                                         bias=prm[:, G, C_BR:C_BR + 1]).then_inc(*ring_act.one())
                    act.wait_ge(*ring_act.at(n, FREED_BY_ACT.index((R_R0, R_R1)[u]) + 1))
                    act.wait_ge(*sq_made.at(n, u + 1 - 4))
                    act.wait_ge(*yl_out[u].at(n, 0))
                    act.sem_inc(settled, 1)
                    nc.scalar.activation(hs[u][:, :], ra[u][:, :], ACT.Tanh, scale=prm[:, G, C_POS4SP:C_POS4SP + 1],
                                         bias=prm[:, G, C_POS4SP:C_POS4SP + 1]).then_inc(*decay.one())
                    nc.scalar.activation(ra[u][:, :], ra[u][:, :], ACT.Exp, scale=prm[:, G, C_NEG4SP:C_NEG4SP + 1],
                                         bias=prm[:, G, C_NEG4SP:C_NEG4SP + 1]).then_inc(*decay.one())
                    act.wait_ge(*decay.at(n, 3 * u + 2))
                    act.wait_ge(*one_minus.at(n, u))
                    act.wait_ge(*x_sq.at(n, 1))
                    nc.scalar.activation(a2[:, :], ra[u][:, :], ACT.Square).then_inc(*decay.one())
                    act.wait_ge(*ring_ready.at(n, (R_I0, R_I1)[u] + 1))
                    act.sem_inc(settled, 1)
                    nc.scalar.activation(ri[u][:, :], bank((R_I0, R_I1)[u]), ACT.Tanh, scale=0.5,
                                         bias=prm[:, G, C_BI:C_BI + 1]).then_inc(*ring_act.one())

                def lru_root(u):
                    act.wait_ge(*one_minus.at(n, u + 1))
                    nc.scalar.activation(hs[u][:, :], hs[u][:, :], ACT.Sqrt).then_inc(*root.one())

                lru_in(0)
                split_w(n, GA0)
                act.wait_ge(*gw_dma.at(n, 4))
                act.wait_ge(*ring_ready.at(n, R_I1 + 1 - NR))
                nc.scalar.activation(gw_hi[:, :, :, :], gw_raw[:, :, :, :], ACT.Copy).then_inc(*gw_high.one())
                high_u(0)
                gate_l(0)
                split_w(n, GA1)
                act.wait_ge(*one_minus.at(n, 0))
                square_x(n, x_in.at(n, 1), x_sq, x_norm.at(n, 0))
                lru_in(1)
                s_copy(0)
                decays(0)
                high_u(1)
                split_w(n, GL1)
                s_exp(0)
                gate_a(0)
                decays(1)
                s_copy(1)
                root_x(n, x_ms.at(n, 1), x_root)
                lru_root(0)
                lru_root(1)
                split_w(n, KVG)
                s_exp(1)
                gate_a(1)
                high_p(0)
                s_copy(2)
                for half in range(2):
                    high_x(h_hi[:, 1 - par], g * P, half, bank(R_XT0 + half),
                           ring_ready.at(n, R_XT0 + half + 1), h_high.one())
                split_w(n, Q0)
                s_exp(2)
                gate_l(1)
                low_o(0)
                high_p(1)
                s_copy(3)
                split_w(n, Q1)
                s_exp(3)
                take_kv(n)
                low_o(1)
                high_p(2)
                split_w(n, NG + XL0)
                high_k(n)
                take_q(n, 0)
                low_o(2)
                high_p(3)
                split_w(n, NG + GL0)
                high_q(n, 0)
                take_q(n, 1)
                low_o(3)
                take_v(n)
                split_w(n, NG + XL1)
                high_q(n, 1)
                high_v(n)
                write_out(n, g, par, qp)

            def write_out(n, g, par, qp):
                q = qp * 2 + par
                act.wait_ge(*ya_done.at(n, NBLK))
                for_dst = y_dram[bass.ds(g * 2, 2), :, bass.ds(q * T, T)].rearrange("e p t -> p e t")
                act.dma_start(for_dst, ya[:, :, :]).then_inc(*ya_out.one())
                for u in range(UNITS):
                    act.wait_ge(*yl_done.at(n, u + 1))
                    act.dma_start(y_dram[bass.ds(g * UNITS + (EC // 2 + u), 1), :, bass.ds(q * T, T)].rearrange(
                        "e p t -> p (e t)"), hs[u][:, :]).then_inc(*yl_out[u].one())

            iterations(act, body)
            act.wait_ge(*ya_out.at(NITER, 0))
            for u in range(UNITS):
                act.wait_ge(*yl_out[u].at(NITER, 0))

        @block.vector
        def _(dve):
            stt = nc.vector.scalar_tensor_tensor

            def split_w(n, i):
                m, i = (n, i) if i < NG else (n + 1, i - NG)
                s = i % WSLOTS
                dve.wait_ge(*w_high.at(m, i + 1))
                nc.vector.tensor_tensor(w_lo[:, s, :, :], w_raw[:, s, :, :], f(w_hi[:, s, :, :]),
                                        ALU.subtract).then_inc(*w_low.one())

            dve.wait_ge(consts_in, N_CONST * 16)
            col = lambda c: prm[:, :, c]
            step = [0]

            def done(ins):
                step[0] += 1
                ins.then_inc(prm_step, 1)
                dve.wait_ge(prm_step, step[0])

            nc.vector.tensor_scalar(prev_mask[:, :, :], cap[:, 0, :].unsqueeze(1).broadcast_to([P, GQ, BLK]),
                                    0.0, None, ALU.is_lt).then_inc(zeroed, 1)
            nc.vector.tensor_scalar(col(C_T1), col(C_LAM), -1.0, None, ALU.mult).then_inc(zeroed, 1)
            dve.wait_ge(zeroed, 7)
            done(nc.vector.tensor_tensor(col(C_T0), col(C_LAM), col(C_T1), ALU.min))
            dve.wait_ge(prm_act, 1)
            done(nc.vector.tensor_scalar(col(C_T0), col(C_T1), 1.0, None, ALU.add))
            dve.wait_ge(prm_act, 2)
            done(nc.vector.tensor_scalar(col(C_POS4SP), col(C_T0), 1.0, None, ALU.is_equal))
            done(nc.vector.tensor_scalar(col(C_T0), col(C_T0), -1.0, None, ALU.add))
            done(nc.vector.tensor_tensor(col(C_T0), col(C_T0), col(C_POS4SP), ALU.add))
            done(nc.vector.reciprocal(col(C_NEG4SP), col(C_T0)))
            done(nc.vector.tensor_tensor(col(C_T2), col(C_T2), col(C_NEG4SP), ALU.mult))
            done(nc.vector.tensor_tensor(col(C_T2), col(C_T2), col(C_POS4SP), ALU.add))
            done(nc.vector.tensor_tensor(col(C_T2), col(C_T2), col(C_T1), ALU.mult))
            done(nc.vector.tensor_scalar(col(C_T0), col(C_LAM), -1.0, 0.0, ALU.mult, ALU.max))
            done(nc.vector.tensor_tensor(col(C_T2), col(C_T2), col(C_T0), ALU.add))
            done(nc.vector.tensor_scalar(col(C_POS4SP), col(C_T2), 4.0, None, ALU.mult))
            done(nc.vector.tensor_scalar(col(C_NEG4SP), col(C_T2), -4.0, None, ALU.mult))
            done(nc.vector.tensor_scalar(col(C_BR), col(C_BR), 0.5, None, ALU.mult))
            done(nc.vector.tensor_scalar(col(C_BI), col(C_BI), 0.5, None, ALU.mult))
            dve.wait_ge(primed, 1)

            def stat_x(sq_in, xms):
                dve.wait_ge(*sq_in)
                nc.vector.tensor_scalar(xs[:, 1:2], xs[:, 0:1], 1.0 / D, EPS, ALU.mult, ALU.add
                                        ).then_inc(*xms.one())

            def norm_x(n, root_in, xrs, xnorm):
                dve.wait_ge(*root_in)
                nc.vector.reciprocal(xs[:, 3:4], xs[:, 2:3]).then_inc(*xrs.one())
                dve.wait_ge(*xrs.at(n, 1))
                stt(out=xb[:, :], in0=xb[:, :], scalar=xs[:, 3:4], in1=gain_row[:, :], op0=ALU.mult,
                    op1=ALU.mult).then_inc(*xnorm.one())

            def low_x(dst, hi, col, half, ps, ready, done):
                dve.wait_ge(*ready)
                at = (slice(None), slice(half * 4, half * 4 + 4), bass.ds(col, P))
                nc.vector.tensor_tensor(dst[at], ps.rearrange("p (k t) -> p k t", k=4), f(hi[at]),
                                        ALU.subtract).then_inc(*done)

            for i in range(KVG, NG):
                split_w(-1, i)
            with dve.Fori(0, NBLK) as b:
                stat_x(pro_sq.at(b, 1), pro_ms)
                norm_x(b, pro_root.at(b, 1), pro_rs, pro_norm)
                for half in range(2):
                    low_x(h_lo[:, 0], h_hi[:, 0], b * P, half, ring[:, half, :], pro_hi.at(b, half + 1),
                          pro_lo.one())
            def turn_k(n, g):
                dve.wait_ge(*k_high.at(n, 0))
                dve.wait_ge(*k_low.at(n, 0))
                nc.vector.tensor_scalar(krot[:, 0:BLK], k_carry[:, g, :], 1.0, None, ALU.mult
                                        ).then_inc(*k_turn.one())
                dve.wait_ge(*ring_act.at(n, FREED_BY_ACT.index(R_KV) + 1))
                dve.wait_ge(*q_rot.at(n, 0))
                dve.sem_inc(settled, 1)
                nc.vector.stream_shuffle(swp[0:HD, :], kraw[0:HD, :], SWAP).then_inc(*k_turn.one())
                nc.vector.tensor_tensor(krot[:, BLK:], kraw[0:HD, :], cosT[0:HD, :], ALU.mult
                                        ).then_inc(*k_turn.one())

            def add_k(n):
                dve.wait_ge(*k_turn.at(n, 3))
                dve.wait_ge(*k_sin.at(n, 1))
                nc.vector.tensor_tensor(krot[:, BLK:], krot[:, BLK:], swp[0:HD, :], ALU.add
                                        ).then_inc(*k_rot.one())

            def low_k(n, g):
                dve.wait_ge(*k_high.at(n, 2))
                nc.vector.tensor_tensor(k_lo[0:HD, :], krot[:, :], f(k_hi[0:HD, :]), ALU.subtract
                                        ).then_inc(*k_low.one())
                dve.wait_ge(*k_low.at(n, 1))
                nc.vector.tensor_copy(k_lo[HD:, :], k_lo[0:HD, :]).then_inc(*k_low.one())
                nc.vector.tensor_scalar(k_carry[:, g, :], krot[:, T:], 1.0, None, ALU.mult
                                        ).then_inc(*k_low.one())

            def turn_q(n, j):
                dve.wait_ge(*ring_act.at(n, FREED_BY_ACT.index((R_Q0, R_Q1)[j]) + 1))
                dve.wait_ge(*q_low.at(n, 2 * j))
                dve.wait_ge(*q_high.at(n, 2 * j))
                dve.wait_ge(*(q_rot.at(n, j) if j else k_rot.at(n, 1)))
                nc.vector.tensor_tensor(qrot[:, :], qraw[:, :], cosT[:, :], ALU.mult
                                        ).then_inc(*q_turn.one())
                nc.vector.stream_shuffle(swp[:, :], qraw[:, :], SWAP).then_inc(*q_turn.one())

            def add_q(n, j):
                dve.wait_ge(*q_turn.at(n, 2 * j + 1))
                dve.wait_ge(*q_sin.at(n, j + 1))
                nc.vector.tensor_tensor(qrot[:, :], qrot[:, :], swp[:, :], ALU.add
                                        ).then_inc(*q_rot.one())

            def low_q(n, j):
                for half in range(2):
                    rows = slice(half * HD, (half + 1) * HD)
                    other = slice((1 - half) * HD, (2 - half) * HD)
                    dve.wait_ge(*q_high.at(n, 2 * j + half + 1))
                    nc.vector.tensor_tensor(q_st[other, 2 * j + half, :], qrot[rows, :],
                                            f(q_st[rows, 2 * j + half, :]), ALU.subtract
                                            ).then_inc(*q_low.one())

            def previous_v(n, g):
                dve.wait_ge(*v_high.at(n, 0))
                dve.wait_ge(*v_kept.at(n, 0))
                nc.vector.tensor_scalar(vraw[:, 0, :], v_carry[:, g, :], 1.0, None, ALU.mult
                                        ).then_inc(*v_prev.one())

            def differ_v(n):
                dve.wait_ge(*v_prev.at(n, 1))
                dve.wait_ge(*ring_act.at(n, FREED_BY_ACT.index(R_VT) + 1))
                dve.wait_ge(*dv_low.at(n, 0))
                nc.vector.tensor_tensor(dvraw[:, :, :], vraw[:, 1:, :], vraw[:, :NBLK, :], ALU.subtract
                                        ).then_inc(*dv_raw.one())

            def low_v(n, g):
                dve.wait_ge(*v_high.at(n, 1))
                nc.vector.tensor_tensor(v_hl[:, :, HD:], vraw[:, :, :], f(v_hl[:, :, 0:HD]), ALU.subtract
                                        ).then_inc(*v_low.one())
                nc.vector.tensor_scalar(v_carry[:, g, :], vraw[:, NBLK, :], 1.0, None, ALU.mult
                                        ).then_inc(*v_kept.one())
                dve.wait_ge(*dv_high.at(n, 1))
                nc.vector.tensor_tensor(dv_hl[:, :, HD:], dvraw[:, :, :], f(dv_hl[:, :, 0:HD]),
                                        ALU.subtract).then_inc(*dv_low.one())

            dve.wait_ge(table_in, 32)
            turn_k(-1, 0)
            split_w(-1, NG + XL0)
            add_k(-1)
            low_k(-1, 0)
            turn_q(-1, 0)
            split_w(-1, NG + GL0)
            add_q(-1, 0)
            low_q(-1, 0)
            turn_q(-1, 1)
            previous_v(-1, 0)
            split_w(-1, NG + XL1)
            add_q(-1, 1)
            low_q(-1, 1)
            differ_v(-1)
            low_v(-1, 0)

            def body(n, g, par, qp, following, nxt_par):
                def silu_a(j):
                    dve.wait_ge(*ga_tanh.at(n, j + 1))
                    stt(out=ya[:, j, :], in0=ya[:, j, :], scalar=1.0, in1=bank((R_GA0, R_GA1)[j]),
                        op0=ALU.add, op1=ALU.mult).then_inc(*ring_dve.one())

                def softmax_a(b):
                    s, t = s_sb[:, b % 2], smax[:, b % 2]
                    dve.wait_ge(*s_cur.at(n, b + 1))
                    dve.sem_inc(settled, 1)
                    nc.vector.copy_predicated(s, prev_mask[:, :, :], ps_s[:, :, 0:BLK]
                                              ).then_inc(*s_sel.one())
                    dve.wait_ge(*s_sel.at(n, b + 1))
                    if b == 0:
                        if par == 0:
                            nc.vector.tensor_tensor(s, s, cap[:, qp, :].unsqueeze(1).broadcast_to([P, GQ, BLK]), ALU.min).then_inc(*s_cap.one())
                        else:
                            dve.sem_inc(s_cap.sem, 1)
                        dve.wait_ge(*s_cap.at(n, 1))
                    nc.vector.tensor_reduce(out=t[:, 0, :], in_=s, op=ALU.max, axis=AXX
                                            ).then_inc(*s_stat.one())
                    dve.wait_ge(*s_stat.at(n, 4 * b + 1))
                    sink = sink_all[:, bass.ds(g * GQ, GQ)]
                    stt(out=t[:, 1, :], in0=t[:, 0, :], scalar=HD ** -0.5, in1=sink, op0=ALU.mult,
                        op1=ALU.max).then_inc(*s_stat.one())
                    dve.wait_ge(*s_stat.at(n, 4 * b + 2))
                    nc.vector.tensor_scalar(t[:, 2, :], t[:, 1, :], -1.0, None, ALU.mult
                                            ).then_inc(*s_stat.one())
                    nc.vector.tensor_tensor(t[:, 3, :], sink, t[:, 1, :], ALU.subtract
                                            ).then_inc(*s_stat.one())

                def softmax_b(b):
                    d = sden[:, b % 2]
                    dve.wait_ge(*p_exp.at(n, (GQ + 1) * (b + 1)))
                    nc.vector.tensor_tensor(d[:, 2, :], d[:, 0, :], d[:, 1, :], ALU.add
                                            ).then_inc(*p_den.one())
                    dve.wait_ge(*p_den.at(n, 2 * b + 1))
                    nc.vector.reciprocal(d[:, 3, :], d[:, 2, :]).then_inc(*p_den.one())
                    dve.wait_ge(*p_den.at(n, 2 * b + 2))
                    nc.vector.tensor_tensor(s_sb[:, b % 2], s_sb[:, b % 2],
                                            d[:, 3, :].unsqueeze(2).broadcast_to([P, GQ, BLK]), ALU.mult
                                            ).then_inc(*p_norm.one())

                def low_p(b):
                    dve.wait_ge(*p_high.at(n, b + 1))
                    nc.vector.tensor_tensor(p_lo[:, :, :], ps_t[:, :, :], f(p_hi[:, :, :]), ALU.subtract
                                            ).then_inc(*p_low.one())

                def gather_o(b):
                    dve.wait_ge(*o_lowdone.at(n, b + 1))
                    dve.wait_ge(*ya_done.at(n, b))
                    pair = lambda ap, s: ap.rearrange("p (j s) t -> p s j t", s=2)[:, s]
                    for s in range(2):
                        nc.vector.tensor_tensor(o_sb[s * HD:(s + 1) * HD, :, :], pair(ps_v[0:HD], s),
                                                pair(o_low, s), ALU.add).then_inc(*o_sum.one())
                    dve.wait_ge(*o_sum.at(n, 2 * b + 2))
                    if b == 0:
                        dve.wait_ge(*ring_dve.at(n, FREED_BY_DVE.index(R_GA1) + 1))
                    y = ya[:, :, b * BLK:(b + 1) * BLK]
                    nc.vector.tensor_tensor(y, y, o_sb[:, :, :], ALU.mult).then_inc(*ya_done.one())

                def conv(u):
                    G = g * UNITS + u
                    dve.wait_ge(*u_conv.at(n, 3 * u + 3 - 3 * UNITS))
                    dve.wait_ge(*xl_kept.at(n, u + 1 - UNITS))
                    nc.vector.tensor_scalar(xl[u][:, 0:CONV - 1], x_carry[:, G, :], 1.0, None, ALU.mult
                                            ).then_inc(*xl_prev.one())
                    dve.wait_ge(*xl_prev.at(n, u + 1))
                    dve.wait_ge(*ring_act.at(n, FREED_BY_ACT.index((R_XL0, R_XL1)[u]) + 1))
                    for i in range(3):
                        tap = 2 - i
                        if i:
                            dve.wait_ge(*u_conv.at(n, 3 * u + i))
                        stt(out=cu[u][:, :], in0=xl[u][:, tap:tap + T],
                            scalar=prm[:, G, C_W0 + tap:C_W0 + tap + 1], in1=cu[u][:, :], op0=ALU.mult,
                            op1=ALU.add).then_inc(*u_conv.one())
                    nc.vector.tensor_scalar(x_carry[:, G, :], xl[u][:, T:], 1.0, None, ALU.mult
                                            ).then_inc(*xl_kept.one())

                def low_u(u):
                    dve.wait_ge(*u_high.at(n, u + 1))
                    nc.vector.tensor_tensor(u_lo[:, :], cu[u][:, :], f(u_hi[:, :]), ALU.subtract
                                            ).then_inc(*u_low.one())

                def silu_l(u):
                    dve.wait_ge(*gl_tanh.at(n, u + 1))
                    stt(out=gl[u][:, :], in0=gl[u][:, :], scalar=1.0, in1=bank((R_GL0, R_GL1)[u]),
                        op0=ALU.add, op1=ALU.mult).then_inc(*ring_dve.one())

                def lru_mid(u):
                    dve.wait_ge(*decay.at(n, 3 * u + 3))
                    stt(out=hs[u][:, :], in0=a2[:, :], scalar=1.0, in1=hs[u][:, :], op0=ALU.add,
                        op1=ALU.mult).then_inc(*one_minus.one())
                    dve.wait_ge(*ring_act.at(n, FREED_BY_ACT.index((R_I0, R_I1)[u]) + 1))
                    stt(out=ri[u][:, :], in0=ri[u][:, :], scalar=1.0, in1=cu[u][:, :], op0=ALU.add,
                        op1=ALU.mult).then_inc(*i_x.one())

                def lru_scan(u):
                    G = g * UNITS + u
                    dve.wait_ge(*scan_in.at(n, u + 1))
                    dve.wait_ge(*h_kept.at(n, u))
                    dve.wait_ge(*one_minus.at(n, u + 1))
                    nc.vector.tensor_tensor_scan(hs[u][:, :], ra[u][:, :], ri[u][:, :], h_carry[:, G, :],
                                                 ALU.mult, ALU.add).then_inc(*scanned.one())
                    dve.wait_ge(*scanned.at(n, u + 1))
                    nc.vector.tensor_scalar(h_carry[:, G, :], hs[u][:, T - 1:], 1.0, None, ALU.mult
                                            ).then_inc(*h_kept.one())

                conv(0)
                split_w(n, GA0)
                dve.wait_ge(*gw_high.at(n, 1))
                nc.vector.tensor_tensor(gw_lo[:, :, :, :], gw_raw[:, :, :, :], f(gw_hi[:, :, :, :]),
                                        ALU.subtract).then_inc(*gw_low.one())
                low_u(0)
                silu_l(0)
                split_w(n, GA1)
                stat_x(x_sq.at(n, 1), x_ms)
                conv(1)
                softmax_a(0)
                low_u(1)
                lru_mid(0)
                split_w(n, GL1)
                softmax_b(0)
                silu_a(0)
                lru_mid(1)
                softmax_a(1)
                norm_x(n, x_root.at(n, 1), x_rs, x_norm)
                lru_scan(0)
                split_w(n, KVG)
                lru_scan(1)
                softmax_b(1)
                silu_a(1)
                low_p(0)
                softmax_a(2)
                for half in range(2):
                    low_x(h_lo[:, 1 - par], h_hi[:, 1 - par], g * P, half, bank(R_XT0 + half),
                          h_high.at(n, half + 1), ring_dve.one())
                split_w(n, Q0)
                softmax_b(2)
                silu_l(1)
                gather_o(0)
                low_p(1)
                softmax_a(3)
                split_w(n, Q1)
                softmax_b(3)
                if nxt_par != par:
                    dve.wait_ge(table_in, (qp * 2 + par + 2) * 32)
                turn_k(n, following)
                gather_o(1)
                low_p(2)
                add_k(n)
                split_w(n, NG + XL0)
                low_k(n, following)
                turn_q(n, 0)
                gather_o(2)
                low_p(3)
                add_q(n, 0)
                split_w(n, NG + GL0)
                low_q(n, 0)
                turn_q(n, 1)
                previous_v(n, following)
                gather_o(3)
                add_q(n, 1)
                split_w(n, NG + XL1)
                low_q(n, 1)
                differ_v(n)
                low_v(n, following)

            iterations(dve, body)

        @block.tensor
        def _(pe):
            mm = nc.tensor.matmul
            passes = ((w_hi, h_hi), (w_hi, h_lo), (w_lo, h_hi))
            with pe.Fori(0, NBLK) as b:
                pe.wait_ge(*pro_norm.at(b, 1))
                for half in range(2):
                    pe.wait_ge(*pro_lo.at(b, half - 1))
                    for k in range(4):
                        c = half * 4 + k
                        last = nc.tensor.transpose(ring[:, half, k * P:(k + 1) * P],
                                                   xb[:, c * P:(c + 1) * P], ident[:, :])
                    last.then_inc(*pro_T.one())
            pe.wait_ge(*pro_lo.at(NBLK - 1, 2))

            def project(n, i, par):
                r = RING_OF_GROUP[i]
                pe.wait_ge(*w_low.at(n, i + 1))
                pe.wait_ge(*bank_free(n, r))
                for k in range(KC):
                    for j, (w, h) in enumerate(passes):
                        last = mm(bank(r), w[:, i % WSLOTS, k, :], h[:, par, k, :],
                                  start=(k == 0 and j == 0), stop=(k == KC - 1 and j == 2))
                last.then_inc(*ring_ready.one())

            def turn_v(n):
                pe.wait_ge(*ring_act.at(n, FREED_BY_ACT.index(R_KV) + 1))
                pe.wait_ge(*bank_free(n, R_VT))
                for b in range(NBLK):
                    last = nc.tensor.transpose(bank(R_VT)[:, b * P:(b + 1) * P],
                                               kraw[:, b * P:(b + 1) * P], ident[:, :])
                last.then_inc(*ring_ready.one())

            for i in range(KVG, NG):
                project(-1, i, 0)
            turn_v(-1)

            def body(n, g, par, qp, following, nxt_par):
                def score(b):
                    if b == 0:
                        pe.wait_ge(*q_low.at(n, 0))
                        pe.wait_ge(*k_low.at(n, 0))
                    pe.wait_ge(*s_sel.at(n, b))
                    for h in range(GQ):
                        for k, st, sp_ in ((k_hi, True, False), (k_lo, False, True)):
                            last = mm(ps_s[:, h, :], q_st[:, h, b * BLK:(b + 1) * BLK],
                                      k[:, b * BLK:(b + 2) * BLK], start=st, stop=sp_)
                    last.then_inc(*scores.one())

                def turn_p(b):
                    pe.wait_ge(*p_norm.at(n, b + 1))
                    pe.wait_ge(*p_low.at(n, b))
                    for h in range(GQ):
                        last = nc.tensor.transpose(ps_t[:, h, :], s_sb[:, b % 2, h, :], ident[:, :])
                    last.then_inc(*p_T.one())

                def weigh_v(b):
                    if b == 0:
                        pe.wait_ge(*v_low.at(n, 0))
                        pe.wait_ge(*dv_low.at(n, 0))
                    pe.wait_ge(*p_low.at(n, b + 1))
                    pe.wait_ge(*p_cur.at(n, 2 * b + 2))
                    pe.wait_ge(*o_sum.at(n, 2 * b))
                    terms = ((v_hl, p_hi), (v_hl, p_lo), (dv_hl, p_hi_c), (dv_hl, p_lo_c))
                    for i, (v, p) in enumerate(terms):
                        last = mm(ps_v[:, :, :], v[:, b, :], p[:, :, :], start=(i == 0), stop=(i == 3))
                    last.then_inc(*pv.one())

                def gates(u):
                    pe.wait_ge(*u_low.at(n, u + 1))
                    if u == 0:
                        pe.wait_ge(*gw_low.at(n, 1))
                    for j in range(2):
                        r = ((R_R0, R_I0), (R_R1, R_I1))[u][j]
                        pe.wait_ge(*bank_free(n, r))
                        for i, (w, v) in enumerate(((gw_hi, u_hi), (gw_hi, u_lo), (gw_lo, u_hi))):
                            last = mm(bank(r), w[:, u, j, :], v[:, :], start=(i == 0), stop=(i == 2))
                        last.then_inc(*ring_ready.one())

                def turn_x():
                    pe.wait_ge(*x_norm.at(n, 1))
                    for half in range(2):
                        pe.wait_ge(*bank_free(n, R_XT0 + half))
                        for k in range(4):
                            c = half * 4 + k
                            last = nc.tensor.transpose(bank(R_XT0 + half)[:, k * P:(k + 1) * P],
                                                       xb[:, c * P:(c + 1) * P], ident[:, :])
                        last.then_inc(*ring_ready.one())

                project(n, XL0, par)
                project(n, GL0, par)
                project(n, XL1, par)
                score(0)
                gates(0)
                project(n, GA0, par)
                gates(1)
                score(1)
                project(n, GA1, par)
                turn_p(0)
                score(2)
                turn_x()
                project(n, GL1, par)
                weigh_v(0)
                turn_p(1)
                score(3)
                if nxt_par != par:
                    pe.wait_ge(*ring_dve.at(n, FREED_BY_DVE.index(R_XT1) + 1))
                project(n, KVG, nxt_par)
                weigh_v(1)
                turn_p(2)
                project(n, Q0, nxt_par)
                weigh_v(2)
                turn_p(3)
                project(n, Q1, nxt_par)
                weigh_v(3)
                turn_v(n)

            iterations(pe, body)

        for sig in signals:
            if sig is not s_cap:
                sig.checked(4, WSLOTS if sig in (w_high, w_low) else 0)
        for sig in pro:
            sig.checked(1)


def phase_b(nc, x, attn_out_gain, lru_out_gain, w_out, final_gain, y_dram, sq_dram, out):
    with ExitStack() as ctx:
        def sb(name, shape, dt=F32):
            return ctx.enter_context(nc.sbuf_tensor(name, shape, dt))

        def sem(name):
            return ctx.enter_context(nc.semaphore(name))

        wo_hi = sb("wo_hi", [P, EC, D], F32R)
        wo_lo = sb("wo_lo", [P, EC, D], F32R)
        wo_raw = sb("wo_raw", [P, 2, D])
        y_raw = sb("y_raw", [P, EC, P])
        y_hi = sb("y_hi", [P, 2, EC, P], F32R)
        y_lo = sb("y_lo", [P, 2, EC, P], F32R)
        sqs = sb("sqs", [P, 2, SEQ])
        res = sb("res", [P, 2, D])
        fgain = sb("fgain", [P, D])
        junk = sb("junk_b", [P, D], BF16)
        egain = sb("egain", [P, EC])
        ones = sb("ones", [P, 1])
        rms = sb("rms", [P, 2, NTOK])
        stat = sb("stat", [P, 2, 4])
        acc = ctx.enter_context(nc.psum_tensor("acc_b", [P, 2, 2, 2, D // 2], F32))
        stat_ps = acc[:, 1, 0, 0, 0:2 * NTOK]

        signals = []

        def signal(name, per, unit=1):
            s = Signal(ctx, nc, name, per, unit)
            signals.append(s)
            return s

        primed = sem("primed_b")
        consts_in = sem("consts_in_b")
        ones_set = sem("ones_set")
        stat_done = sem("stat_done")
        rms_step = sem("rms_step")
        rms_root = sem("rms_root")
        settled = sem("settled_b")
        wo_in = [signal(f"wo_in{s}", 1, 16) for s in range(2)]
        wo_high = signal("wo_high", 2)
        wo_low = signal("wo_low", 2)
        y_in = signal("y_in", 2, 16)
        y_high = signal("y_high", 2)
        y_low = signal("y_low", 2)
        x_in = [signal(f"x_in_b{s}", 1, 16) for s in range(2)]
        product = signal("product", 2)
        added = signal("added", 4)
        sq_done = signal("sq_done", 2)
        mean = signal("mean", 2)
        rooted = signal("rooted", 2)
        recip = signal("recip", 2)
        normed = signal("normed", 2)
        stored = [Signal(ctx, nc, f"stored{s}", 1, 16, lead=0) for s in range(2)]

        f = lambda ap: ap.bitcast(F32)
        N_CONST = 4
        block = ctx.enter_context(nc.Block())

        def store(pool, m, s):
            pool.wait_ge(*normed.at(m, s + 1))
            pool.sem_inc(settled, 1)
            pool.dma_start(out[0, bass.ds(m * (2 * P) + s * P, P), :], res[:, s, :]
                         ).then_inc(*stored[s].one())

        @block.sync
        def _(sp):
            with nc.allow_non_contiguous_dma(reason="per-channel gains, once"):
                for i, v in enumerate((attn_out_gain, lru_out_gain)):
                    sp.dma_start(egain[:, i * (EC // 2):(i + 1) * (EC // 2)],
                                 v.rearrange("o (e p) -> p (o e)", p=P)).then_inc(consts_in, 16)
            sp.dma_start(sqs[:, :, :], sq_dram).then_inc(consts_in, 16)
            sp.dma_start(fgain[:, :], final_gain.rearrange("(o d) -> o d", o=1).broadcast_to([P, D])
                         ).then_inc(consts_in, 16)
            sp.wait_ge(primed, 1)
            with sp.Fori(0, EC // 2) as i:
                for s in range(2):
                    sp.wait_ge(*wo_low.at(i, s - 1))
                    sp.dma_start(wo_raw[:, s, :], w_out[0, bass.ds(i * (2 * P) + s * P, P), :]
                                 ).then_inc(*wo_in[s].one())
            with sp.Fori(0, NTOK // 2) as m:
                for s in range(2):
                    sp.wait_ge(*y_low.at(m, s))
                    sp.dma_start(y_raw[:, :, :], y_dram[:, :, bass.ds(m * (2 * P) + s * P, P)].rearrange(
                        "e p t -> p e t")).then_inc(*y_in.one())
                    sp.wait_ge(*stored[s].at(m, 0))
                    sp.dma_start(res[:, s, :], x[0, bass.ds(m * (2 * P) + s * P, P), :]
                                 ).then_inc(*x_in[s].one())
            sp.wait_ge(*y_low.at(NTOK // 2, 0))
            sp.sem_inc(y_in.sem, 16)

        @block.gpsimd
        def _(pool):
            for s in signals:
                pool.sem_inc(s.sem, s.prime)
            pool.sem_inc(primed, 1)
            nc.gpsimd.memset(ones[:, :], 1.0).then_inc(ones_set, 1)
            with pool.Fori(0, NTOK // 2) as m:
                for s in range(2):
                    store(pool, m, s)
            for s in range(2):
                pool.wait_ge(*stored[s].at(NTOK // 2, 0))

        @block.scalar
        def _(act):
            act.wait_ge(primed, 1)
            act.wait_ge(consts_in, N_CONST * 16)
            with act.Fori(0, EC // 2) as i:
                for s in range(2):
                    e = i * 2 + s
                    act.wait_ge(*wo_in[s].at(i, 1))
                    act.sem_inc(settled, 1)
                    nc.scalar.activation(wo_hi[:, e, :], wo_raw[:, s, :], ACT.Copy,
                                         scale=egain[:, bass.ds(e, 1)]).then_inc(*wo_high.one())
            act.wait_ge(rms_step, 2)
            nc.scalar.activation(rms[:, :, :], rms[:, :, :], ACT.Sqrt).then_inc(rms_root, 1)

            def high_y(m, s):
                act.wait_ge(*y_in.at(m, s + 1))
                act.wait_ge(*product.at(m, s - 1))
                nc.scalar.activation(y_hi[:, s, :, :], y_raw[:, :, :], ACT.Copy).then_inc(*y_high.one())

            high_y(0, 0)
            with act.Fori(0, NTOK // 2) as m:
                for s in range(2):
                    if s == 0:
                        high_y(m, 1)
                    else:
                        high_y(m + 1, 0)
                    act.wait_ge(*added.at(m, 2 * s + 2))
                    nc.scalar.activation(junk[:, :], res[:, s, :], ACT.Square, accum_out=stat[:, s, 0:1]
                                         ).then_inc(*sq_done.one())
                    act.wait_ge(*mean.at(m, s + 1))
                    nc.scalar.activation(stat[:, s, 2:3], stat[:, s, 1:2], ACT.Sqrt).then_inc(*rooted.one())

        @block.vector
        def _(dve):
            stt = nc.vector.scalar_tensor_tensor
            dve.wait_ge(primed, 1)
            dve.wait_ge(consts_in, N_CONST * 16)
            with dve.Fori(0, EC // 2) as i:
                for s in range(2):
                    e = i * 2 + s
                    dve.wait_ge(*wo_high.at(i, s + 1))
                    stt(out=wo_lo[:, e, :], in0=wo_raw[:, s, :], scalar=egain[:, bass.ds(e, 1)],
                        in1=f(wo_hi[:, e, :]), op0=ALU.mult, op1=ALU.subtract).then_inc(*wo_low.one())
            dve.wait_ge(stat_done, 1)
            st = stat_ps.rearrange("p (g t) -> p g t", g=2)
            for g, k in ((0, 4.0), (1, 16.0)):
                nc.vector.tensor_scalar(rms[:, g, :], st[:, g, :], 1.0 / 1024, k * EPS, ALU.mult, ALU.add
                                        ).then_inc(rms_step, 1)
            dve.wait_ge(rms_root, 1)
            nc.vector.reciprocal(rms[:, :, :], rms[:, :, :]).then_inc(rms_step, 1)
            dve.wait_ge(rms_step, 3)

            def low_y(m, s):
                dve.wait_ge(*y_high.at(m, s + 1))
                nc.vector.tensor_tensor(y_lo[:, s, :, :], y_raw[:, :, :], f(y_hi[:, s, :, :]), ALU.subtract
                                        ).then_inc(*y_low.one())

            low_y(0, 0)
            with dve.Fori(0, NTOK // 2) as m:
                for s in range(2):
                    if s == 0:
                        low_y(m, 1)
                    else:
                        low_y(m + 1, 0)
                    dve.wait_ge(*product.at(m, s + 1))
                    dve.wait_ge(*x_in[s].at(m, 1))
                    r = res[:, s, :].rearrange("p (h c) -> p h c", h=2)
                    for g in range(2):
                        if g:
                            dve.wait_ge(*added.at(m, 2 * s + 1))
                        stt(out=r, in0=acc[:, s, g, :, :], scalar=rms[:, g, bass.ds(m * 2 + s, 1)], in1=r,
                            op0=ALU.mult, op1=ALU.add).then_inc(*added.one())
                    dve.wait_ge(*sq_done.at(m, s + 1))
                    nc.vector.tensor_scalar(stat[:, s, 1:2], stat[:, s, 0:1], 1.0 / D, EPS, ALU.mult, ALU.add
                                            ).then_inc(*mean.one())
                    dve.wait_ge(*rooted.at(m, s + 1))
                    nc.vector.reciprocal(stat[:, s, 3:4], stat[:, s, 2:3]).then_inc(*recip.one())
                    dve.wait_ge(*recip.at(m, s + 1))
                    stt(out=res[:, s, :], in0=res[:, s, :], scalar=stat[:, s, 3:4], in1=fgain[:, :],
                        op0=ALU.mult, op1=ALU.mult).then_inc(*normed.one())

        @block.tensor
        def _(pe):
            pe.wait_ge(consts_in, N_CONST * 16)
            pe.wait_ge(ones_set, 1)
            for g in range(2):
                for t in range(NTOK):
                    last = nc.tensor.matmul(stat_ps[:, g * NTOK + t:g * NTOK + t + 1],
                                            sqs[:, g, t * P:(t + 1) * P], ones[:, :], start=True, stop=True)
            last.then_inc(stat_done, 1)
            pe.wait_ge(rms_step, 2)
            pe.wait_ge(primed, 1)
            with pe.Fori(0, NTOK // 2) as m:
                for s in range(2):
                    pe.wait_ge(*y_low.at(m, s + 1))
                    pe.wait_ge(*added.at(m, 2 * s + 2 - 4))
                    for e in range(EC):
                        if s == 0:
                            pe.wait_ge(*wo_low.at(e // 2, e % 2 + 1))
                        g = e // (EC // 2)
                        for j, (y, w) in enumerate(((y_hi, wo_hi), (y_hi, wo_lo), (y_lo, wo_hi))):
                            for h in range(2):
                                last = nc.tensor.matmul(
                                    acc[:, s, g, h, :], y[:, s, e, :],
                                    w[:, e, h * (D // 2):(h + 1) * (D // 2)],
                                    start=(e % (EC // 2) == 0 and j == 0),
                                    stop=(e % (EC // 2) == EC // 2 - 1 and j == 2))
                    last.then_inc(*product.one())


def rope_tables():
    half = ROT // 2
    inv = np.float32(500000.0) ** (-np.arange(0, ROT, 2, dtype=np.float32) / np.float32(ROT))
    ang = np.arange(SEQ, dtype=np.float32)[None, :] * inv.astype(np.float32)[:, None]
    cos, sin = np.cos(ang), np.sin(ang)
    c = np.ones((P, SEQ), np.float32)
    s = np.zeros((P, SEQ), np.float32)
    for head in range(2):
        r = head * HD
        c[r:r + half], c[r + half:r + ROT] = cos, cos
        s[r:r + half], s[r + half:r + ROT] = -sin, sin
    return c, s


_INPUTS = ["x", "ln_gain", "w_in", "sinks", "conv_w", "conv_b", "w_rgate", "b_rgate", "w_igate", "b_igate",
           "lru_lambda", "attn_out_gain", "lru_out_gain", "w_out", "final_gain"]


def constants():
    cos, sin = rope_tables()
    query, key = np.arange(BLK)[:, None], np.arange(BLK)[None, :]
    prev = key > query
    cap = np.full((P, 2, BLK), BIG, np.float32)
    cap[:, 0, :][prev] = NEG
    return {"rope_cos": cos, "rope_sin": sin, "first_cap": cap,
            "identity": np.eye(P, dtype=np.float32)}


def kernel(**inputs):
    import concourse.bacc as bacc
    from concourse.bass_utils import run_bass_kernel_spmd

    nc = bacc.Bacc("TRN2", target_bir_lowering=False, num_devices=1)
    arrays, args = {}, {}
    for name, a in {**{k: inputs[k] for k in _INPUTS}, **constants()}.items():
        a = np.ascontiguousarray(a)
        arrays[name + "_d"] = a
        args[name] = nc.dram_tensor(name + "_d", a.shape, mybir.dt.from_np(a.dtype), kind="ExternalInput").ap()
    out = nc.dram_tensor("out_d", (1, SEQ, D), F32, kind="ExternalOutput").ap()
    hymba_kernel(nc, out=out, **args)
    r = run_bass_kernel_spmd(nc, [arrays], core_ids=[0])
    return r.results[0]["out_d"]
```

```python
from contextlib import ExitStack

import numpy as np

import concourse.bass as bass
from concourse import mybir

F32 = mybir.dt.float32
F32R = mybir.dt.float32r
BF16 = mybir.dt.bfloat16
U8 = mybir.dt.uint8
ALU = mybir.AluOpType
ACT = mybir.ActivationFunctionType
AXX = mybir.AxisListType.X

P = 128
SEQ, D = 2048, 1024
KC = D // P
HD = 64
KV, GQ = 4, 4
BLK = 128
ROT = HD // 4
T = 512
NBLK = T // BLK
NQUART = SEQ // T
NITER = NQUART * KV
LRU_W = 1024
UNITS = LRU_W // P // KV
BW = 64
EPS = 1e-6
MIX = 2048
EC = MIX // P
NTOK = SEQ // P
LAG = 4
CONV = 4
BIG = 3.0e38
NEG = -1.0e30

COL_Q, COL_K, COL_V = 0, 1024, 1024 + KV * HD
COL_GA = COL_V + KV * HD
COL_XL = COL_GA + 1024
COL_GL = COL_XL + LRU_W

XL0, GL0, XL1, GA0, GA1, GL1, KVG, Q0, Q1 = range(9)
NG = 9
WSLOTS = 3
(R_XL0, R_GL0, R_XL1, R_R0, R_I0, R_GA0, R_R1, R_I1, R_GA1, R_XT0, R_XT1, R_GL1, R_KV, R_Q0, R_Q1,
 R_VT) = range(16)
NR = 16
RING = 4
RING_OF_GROUP = [R_XL0, R_GL0, R_XL1, R_GA0, R_GA1, R_GL1, R_KV, R_Q0, R_Q1]
FREED_BY_DVE = [R_GL0, R_GA0, R_GA1, R_XT0, R_XT1, R_GL1]
FREED_BY_ACT = [r for r in range(NR) if r not in FREED_BY_DVE]

(C_W0, C_W1, C_W2, C_W3, C_CB, C_BR, C_BI, C_LAM, C_NEG4SP, C_POS4SP, C_T0, C_T1, C_T2) = range(13)
NPRM = 13


SWAP = [(i + ROT // 2) % ROT if i < ROT else i for i in range(32)]


class Signal:

    def __init__(self, ctx, nc, name, per, unit=1, lead=1, ahead=0):
        self.sem = ctx.enter_context(nc.semaphore(name))
        self.name, self.per, self.unit, self.lead, self.count = name, per, unit, lead, 0
        self.prime = (lead * per - ahead) * unit
        self.ahead = ahead

    def at(self, n, k):
        return self.sem, n * (self.per * self.unit) + (self.lead * self.per + k) * self.unit

    def one(self):
        self.count += 1
        return self.sem, self.unit

    def checked(self, bodies, beyond=0):
        assert self.count == bodies * self.per + self.ahead + beyond, (self.name, self.count, self.per)


def hymba_kernel(nc, x, ln_gain, w_in, sinks, conv_w, conv_b, w_rgate, b_rgate, w_igate, b_igate,
                 lru_lambda, attn_out_gain, lru_out_gain, w_out, final_gain,
                 rope_cos, rope_sin, first_cap, identity, out):
    y_dram = nc.dram_tensor("y_scratch", (EC, P, SEQ), F32, kind="Internal").ap()

    with ExitStack() as top:
        def sb(name, shape, dt=F32):
            return top.enter_context(nc.sbuf_tensor(name, shape, dt))

        ident = sb("ident", [P, P])
        ones = sb("ones", [P, 1])
        w_raw = sb("w_raw", [P, WSLOTS, KC * P])
        egain = sb("egain", [P, EC])
        acc = sb("acc", [P, 2, 2, T])
        sums = sb("sums", [P, 2, NTOK + NBLK])
        shared = (ident, ones, w_raw, egain, acc, sums)

        phase_a(nc, x, ln_gain, w_in, sinks, conv_w, conv_b, w_rgate, b_rgate, w_igate, b_igate,
                lru_lambda, attn_out_gain, lru_out_gain, w_out, rope_cos, rope_sin, first_cap, identity,
                y_dram, shared)
        phase_b(nc, x, w_out, final_gain, y_dram, out, shared)


def phase_a(nc, x, ln_gain, w_in, sinks, conv_w, conv_b, w_rgate, b_rgate, w_igate, b_igate,
            lru_lambda, attn_out_gain, lru_out_gain, w_out, rope_cos, rope_sin, first_cap, identity,
            y_dram, shared):
    ident, ones, w_raw_flat, egain, acc, sums = shared
    w_raw = w_raw_flat[:, :, :].rearrange("p s (k c) -> p s k c", k=KC)
    with ExitStack() as ctx:
        signals = []

        def sb(name, shape, dt=F32):
            return ctx.enter_context(nc.sbuf_tensor(name, shape, dt))

        def sem(name):
            return ctx.enter_context(nc.semaphore(name))

        def signal(name, per, unit=1, ahead=0):
            s = Signal(ctx, nc, name, per, unit, lead=2, ahead=ahead)
            signals.append(s)
            return s

        h_hi = sb("h_hi", [P, 2, KC, T], F32R)
        h_lo = sb("h_lo", [P, 2, KC, T], F32R)
        w_hi = sb("w_hi", [P, WSLOTS, KC, P], F32R)
        w_lo = sb("w_lo", [P, WSLOTS, KC, P], F32R)
        xb = sb("xb", [P, D])
        gain_row = sb("gain_row", [P, D])
        xs = sb("x_stat", [P, 4])
        cosT = sb("cosT", [P, T])
        sinT = sb("sinT", [P, T])
        prev_mask = sb("prev_mask", [P, GQ, BLK], U8)
        cap = sb("cap", [P, 2, BLK])
        sink_all = sb("sink_all", [P, KV * GQ])
        prm = sb("prm", [P, LRU_W // P, NPRM])
        kraw = sb("kraw", [P, T])
        swp = sb("swp", [P, T])
        krot = sb("krot", [HD, BLK + T])
        k_hi = sb("k_hi", [P, BLK + T], F32R)
        k_lo = sb("k_lo", [P, BLK + T], F32R)
        kc_ol = sb("kc_ol", [P, KV, BLK])
        k_carry, o_low = kc_ol[0:HD], kc_ol[HD:]
        vraw = sb("vraw", [P, 1 + NBLK, HD])
        v_hl = sb("v_hl", [P, 1 + NBLK, 2 * HD], F32R)
        dvraw = sb("dvraw", [P, NBLK, HD])
        dv_hl = sb("dv_hl", [P, NBLK, 2 * HD], F32R)
        v_carry = sb("v_carry", [P, KV, HD])
        qraw = sb("qraw", [P, T])
        qrot = sb("qrot", [P, T])
        q_st = sb("q_st", [P, GQ, T], F32R)
        s_sb = sb("s_sb", [P, 2, GQ, BLK])
        smax = sb("smax", [P, 2, 4, GQ])
        sden = sb("sden", [P, 2, 4, GQ])
        p_hi = sb("p_hi", [P, GQ, BLK], F32R)
        p_lo = sb("p_lo", [P, GQ, BLK], F32R)
        p_hi_c = sb("p_hi_c", [P, GQ, BLK], F32R)
        p_lo_c = sb("p_lo_c", [P, GQ, BLK], F32R)
        o_sb = sb("o_sb", [P, 2, BLK])
        ya = sb("ya", [P, 2, T])
        sq = sb("sq", [P, T])
        xl = sb("xl", [P, CONV - 1 + T])
        cu = [sb(f"cu{u}", [P, T]) for u in range(UNITS)]
        u_hi = sb("u_hi", [P, T], F32R)
        u_lo = sb("u_lo", [P, T], F32R)
        ra = [sb(f"ra{u}", [P, T]) for u in range(UNITS)]
        a2 = sb("a2", [P, T])
        ri = [sb(f"ri{u}", [P, T]) for u in range(UNITS)]
        gl = sb("gl", [P, T])
        hs = [sb(f"hs{u}", [P, T]) for u in range(UNITS)]
        x_carry = sb("x_carry", [P, LRU_W // P, CONV - 1])
        h_carry = sb("h_carry", [P, LRU_W // P, 1])
        gw_raw = sb("gw_raw", [P, UNITS, 2, P])
        gw_hi = sb("gw_hi", [P, UNITS, 2, P], F32R)
        gw_lo = sb("gw_lo", [P, UNITS, 2, P], F32R)

        ring = ctx.enter_context(nc.psum_tensor("ring", [P, RING, T], F32))
        ps_s = ctx.enter_context(nc.psum_tensor("ps_s", [P, GQ, 2 * BLK], F32))
        ps_t = ctx.enter_context(nc.psum_tensor("ps_t", [P, GQ, BLK], F32))
        ps_v = ctx.enter_context(nc.psum_tensor("ps_v", [P, GQ, BLK], F32))

        primed = sem("primed")
        consts_in = sem("consts_in")
        zeroed = sem("zeroed")
        prm_step = sem("prm_step")
        prm_act = sem("prm_act")
        pro_x_in = [sem(f"pro_x_in{b}") for b in range(NBLK)]
        early_in = sem("early_in")
        pro_sq, pro_ms, pro_root, pro_rs, pro_norm, pro_T, pro_hi, pro_lo = (
            sem("pro_" + s) for s in ("sq", "ms", "root", "rs", "norm", "T", "hi", "lo"))
        masks = sem("masks")
        table_in = sem("table_in")
        settled = sem("settled")

        w_in_dma = [signal(f"w_in_dma{s}", 4 if s == 0 else 3, 16, ahead=2 if s == 0 else 1)
                    for s in range(WSLOTS)]
        W_DMA_AT = {XL0: 1, GL0: 1, XL1: 1, GA0: 2, GA1: 2, GL1: 2, KVG: 4, Q0: 3, Q1: 3}
        w_high = signal("w_high", NG, ahead=3)
        w_low = signal("w_low", NG, ahead=3)
        ring_ready = signal("ring_ready", NR, ahead=4)
        ring_act = signal("ring_act", len(FREED_BY_ACT), ahead=4)
        ring_dve = signal("ring_dve", len(FREED_BY_DVE))
        x_in = signal("x_in", 1, 16)
        x_sq = signal("x_sq", 1)
        x_ms = signal("x_ms", 1)
        x_root = signal("x_root", 1)
        x_rs = signal("x_rs", 1)
        x_norm = signal("x_norm", 1)
        h_high = signal("h_high", 2)
        k_turn = signal("k_turn", 3, ahead=3)
        k_sin = signal("k_sin", 1, ahead=1)
        k_rot = signal("k_rot", 1, ahead=1)
        k_high = signal("k_high", 2, ahead=2)
        k_low = signal("k_low", 3, ahead=3)
        q_turn = signal("q_turn", 4, ahead=4)
        q_sin = signal("q_sin", 2, ahead=2)
        q_rot = signal("q_rot", 2, ahead=2)
        q_high = signal("q_high", 4, ahead=4)
        q_low = signal("q_low", 4, ahead=4)
        v_prev = signal("v_prev", 1, ahead=1)
        v_high = signal("v_high", 1, ahead=1)
        v_low = signal("v_low", 1, ahead=1)
        dv_raw = signal("dv_raw", 1, ahead=1)
        dv_high = signal("dv_high", 1, ahead=1)
        dv_low = signal("dv_low", 1, ahead=1)
        v_kept = signal("v_kept", 1, ahead=1)
        scores = signal("scores", NBLK)
        s_cur = signal("s_cur", NBLK)
        s_sel = signal("s_sel", NBLK)
        s_cap = signal("s_cap", 1)
        s_stat = signal("s_stat", 4 * NBLK)
        p_exp = signal("p_exp", NBLK * (GQ + 1))
        p_den = signal("p_den", 2 * NBLK)
        p_norm = signal("p_norm", NBLK)
        p_T = signal("p_T", NBLK)
        p_high = signal("p_high", NBLK)
        p_low = signal("p_low", NBLK)
        p_cur = signal("p_cur", 2 * NBLK)
        pv = signal("pv", NBLK)
        o_lowdone = signal("o_lowdone", NBLK)
        o_sum = signal("o_sum", 2 * NBLK)
        ga_tanh = signal("ga_tanh", 2)
        ya_done = signal("ya_done", NBLK)
        ya_out = signal("ya_out", 1, 16)
        sq_made = signal("sq_made", 4)
        sq_added = signal("sq_added", 4)
        xl_prev = signal("xl_prev", UNITS)
        xl_in = signal("xl_in", UNITS)
        u_conv = signal("u_conv", 3 * UNITS)
        xl_kept = signal("xl_kept", UNITS)
        u_high = signal("u_high", UNITS)
        u_low = signal("u_low", UNITS)
        gw_dma = signal("gw_dma", 4, 16)
        gw_high = signal("gw_high", 1)
        gw_low = signal("gw_low", 1)
        decay = signal("decay", 3 * UNITS)
        one_minus = signal("one_minus", UNITS)
        root = signal("root", UNITS)
        i_x = signal("i_x", UNITS)
        scan_in = signal("scan_in", UNITS)
        scanned = signal("scanned", UNITS)
        h_kept = signal("h_kept", UNITS)
        gl_tanh = signal("gl_tanh", UNITS)
        yl_done = signal("yl_done", UNITS)
        yl_out = [signal(f"yl_out{u}", 1, 16) for u in range(UNITS)]
        stat_sum = Signal(ctx, nc, "stat_sum", 1)
        stat_kept = Signal(ctx, nc, "stat_kept", 1)
        quarterly = [stat_sum, stat_kept]
        acc_zero = sem("acc_zero")

        bank = lambda r: ring[:, r % RING, :]
        f = lambda ap: ap.bitcast(F32)

        pro_x = [xb[:, :], ya[:, :, :].rearrange("p j t -> p (j t)"),
                 s_sb[:, :, :, :].rearrange("p s h t -> p (s h t)"),
                 acc[:, 1, :, :].rearrange("p w t -> p (w t)")]
        pro_stat = smax[:, 0, :, :]

        def bank_free(n, r):
            before = (r - RING) % NR
            late = 0 if r >= RING else 1
            if before in FREED_BY_ACT:
                return ring_act.at(n, FREED_BY_ACT.index(before) + 1 - late * len(FREED_BY_ACT))
            return ring_dve.at(n, FREED_BY_DVE.index(before) + 1 - late * len(FREED_BY_DVE))

        def iterations(eng, body, quarter_start=None):
            with eng.Fori(0, NQUART // 2) as qp:
                for par in range(2):
                    if quarter_start:
                        quarter_start(qp, par)
                    eng.sem_inc(settled, 1)
                    with eng.Fori(0, KV - 1) as g:
                        body(qp * (2 * KV) + (g + par * KV), g, par, qp, g + 1, par)
                    eng.sem_inc(settled, 1)
                    body(qp * (2 * KV) + (KV - 1 + par * KV), KV - 1, par, qp, 0, 1 - par)

        N_CONST = 12
        block = ctx.enter_context(nc.Block())

        @block.sync
        def _(sp):
            for b in range(NBLK):
                sp.dma_start(pro_x[b], x[0, b * P:(b + 1) * P, :]).then_inc(pro_x_in[b], 16)
            sp.dma_start(gain_row[:, :], ln_gain.broadcast_to([P, D])).then_inc(early_in, 16)
            sp.dma_start(ident[:, :], identity).then_inc(early_in, 16)

            def load_consts():
                chan = lambda v: v.rearrange("o (u p) -> p (o u)", p=P)
                sp.dma_start(sink_all[:, :], sinks.broadcast_to([P, KV * GQ])).then_inc(consts_in, 16)
                with nc.allow_non_contiguous_dma(reason="per-channel parameters, a few KB once"):
                    for i in range(CONV):
                        sp.dma_start(prm[:, :, C_W0 + i], conv_w[0, i:i + 1, :].rearrange(
                            "o (u p) -> p (o u)", p=P)).then_inc(consts_in, 16)
                    for col, v in ((C_CB, conv_b), (C_BR, b_rgate), (C_BI, b_igate), (C_LAM, lru_lambda)):
                        sp.dma_start(prm[:, :, col], chan(v)).then_inc(consts_in, 16)
                    for i, v in enumerate((attn_out_gain, lru_out_gain)):
                        sp.dma_start(egain[:, i * (EC // 2):(i + 1) * (EC // 2)],
                                     v.rearrange("o (e p) -> p (o e)", p=P)).then_inc(consts_in, 16)
                sp.dma_start(cap[:, :, :], first_cap).then_inc(consts_in, 16)

            def load_group(n, i, col):
                sp.wait_ge(*w_low.at(n, i + 1 - WSLOTS))
                sp.dma_start(w_raw[:, i % WSLOTS, :, :],
                             w_in[0, :, bass.ds(col, P)].rearrange("(k p) c -> p k c", p=P)
                             ).then_inc(*w_in_dma[i % WSLOTS].one())

            def load_next(n, g):
                sp.wait_ge(*w_low.at(n, KVG + 1 - WSLOTS))
                for half, col in ((0, COL_K), (1, COL_V)):
                    sp.dma_start(w_raw[:, 0, :, half * HD:(half + 1) * HD],
                                 w_in[0, :, bass.ds(g * HD + col, HD)].rearrange("(k p) c -> p k c", p=P)
                                 ).then_inc(*w_in_dma[0].one())
                load_group(n, Q0, g * (2 * P) + COL_Q)
                load_group(n, Q1, g * (2 * P) + (COL_Q + P))

            def load_tables(col):
                sp.dma_start(cosT[:, :], rope_cos[:, bass.ds(col, T)]).then_inc(table_in, 16)
                sp.dma_start(sinT[:, :], rope_sin[:, bass.ds(col, T)]).then_inc(table_in, 16)

            sp.wait_ge(primed, 1)
            load_next(-1, 0)
            load_tables(0)
            load_consts()
            sp.wait_ge(zeroed, 6)
            sp.wait_ge(pro_T, 2 * NBLK)

            def body(n, g, par, qp, following, nxt_par):
                load_group(n, XL0, g * (2 * P) + COL_XL)
                load_group(n, GL0, g * (2 * P) + COL_GL)
                sp.wait_ge(*ring_ready.at(n, R_XT1 + 1 - NR))
                first = (qp * (2 * KV) + (g + KV)) if par == 0 else (g + 2 * KV)
                sp.dma_start(xb[:, :], x[0, bass.ds(first * P, P), :]).then_inc(*x_in.one())
                load_group(n, XL1, g * (2 * P) + (COL_XL + P))
                sp.wait_ge(*gw_low.at(n, 0))
                for j, w in enumerate((w_rgate, w_igate)):
                    for half in range(2):
                        rows = slice(half * BW, (half + 1) * BW)
                        sp.dma_start(gw_raw[rows, :, j, rows],
                                     w[0, bass.ds(g * (2 * UNITS), 2 * UNITS), :, :].rearrange(
                                         "(u h) c d -> c h u d", h=2)[:, half, :, :]
                                     ).then_inc(*gw_dma.one())
                if nxt_par != par:
                    sp.wait_ge(*q_rot.at(n, 0))
                    load_tables((qp * 2 + 1) * T if par == 0 else 2 * T)
                load_group(n, GA0, g * (2 * P) + COL_GA)
                load_group(n, GA1, g * (2 * P) + (COL_GA + P))
                load_group(n, GL1, g * (2 * P) + (COL_GL + P))
                load_next(n, following)

            iterations(sp, body)
            for s in range(WSLOTS):
                sp.wait_ge(*w_low.at(NITER, s + 1 - WSLOTS))
                sp.dma_start(w_raw_flat[:, s, :], w_out[0, s * P:(s + 1) * P, :]).then_inc(w_in_dma[s].sem, 16)

        @block.gpsimd
        def _(pool):
            for s in signals + quarterly:
                pool.sem_inc(s.sem, s.prime)
            pool.sem_inc(primed, 1)
            for ap in (k_carry, v_carry[:, :, :], x_carry[:, :, :], h_carry[:, :, :], gw_raw[:, :, :, :]):
                nc.gpsimd.memset(ap, 0.0).then_inc(zeroed, 1)
            nc.gpsimd.memset(ones[:, :], 1.0).then_inc(zeroed, 1)

            def quarter_start(qp, par):
                q = qp * 2 + par
                pool.wait_ge(*stat_sum.at(q, 0))
                pool.sem_inc(settled, 1)
                nc.gpsimd.memset(acc[:, par, :, :], 0.0).then_inc(acc_zero, 1)
                pool.wait_ge(acc_zero, q + 1)

            def add_square(n, par, i, y, which, ready):
                pool.wait_ge(*ready)
                pool.wait_ge(*sq_added.at(n, i))
                nc.gpsimd.tensor_tensor(sq[:, :], y, y, ALU.mult).then_inc(*sq_made.one())
                pool.wait_ge(*sq_made.at(n, i + 1))
                nc.gpsimd.tensor_tensor(acc[:, par, which, :], acc[:, par, which, :], sq[:, :], ALU.add
                                        ).then_inc(*sq_added.one())

            def lru_tail(n, u):
                pool.wait_ge(*root.at(n, u + 1))
                pool.wait_ge(*i_x.at(n, u + 1))
                nc.gpsimd.tensor_tensor(ri[u][:, :], ri[u][:, :], hs[u][:, :], ALU.mult
                                        ).then_inc(*scan_in.one())

            def p_current(n, b):
                for k, (src, dst, ready) in enumerate(((p_hi, p_hi_c, p_high), (p_lo, p_lo_c, p_low))):
                    pool.wait_ge(*ready.at(n, b + 1))
                    if k == 0:
                        pool.wait_ge(*pv.at(n, b))
                    pool.sem_inc(settled, 1)
                    nc.gpsimd.affine_select(out=dst[:, :, :], in_=f(src[:, :, :]), compare_op=ALU.is_ge,
                                            fill=0.0, base=0, pattern=[[0, GQ], [1, BLK]],
                                            channel_multiplier=-1).then_inc(*p_cur.one())

            def sine_k(n):
                pool.wait_ge(*k_turn.at(n, 2))
                nc.gpsimd.tensor_tensor(swp[0:HD, :], swp[0:HD, :], sinT[0:HD, :], ALU.mult
                                        ).then_inc(*k_sin.one())

            def sine_q(n, j):
                pool.wait_ge(*q_turn.at(n, 2 * j + 2))
                nc.gpsimd.tensor_tensor(swp[:, :], swp[:, :], sinT[:, :], ALU.mult
                                        ).then_inc(*q_sin.one())

            def body(n, g, par, qp, following, nxt_par):
                lru_tail(n, 0)
                lru_tail(n, 1)
                lru_gate(n, par, 0)
                p_current(n, 0)
                p_current(n, 1)
                if nxt_par != par:
                    pool.wait_ge(table_in, (qp * 2 + par + 2) * 32)
                sine_k(n)
                p_current(n, 2)
                lru_gate(n, par, 1)
                sine_q(n, 0)
                p_current(n, 3)
                sine_q(n, 1)
                attention_squares(n, par)

            def attention_squares(n, par):
                pool.wait_ge(*ya_done.at(n, NBLK))
                for j in range(2):
                    add_square(n, par, 2 + j, ya[:, j, :], 0, ya_done.at(n, NBLK))

            def lru_gate(n, par, u):
                pool.wait_ge(*h_kept.at(n, u + 1))
                pool.wait_ge(*ring_dve.at(n, FREED_BY_DVE.index((R_GL0, R_GL1)[u]) + 1))
                nc.gpsimd.tensor_tensor(hs[u][:, :], hs[u][:, :], gl[:, :], ALU.mult
                                        ).then_inc(*yl_done.one())
                add_square(n, par, u, hs[u][:, :], 1, yl_done.at(n, u + 1))

            pool.wait_ge(table_in, 32)
            sine_k(-1)
            sine_q(-1, 0)
            sine_q(-1, 1)
            iterations(pool, body, quarter_start)

        @block.scalar
        def _(act):
            def split_w(n, i):
                m, i = (n, i) if i < NG else (n + 1, i - NG)
                s = i % WSLOTS
                act.wait_ge(*w_in_dma[s].at(m, W_DMA_AT[i]))
                prev = i - WSLOTS
                act.wait_ge(*ring_ready.at(m, RING_OF_GROUP[prev] + 1 - (NR if prev < 0 else 0)))
                nc.scalar.activation(w_hi[:, s, :, :], w_raw[:, s, :, :], ACT.Copy
                                     ).then_inc(*w_high.one())

            act.wait_ge(primed, 1)

            def square_x(n, xin, xsq, free):
                act.wait_ge(*xin)
                act.wait_ge(*free)
                nc.scalar.activation(a2[:, :].bitcast(BF16), xb[:, :], ACT.Square, accum_out=xs[:, 0:1]
                                     ).then_inc(*xsq.one())

            def root_x(n, xms, xroot):
                act.wait_ge(*xms)
                nc.scalar.activation(xs[:, 2:3], xs[:, 1:2], ACT.Sqrt).then_inc(*xroot.one())

            def high_x(dst, col, half, ps, ready, done):
                act.wait_ge(*ready)
                act.sem_inc(settled, 1)
                nc.scalar.activation(dst[:, half * 4:half * 4 + 4, bass.ds(col, P)],
                                     ps.rearrange("p (k t) -> p k t", k=4), ACT.Copy).then_inc(*done)

            for b in range(NBLK):
                act.wait_ge(pro_x_in[b], 16)
                if b:
                    act.wait_ge(pro_sq, b)
                nc.scalar.activation(a2[:, :].bitcast(BF16), pro_x[b], ACT.Square,
                                     accum_out=pro_stat[:, 0, b:b + 1]).then_inc(pro_sq, 1)
            act.wait_ge(pro_ms, 1)
            nc.scalar.activation(pro_stat[:, 2, :], pro_stat[:, 1, :], ACT.Sqrt).then_inc(pro_root, 1)
            split_w(-1, KVG)
            for i in range(2 * NBLK):
                b, half = divmod(i, 2)
                high_x(h_hi[:, 0], b * P, half, ring[:, i % RING, :], (pro_T, i + 1), (pro_hi, 1))
                if i in (2, 5):
                    split_w(-1, Q0 if i == 2 else Q1)
            act.wait_ge(consts_in, N_CONST * 16)
            act.wait_ge(prm_step, 1)
            nc.scalar.activation(prm[:, :, C_T1], prm[:, :, C_T0], ACT.Exp).then_inc(prm_act, 1)
            act.wait_ge(prm_step, 2)
            nc.scalar.activation(prm[:, :, C_T2], prm[:, :, C_T0], ACT.Ln).then_inc(prm_act, 1)

            def take_kv(n):
                act.wait_ge(*ring_ready.at(n, R_KV + 1))
                act.wait_ge(*ring_ready.at(n, R_VT + 1 - NR))
                act.wait_ge(*k_rot.at(n, 0))
                nc.scalar.activation(kraw[:, :], bank(R_KV), ACT.Copy).then_inc(*ring_act.one())

            def take_q(n, j):
                act.wait_ge(*ring_ready.at(n, (R_Q0, R_Q1)[j] + 1))
                act.wait_ge(*q_turn.at(n, 2 * j))
                nc.scalar.activation(qraw[:, :], bank((R_Q0, R_Q1)[j]), ACT.Copy).then_inc(*ring_act.one())

            def high_k(n):
                act.wait_ge(*k_rot.at(n, 1))
                act.wait_ge(*scores.at(n, NBLK))
                for half in range(2):
                    nc.scalar.activation(k_hi[half * HD:(half + 1) * HD, :], krot[:, :], ACT.Copy
                                         ).then_inc(*k_high.one())

            def high_q(n, j):
                act.wait_ge(*q_rot.at(n, j + 1))
                act.wait_ge(*scores.at(n, NBLK))
                for half in range(2):
                    rows = slice(half * HD, (half + 1) * HD)
                    nc.scalar.activation(q_st[rows, 2 * j + half, :], qrot[rows, :], ACT.Copy
                                         ).then_inc(*q_high.one())

            def take_v(n):
                act.wait_ge(*ring_ready.at(n, R_VT + 1))
                act.wait_ge(*v_kept.at(n, 0))
                nc.scalar.activation(vraw[:, 1:, :], bank(R_VT).rearrange("p (b c) -> p b c", c=P)[:, :, HD:],
                                     ACT.Copy).then_inc(*ring_act.one())

            def high_v(n):
                act.wait_ge(*v_prev.at(n, 1))
                act.wait_ge(*ring_act.at(n, FREED_BY_ACT.index(R_VT) + 1))
                act.wait_ge(*pv.at(n, NBLK))
                nc.scalar.activation(v_hl[:, :, 0:HD], vraw[:, :, :], ACT.Copy).then_inc(*v_high.one())
                act.wait_ge(*dv_raw.at(n, 1))
                nc.scalar.activation(dv_hl[:, :, 0:HD], dvraw[:, :, :], ACT.Copy).then_inc(*dv_high.one())

            take_kv(-1)
            split_w(-1, NG + XL0)
            take_q(-1, 0)
            high_k(-1)
            split_w(-1, NG + GL0)
            take_q(-1, 1)
            high_q(-1, 0)
            split_w(-1, NG + XL1)
            take_v(-1)
            high_q(-1, 1)
            high_v(-1)

            def body(n, g, par, qp, following, nxt_par):
                def gate_a(j):
                    act.wait_ge(*ring_ready.at(n, (R_GA0, R_GA1)[j] + 1))
                    if j == 0:
                        act.wait_ge(*ya_out.at(n, 0))
                        act.wait_ge(*sq_made.at(n, 0))
                    nc.scalar.activation(ya[:, j, :], bank((R_GA0, R_GA1)[j]), ACT.Tanh, scale=0.5
                                         ).then_inc(*ga_tanh.one())

                def s_copy(b):
                    act.wait_ge(*scores.at(n, b + 1))
                    act.wait_ge(*p_T.at(n, b - 1))
                    nc.scalar.activation(s_sb[:, b % 2], ps_s[:, :, BLK:], ACT.Copy).then_inc(*s_cur.one())

                def s_exp(b):
                    act.wait_ge(*s_stat.at(n, 4 * b + 4))
                    for h in range(GQ):
                        nc.scalar.activation(s_sb[:, b % 2, h, :], s_sb[:, b % 2, h, :], ACT.Exp,
                                             bias=smax[:, b % 2, 2, h:h + 1], scale=HD ** -0.5,
                                             accum_out=sden[:, b % 2, 0, h:h + 1]).then_inc(*p_exp.one())
                    nc.scalar.activation(sden[:, b % 2, 1, :], smax[:, b % 2, 3, :], ACT.Exp
                                         ).then_inc(*p_exp.one())

                def high_p(b):
                    act.wait_ge(*p_T.at(n, b + 1))
                    act.wait_ge(*pv.at(n, b))
                    act.wait_ge(*p_cur.at(n, 2 * b))
                    nc.scalar.activation(p_hi[:, :, :], ps_t[:, :, :], ACT.Copy).then_inc(*p_high.one())

                def low_o(b):
                    act.wait_ge(*pv.at(n, b + 1))
                    act.wait_ge(*o_sum.at(n, 2 * b))
                    nc.scalar.activation(o_low, ps_v[HD:, :, :], ACT.Copy
                                         ).then_inc(*o_lowdone.one())

                def lru_in(u):
                    r = (R_XL0, R_XL1)[u]
                    G = g * UNITS + u
                    act.wait_ge(*ring_ready.at(n, r + 1))
                    act.wait_ge(*xl_kept.at(n, u))
                    act.wait_ge(*i_x.at(n, u + 1 - UNITS))
                    nc.scalar.activation(xl[:, CONV - 1:], bank(r), ACT.Copy).then_inc(*xl_in.one())
                    act.sem_inc(settled, 1)
                    nc.scalar.activation(cu[u][:, :], bank(r), ACT.Identity,
                                         scale=prm[:, G, C_W3:C_W3 + 1], bias=prm[:, G, C_CB:C_CB + 1]
                                         ).then_inc(*ring_act.one())

                def high_u(u):
                    act.wait_ge(*u_conv.at(n, 3 * u + 3))
                    act.wait_ge(*ring_ready.at(n, R_I0 + 1 if u else R_I1 + 1 - NR))
                    nc.scalar.activation(u_hi[:, :], cu[u][:, :], ACT.Copy).then_inc(*u_high.one())

                def gate_l(u):
                    act.wait_ge(*ring_ready.at(n, (R_GL0, R_GL1)[u] + 1))
                    act.wait_ge(*yl_done.at(n, u))
                    nc.scalar.activation(gl[:, :], bank((R_GL0, R_GL1)[u]), ACT.Tanh, scale=0.5
                                         ).then_inc(*gl_tanh.one())

                def decays(u):
                    G = g * UNITS + u
                    act.wait_ge(*ring_ready.at(n, (R_R0, R_R1)[u] + 1))
                    act.wait_ge(*scanned.at(n, u + 1 - UNITS))
                    act.sem_inc(settled, 1)
                    nc.scalar.activation(ra[u][:, :], bank((R_R0, R_R1)[u]), ACT.Tanh, scale=0.5,
                                         bias=prm[:, G, C_BR:C_BR + 1]).then_inc(*ring_act.one())
                    act.wait_ge(*ring_act.at(n, FREED_BY_ACT.index((R_R0, R_R1)[u]) + 1))
                    act.wait_ge(*sq_made.at(n, u + 1 - 4))
                    act.wait_ge(*yl_out[u].at(n, 0))
                    act.sem_inc(settled, 1)
                    nc.scalar.activation(hs[u][:, :], ra[u][:, :], ACT.Tanh, scale=prm[:, G, C_POS4SP:C_POS4SP + 1],
                                         bias=prm[:, G, C_POS4SP:C_POS4SP + 1]).then_inc(*decay.one())
                    nc.scalar.activation(ra[u][:, :], ra[u][:, :], ACT.Exp, scale=prm[:, G, C_NEG4SP:C_NEG4SP + 1],
                                         bias=prm[:, G, C_NEG4SP:C_NEG4SP + 1]).then_inc(*decay.one())
                    act.wait_ge(*decay.at(n, 3 * u + 2))
                    act.wait_ge(*one_minus.at(n, u))
                    act.wait_ge(*x_sq.at(n, 1))
                    nc.scalar.activation(a2[:, :], ra[u][:, :], ACT.Square).then_inc(*decay.one())
                    act.wait_ge(*ring_ready.at(n, (R_I0, R_I1)[u] + 1))
                    act.sem_inc(settled, 1)
                    nc.scalar.activation(ri[u][:, :], bank((R_I0, R_I1)[u]), ACT.Tanh, scale=0.5,
                                         bias=prm[:, G, C_BI:C_BI + 1]).then_inc(*ring_act.one())

                def lru_root(u):
                    act.wait_ge(*one_minus.at(n, u + 1))
                    nc.scalar.activation(hs[u][:, :], hs[u][:, :], ACT.Sqrt).then_inc(*root.one())

                lru_in(0)
                split_w(n, GA0)
                act.wait_ge(*gw_dma.at(n, 4))
                act.wait_ge(*ring_ready.at(n, R_I1 + 1 - NR))
                nc.scalar.activation(gw_hi[:, :, :, :], gw_raw[:, :, :, :], ACT.Copy).then_inc(*gw_high.one())
                high_u(0)
                gate_l(0)
                split_w(n, GA1)
                act.wait_ge(*one_minus.at(n, 0))
                square_x(n, x_in.at(n, 1), x_sq, x_norm.at(n, 0))
                lru_in(1)
                s_copy(0)
                decays(0)
                high_u(1)
                split_w(n, GL1)
                s_exp(0)
                gate_a(0)
                decays(1)
                s_copy(1)
                root_x(n, x_ms.at(n, 1), x_root)
                lru_root(0)
                lru_root(1)
                split_w(n, KVG)
                s_exp(1)
                gate_a(1)
                high_p(0)
                s_copy(2)
                for half in range(2):
                    high_x(h_hi[:, 1 - par], g * P, half, bank(R_XT0 + half),
                           ring_ready.at(n, R_XT0 + half + 1), h_high.one())
                split_w(n, Q0)
                s_exp(2)
                gate_l(1)
                low_o(0)
                high_p(1)
                s_copy(3)
                split_w(n, Q1)
                s_exp(3)
                take_kv(n)
                low_o(1)
                high_p(2)
                split_w(n, NG + XL0)
                high_k(n)
                take_q(n, 0)
                low_o(2)
                high_p(3)
                split_w(n, NG + GL0)
                high_q(n, 0)
                take_q(n, 1)
                low_o(3)
                take_v(n)
                split_w(n, NG + XL1)
                high_q(n, 1)
                high_v(n)
                write_out(n, g, par, qp)

            def write_out(n, g, par, qp):
                q = qp * 2 + par
                act.wait_ge(*ya_done.at(n, NBLK))
                for_dst = y_dram[bass.ds(g * 2, 2), :, bass.ds(q * T, T)].rearrange("e p t -> p e t")
                act.dma_start(for_dst, ya[:, :, :]).then_inc(*ya_out.one())
                for u in range(UNITS):
                    act.wait_ge(*yl_done.at(n, u + 1))
                    act.dma_start(y_dram[bass.ds(g * UNITS + (EC // 2 + u), 1), :, bass.ds(q * T, T)].rearrange(
                        "e p t -> p (e t)"), hs[u][:, :]).then_inc(*yl_out[u].one())

            iterations(act, body)
            act.wait_ge(*ya_out.at(NITER, 0))
            for u in range(UNITS):
                act.wait_ge(*yl_out[u].at(NITER, 0))

        @block.vector
        def _(dve):
            stt = nc.vector.scalar_tensor_tensor

            def split_w(n, i):
                m, i = (n, i) if i < NG else (n + 1, i - NG)
                s = i % WSLOTS
                dve.wait_ge(*w_high.at(m, i + 1))
                nc.vector.tensor_tensor(w_lo[:, s, :, :], w_raw[:, s, :, :], f(w_hi[:, s, :, :]),
                                        ALU.subtract).then_inc(*w_low.one())

            dve.wait_ge(primed, 1)

            def stat_x(sq_in, xms):
                dve.wait_ge(*sq_in)
                nc.vector.tensor_scalar(xs[:, 1:2], xs[:, 0:1], 1.0 / D, EPS, ALU.mult, ALU.add
                                        ).then_inc(*xms.one())

            def norm_x(n, root_in, xrs, xnorm):
                dve.wait_ge(*root_in)
                nc.vector.reciprocal(xs[:, 3:4], xs[:, 2:3]).then_inc(*xrs.one())
                dve.wait_ge(*xrs.at(n, 1))
                stt(out=xb[:, :], in0=xb[:, :], scalar=xs[:, 3:4], in1=gain_row[:, :], op0=ALU.mult,
                    op1=ALU.mult).then_inc(*xnorm.one())

            def low_x(dst, hi, col, half, ps, ready, done):
                dve.wait_ge(*ready)
                at = (slice(None), slice(half * 4, half * 4 + 4), bass.ds(col, P))
                nc.vector.tensor_tensor(dst[at], ps.rearrange("p (k t) -> p k t", k=4), f(hi[at]),
                                        ALU.subtract).then_inc(*done)

            dve.wait_ge(pro_sq, NBLK)
            nc.vector.tensor_scalar(pro_stat[:, 1, :], pro_stat[:, 0, :], 1.0 / D, EPS, ALU.mult, ALU.add
                                    ).then_inc(pro_ms, 1)
            dve.wait_ge(pro_root, 1)
            nc.vector.reciprocal(pro_stat[:, 3, :], pro_stat[:, 2, :]).then_inc(pro_rs, 1)
            dve.wait_ge(pro_rs, 1)
            dve.wait_ge(early_in, 32)
            for b in range(NBLK):
                stt(out=pro_x[b], in0=pro_x[b], scalar=pro_stat[:, 3, b:b + 1], in1=gain_row[:, :],
                    op0=ALU.mult, op1=ALU.mult).then_inc(pro_norm, 1)
                if b == 1:
                    split_w(-1, KVG)
            for i in range(2 * NBLK):
                b, half = divmod(i, 2)
                low_x(h_lo[:, 0], h_hi[:, 0], b * P, half, ring[:, i % RING, :], (pro_hi, i + 1), (pro_lo, 1))
                if i in (3, 7):
                    split_w(-1, Q0 if i == 3 else Q1)
            dve.wait_ge(consts_in, N_CONST * 16)
            col = lambda c: prm[:, :, c]
            step = [0]

            def done(ins):
                step[0] += 1
                ins.then_inc(prm_step, 1)
                dve.wait_ge(prm_step, step[0])

            nc.vector.tensor_scalar(prev_mask[:, :, :], cap[:, 0, :].unsqueeze(1).broadcast_to([P, GQ, BLK]),
                                    0.0, None, ALU.is_lt).then_inc(masks, 1)
            nc.vector.tensor_scalar(col(C_T1), col(C_LAM), -1.0, None, ALU.mult).then_inc(masks, 1)
            dve.wait_ge(zeroed, 6)
            dve.wait_ge(masks, 2)
            done(nc.vector.tensor_tensor(col(C_T0), col(C_LAM), col(C_T1), ALU.min))
            dve.wait_ge(prm_act, 1)
            done(nc.vector.tensor_scalar(col(C_T0), col(C_T1), 1.0, None, ALU.add))
            dve.wait_ge(prm_act, 2)
            done(nc.vector.tensor_scalar(col(C_POS4SP), col(C_T0), 1.0, None, ALU.is_equal))
            done(nc.vector.tensor_scalar(col(C_T0), col(C_T0), -1.0, None, ALU.add))
            done(nc.vector.tensor_tensor(col(C_T0), col(C_T0), col(C_POS4SP), ALU.add))
            done(nc.vector.reciprocal(col(C_NEG4SP), col(C_T0)))
            done(nc.vector.tensor_tensor(col(C_T2), col(C_T2), col(C_NEG4SP), ALU.mult))
            done(nc.vector.tensor_tensor(col(C_T2), col(C_T2), col(C_POS4SP), ALU.add))
            done(nc.vector.tensor_tensor(col(C_T2), col(C_T2), col(C_T1), ALU.mult))
            done(nc.vector.tensor_scalar(col(C_T0), col(C_LAM), -1.0, 0.0, ALU.mult, ALU.max))
            done(nc.vector.tensor_tensor(col(C_T2), col(C_T2), col(C_T0), ALU.add))
            done(nc.vector.tensor_scalar(col(C_POS4SP), col(C_T2), 4.0, None, ALU.mult))
            done(nc.vector.tensor_scalar(col(C_NEG4SP), col(C_T2), -4.0, None, ALU.mult))
            done(nc.vector.tensor_scalar(col(C_BR), col(C_BR), 0.5, None, ALU.mult))
            done(nc.vector.tensor_scalar(col(C_BI), col(C_BI), 0.5, None, ALU.mult))

            def turn_k(n, g):
                dve.wait_ge(*k_high.at(n, 0))
                dve.wait_ge(*k_low.at(n, 0))
                nc.vector.tensor_scalar(krot[:, 0:BLK], k_carry[:, g, :], 1.0, None, ALU.mult
                                        ).then_inc(*k_turn.one())
                dve.wait_ge(*ring_act.at(n, FREED_BY_ACT.index(R_KV) + 1))
                dve.wait_ge(*q_rot.at(n, 0))
                dve.sem_inc(settled, 1)
                nc.vector.stream_shuffle(swp[0:HD, :], kraw[0:HD, :], SWAP).then_inc(*k_turn.one())
                nc.vector.tensor_tensor(krot[:, BLK:], kraw[0:HD, :], cosT[0:HD, :], ALU.mult
                                        ).then_inc(*k_turn.one())

            def add_k(n):
                dve.wait_ge(*k_turn.at(n, 3))
                dve.wait_ge(*k_sin.at(n, 1))
                nc.vector.tensor_tensor(krot[:, BLK:], krot[:, BLK:], swp[0:HD, :], ALU.add
                                        ).then_inc(*k_rot.one())

            def low_k(n, g):
                dve.wait_ge(*k_high.at(n, 2))
                nc.vector.tensor_tensor(k_lo[0:HD, :], krot[:, :], f(k_hi[0:HD, :]), ALU.subtract
                                        ).then_inc(*k_low.one())
                dve.wait_ge(*k_low.at(n, 1))
                nc.vector.tensor_copy(k_lo[HD:, :], k_lo[0:HD, :]).then_inc(*k_low.one())
                nc.vector.tensor_scalar(k_carry[:, g, :], krot[:, T:], 1.0, None, ALU.mult
                                        ).then_inc(*k_low.one())

            def turn_q(n, j):
                dve.wait_ge(*ring_act.at(n, FREED_BY_ACT.index((R_Q0, R_Q1)[j]) + 1))
                dve.wait_ge(*q_low.at(n, 2 * j))
                dve.wait_ge(*q_high.at(n, 2 * j))
                dve.wait_ge(*(q_rot.at(n, j) if j else k_rot.at(n, 1)))
                nc.vector.tensor_tensor(qrot[:, :], qraw[:, :], cosT[:, :], ALU.mult
                                        ).then_inc(*q_turn.one())
                nc.vector.stream_shuffle(swp[:, :], qraw[:, :], SWAP).then_inc(*q_turn.one())

            def add_q(n, j):
                dve.wait_ge(*q_turn.at(n, 2 * j + 1))
                dve.wait_ge(*q_sin.at(n, j + 1))
                nc.vector.tensor_tensor(qrot[:, :], qrot[:, :], swp[:, :], ALU.add
                                        ).then_inc(*q_rot.one())

            def low_q(n, j):
                for half in range(2):
                    rows = slice(half * HD, (half + 1) * HD)
                    other = slice((1 - half) * HD, (2 - half) * HD)
                    dve.wait_ge(*q_high.at(n, 2 * j + half + 1))
                    nc.vector.tensor_tensor(q_st[other, 2 * j + half, :], qrot[rows, :],
                                            f(q_st[rows, 2 * j + half, :]), ALU.subtract
                                            ).then_inc(*q_low.one())

            def previous_v(n, g):
                dve.wait_ge(*v_high.at(n, 0))
                dve.wait_ge(*v_kept.at(n, 0))
                nc.vector.tensor_scalar(vraw[:, 0, :], v_carry[:, g, :], 1.0, None, ALU.mult
                                        ).then_inc(*v_prev.one())

            def differ_v(n):
                dve.wait_ge(*v_prev.at(n, 1))
                dve.wait_ge(*ring_act.at(n, FREED_BY_ACT.index(R_VT) + 1))
                dve.wait_ge(*dv_low.at(n, 0))
                nc.vector.tensor_tensor(dvraw[:, :, :], vraw[:, 1:, :], vraw[:, :NBLK, :], ALU.subtract
                                        ).then_inc(*dv_raw.one())

            def low_v(n, g):
                dve.wait_ge(*v_high.at(n, 1))
                nc.vector.tensor_tensor(v_hl[:, :, HD:], vraw[:, :, :], f(v_hl[:, :, 0:HD]), ALU.subtract
                                        ).then_inc(*v_low.one())
                nc.vector.tensor_scalar(v_carry[:, g, :], vraw[:, NBLK, :], 1.0, None, ALU.mult
                                        ).then_inc(*v_kept.one())
                dve.wait_ge(*dv_high.at(n, 1))
                nc.vector.tensor_tensor(dv_hl[:, :, HD:], dvraw[:, :, :], f(dv_hl[:, :, 0:HD]),
                                        ALU.subtract).then_inc(*dv_low.one())

            dve.wait_ge(table_in, 32)
            turn_k(-1, 0)
            split_w(-1, NG + XL0)
            add_k(-1)
            low_k(-1, 0)
            turn_q(-1, 0)
            split_w(-1, NG + GL0)
            add_q(-1, 0)
            low_q(-1, 0)
            turn_q(-1, 1)
            previous_v(-1, 0)
            split_w(-1, NG + XL1)
            add_q(-1, 1)
            low_q(-1, 1)
            differ_v(-1)
            low_v(-1, 0)

            def body(n, g, par, qp, following, nxt_par):
                def silu_a(j):
                    dve.wait_ge(*ga_tanh.at(n, j + 1))
                    stt(out=ya[:, j, :], in0=ya[:, j, :], scalar=1.0, in1=bank((R_GA0, R_GA1)[j]),
                        op0=ALU.add, op1=ALU.mult).then_inc(*ring_dve.one())

                def softmax_a(b):
                    s, t = s_sb[:, b % 2], smax[:, b % 2]
                    dve.wait_ge(*s_cur.at(n, b + 1))
                    dve.sem_inc(settled, 1)
                    nc.vector.copy_predicated(s, prev_mask[:, :, :], ps_s[:, :, 0:BLK]
                                              ).then_inc(*s_sel.one())
                    dve.wait_ge(*s_sel.at(n, b + 1))
                    if b == 0:
                        if par == 0:
                            nc.vector.tensor_tensor(s, s, cap[:, qp, :].unsqueeze(1).broadcast_to([P, GQ, BLK]), ALU.min).then_inc(*s_cap.one())
                        else:
                            dve.sem_inc(s_cap.sem, 1)
                        dve.wait_ge(*s_cap.at(n, 1))
                    nc.vector.tensor_reduce(out=t[:, 0, :], in_=s, op=ALU.max, axis=AXX
                                            ).then_inc(*s_stat.one())
                    dve.wait_ge(*s_stat.at(n, 4 * b + 1))
                    sink = sink_all[:, bass.ds(g * GQ, GQ)]
                    stt(out=t[:, 1, :], in0=t[:, 0, :], scalar=HD ** -0.5, in1=sink, op0=ALU.mult,
                        op1=ALU.max).then_inc(*s_stat.one())
                    dve.wait_ge(*s_stat.at(n, 4 * b + 2))
                    nc.vector.tensor_scalar(t[:, 2, :], t[:, 1, :], -1.0, None, ALU.mult
                                            ).then_inc(*s_stat.one())
                    nc.vector.tensor_tensor(t[:, 3, :], sink, t[:, 1, :], ALU.subtract
                                            ).then_inc(*s_stat.one())

                def softmax_b(b):
                    d = sden[:, b % 2]
                    dve.wait_ge(*p_exp.at(n, (GQ + 1) * (b + 1)))
                    nc.vector.tensor_tensor(d[:, 2, :], d[:, 0, :], d[:, 1, :], ALU.add
                                            ).then_inc(*p_den.one())
                    dve.wait_ge(*p_den.at(n, 2 * b + 1))
                    nc.vector.reciprocal(d[:, 3, :], d[:, 2, :]).then_inc(*p_den.one())
                    dve.wait_ge(*p_den.at(n, 2 * b + 2))
                    nc.vector.tensor_tensor(s_sb[:, b % 2], s_sb[:, b % 2],
                                            d[:, 3, :].unsqueeze(2).broadcast_to([P, GQ, BLK]), ALU.mult
                                            ).then_inc(*p_norm.one())

                def low_p(b):
                    dve.wait_ge(*p_high.at(n, b + 1))
                    nc.vector.tensor_tensor(p_lo[:, :, :], ps_t[:, :, :], f(p_hi[:, :, :]), ALU.subtract
                                            ).then_inc(*p_low.one())

                def gather_o(b):
                    dve.wait_ge(*o_lowdone.at(n, b + 1))
                    dve.wait_ge(*ya_done.at(n, b))
                    pair = lambda ap, s: ap.rearrange("p (j s) t -> p s j t", s=2)[:, s]
                    for s in range(2):
                        nc.vector.tensor_tensor(o_sb[s * HD:(s + 1) * HD, :, :], pair(ps_v[0:HD], s),
                                                pair(o_low, s), ALU.add).then_inc(*o_sum.one())
                    dve.wait_ge(*o_sum.at(n, 2 * b + 2))
                    if b == 0:
                        dve.wait_ge(*ring_dve.at(n, FREED_BY_DVE.index(R_GA1) + 1))
                    y = ya[:, :, b * BLK:(b + 1) * BLK]
                    nc.vector.tensor_tensor(y, y, o_sb[:, :, :], ALU.mult).then_inc(*ya_done.one())

                def conv(u):
                    G = g * UNITS + u
                    dve.wait_ge(*u_conv.at(n, 3 * u))
                    dve.wait_ge(*xl_kept.at(n, u))
                    nc.vector.tensor_scalar(xl[:, 0:CONV - 1], x_carry[:, G, :], 1.0, None, ALU.mult
                                            ).then_inc(*xl_prev.one())
                    dve.wait_ge(*xl_prev.at(n, u + 1))
                    dve.wait_ge(*ring_act.at(n, FREED_BY_ACT.index((R_XL0, R_XL1)[u]) + 1))
                    for i in range(3):
                        tap = 2 - i
                        if i:
                            dve.wait_ge(*u_conv.at(n, 3 * u + i))
                        stt(out=cu[u][:, :], in0=xl[:, tap:tap + T],
                            scalar=prm[:, G, C_W0 + tap:C_W0 + tap + 1], in1=cu[u][:, :], op0=ALU.mult,
                            op1=ALU.add).then_inc(*u_conv.one())
                    nc.vector.tensor_scalar(x_carry[:, G, :], xl[:, T:], 1.0, None, ALU.mult
                                            ).then_inc(*xl_kept.one())

                def low_u(u):
                    dve.wait_ge(*u_high.at(n, u + 1))
                    nc.vector.tensor_tensor(u_lo[:, :], cu[u][:, :], f(u_hi[:, :]), ALU.subtract
                                            ).then_inc(*u_low.one())

                def silu_l(u):
                    dve.wait_ge(*gl_tanh.at(n, u + 1))
                    stt(out=gl[:, :], in0=gl[:, :], scalar=1.0, in1=bank((R_GL0, R_GL1)[u]),
                        op0=ALU.add, op1=ALU.mult).then_inc(*ring_dve.one())

                def lru_mid(u):
                    dve.wait_ge(*decay.at(n, 3 * u + 3))
                    stt(out=hs[u][:, :], in0=a2[:, :], scalar=1.0, in1=hs[u][:, :], op0=ALU.add,
                        op1=ALU.mult).then_inc(*one_minus.one())
                    dve.wait_ge(*ring_act.at(n, FREED_BY_ACT.index((R_I0, R_I1)[u]) + 1))
                    stt(out=ri[u][:, :], in0=ri[u][:, :], scalar=1.0, in1=cu[u][:, :], op0=ALU.add,
                        op1=ALU.mult).then_inc(*i_x.one())

                def lru_scan(u):
                    G = g * UNITS + u
                    dve.wait_ge(*scan_in.at(n, u + 1))
                    dve.wait_ge(*h_kept.at(n, u))
                    dve.wait_ge(*one_minus.at(n, u + 1))
                    nc.vector.tensor_tensor_scan(hs[u][:, :], ra[u][:, :], ri[u][:, :], h_carry[:, G, :],
                                                 ALU.mult, ALU.add).then_inc(*scanned.one())
                    dve.wait_ge(*scanned.at(n, u + 1))
                    nc.vector.tensor_scalar(h_carry[:, G, :], hs[u][:, T - 1:], 1.0, None, ALU.mult
                                            ).then_inc(*h_kept.one())

                conv(0)
                split_w(n, GA0)
                dve.wait_ge(*gw_high.at(n, 1))
                nc.vector.tensor_tensor(gw_lo[:, :, :, :], gw_raw[:, :, :, :], f(gw_hi[:, :, :, :]),
                                        ALU.subtract).then_inc(*gw_low.one())
                low_u(0)
                silu_l(0)
                split_w(n, GA1)
                stat_x(x_sq.at(n, 1), x_ms)
                conv(1)
                softmax_a(0)
                if nxt_par != par:
                    q = qp * 2 + par
                    dve.wait_ge(*stat_sum.at(q, 1))
                    dve.sem_inc(settled, 1)
                    nc.vector.tensor_scalar(sums[:, :, bass.ds(q * NBLK, NBLK)],
                                            ps_t[:, 0, 0:2 * NBLK].rearrange("p (w b) -> p w b", w=2), 1.0, None,
                                            ALU.mult).then_inc(*stat_kept.one())
                low_u(1)
                lru_mid(0)
                split_w(n, GL1)
                softmax_b(0)
                silu_a(0)
                lru_mid(1)
                softmax_a(1)
                norm_x(n, x_root.at(n, 1), x_rs, x_norm)
                lru_scan(0)
                split_w(n, KVG)
                lru_scan(1)
                softmax_b(1)
                silu_a(1)
                low_p(0)
                softmax_a(2)
                for half in range(2):
                    low_x(h_lo[:, 1 - par], h_hi[:, 1 - par], g * P, half, bank(R_XT0 + half),
                          h_high.at(n, half + 1), ring_dve.one())
                split_w(n, Q0)
                softmax_b(2)
                silu_l(1)
                gather_o(0)
                low_p(1)
                softmax_a(3)
                split_w(n, Q1)
                softmax_b(3)
                if nxt_par != par:
                    dve.wait_ge(table_in, (qp * 2 + par + 2) * 32)
                turn_k(n, following)
                gather_o(1)
                low_p(2)
                add_k(n)
                split_w(n, NG + XL0)
                low_k(n, following)
                turn_q(n, 0)
                gather_o(2)
                low_p(3)
                add_q(n, 0)
                split_w(n, NG + GL0)
                low_q(n, 0)
                turn_q(n, 1)
                previous_v(n, following)
                gather_o(3)
                add_q(n, 1)
                split_w(n, NG + XL1)
                low_q(n, 1)
                differ_v(n)
                low_v(n, following)

            iterations(dve, body)

        @block.tensor
        def _(pe):
            mm = nc.tensor.matmul
            passes = ((w_hi, h_hi), (w_hi, h_lo), (w_lo, h_hi))
            pe.wait_ge(early_in, 32)
            for i in range(2 * NBLK):
                b, half = divmod(i, 2)
                pe.wait_ge(pro_norm, b + 1)
                if i >= RING:
                    pe.wait_ge(pro_lo, i - RING + 1)
                for k in range(4):
                    c = half * 4 + k
                    last = nc.tensor.transpose(ring[:, i % RING, k * P:(k + 1) * P],
                                               pro_x[b][:, c * P:(c + 1) * P], ident[:, :])
                last.then_inc(pro_T, 1)
            pe.wait_ge(pro_lo, 2 * NBLK)

            def project(n, i, par):
                r = RING_OF_GROUP[i]
                pe.wait_ge(*w_low.at(n, i + 1))
                pe.wait_ge(*bank_free(n, r))
                for k in range(KC):
                    for j, (w, h) in enumerate(passes):
                        last = mm(bank(r), w[:, i % WSLOTS, k, :], h[:, par, k, :],
                                  start=(k == 0 and j == 0), stop=(k == KC - 1 and j == 2))
                last.then_inc(*ring_ready.one())

            def turn_v(n):
                pe.wait_ge(*ring_act.at(n, FREED_BY_ACT.index(R_KV) + 1))
                pe.wait_ge(*bank_free(n, R_VT))
                for b in range(NBLK):
                    last = nc.tensor.transpose(bank(R_VT)[:, b * P:(b + 1) * P],
                                               kraw[:, b * P:(b + 1) * P], ident[:, :])
                last.then_inc(*ring_ready.one())

            for i in range(KVG, NG):
                project(-1, i, 0)
            turn_v(-1)

            def body(n, g, par, qp, following, nxt_par):
                def score(b):
                    if b == 0:
                        pe.wait_ge(*q_low.at(n, 0))
                        pe.wait_ge(*k_low.at(n, 0))
                    pe.wait_ge(*s_sel.at(n, b))
                    for h in range(GQ):
                        for k, st, sp_ in ((k_hi, True, False), (k_lo, False, True)):
                            last = mm(ps_s[:, h, :], q_st[:, h, b * BLK:(b + 1) * BLK],
                                      k[:, b * BLK:(b + 2) * BLK], start=st, stop=sp_)
                    last.then_inc(*scores.one())

                def sum_squares():
                    pe.wait_ge(*sq_added.at(n, 0))
                    pe.wait_ge(*p_low.at(n, 0))
                    for which in range(2):
                        for b in range(NBLK):
                            i = which * NBLK + b
                            last = mm(ps_t[:, 0, i:i + 1], acc[:, 1 - par, which, b * BLK:(b + 1) * BLK],
                                      ones[:, :], start=True, stop=True)
                    last.then_inc(*stat_sum.one())

                def turn_p(b):
                    pe.wait_ge(*p_norm.at(n, b + 1))
                    if b == 0 and nxt_par != par:
                        pe.wait_ge(*stat_kept.at(qp * 2 + par, 1))
                    pe.wait_ge(*p_low.at(n, b))
                    for h in range(GQ):
                        last = nc.tensor.transpose(ps_t[:, h, :], s_sb[:, b % 2, h, :], ident[:, :])
                    last.then_inc(*p_T.one())

                def weigh_v(b):
                    if b == 0:
                        pe.wait_ge(*v_low.at(n, 0))
                        pe.wait_ge(*dv_low.at(n, 0))
                    pe.wait_ge(*p_low.at(n, b + 1))
                    pe.wait_ge(*p_cur.at(n, 2 * b + 2))
                    pe.wait_ge(*o_sum.at(n, 2 * b))
                    terms = ((v_hl, p_hi), (v_hl, p_lo), (dv_hl, p_hi_c), (dv_hl, p_lo_c))
                    for i, (v, p) in enumerate(terms):
                        last = mm(ps_v[:, :, :], v[:, b, :], p[:, :, :], start=(i == 0), stop=(i == 3))
                    last.then_inc(*pv.one())

                def gates(u):
                    pe.wait_ge(*u_low.at(n, u + 1))
                    if u == 0:
                        pe.wait_ge(*gw_low.at(n, 1))
                    for j in range(2):
                        r = ((R_R0, R_I0), (R_R1, R_I1))[u][j]
                        pe.wait_ge(*bank_free(n, r))
                        for i, (w, v) in enumerate(((gw_hi, u_hi), (gw_hi, u_lo), (gw_lo, u_hi))):
                            last = mm(bank(r), w[:, u, j, :], v[:, :], start=(i == 0), stop=(i == 2))
                        last.then_inc(*ring_ready.one())

                def turn_x():
                    pe.wait_ge(*x_norm.at(n, 1))
                    for half in range(2):
                        pe.wait_ge(*bank_free(n, R_XT0 + half))
                        for k in range(4):
                            c = half * 4 + k
                            last = nc.tensor.transpose(bank(R_XT0 + half)[:, k * P:(k + 1) * P],
                                                       xb[:, c * P:(c + 1) * P], ident[:, :])
                        last.then_inc(*ring_ready.one())

                project(n, XL0, par)
                project(n, GL0, par)
                project(n, XL1, par)
                score(0)
                if nxt_par != par:
                    sum_squares()
                gates(0)
                project(n, GA0, par)
                gates(1)
                score(1)
                project(n, GA1, par)
                turn_p(0)
                score(2)
                turn_x()
                project(n, GL1, par)
                weigh_v(0)
                turn_p(1)
                score(3)
                if nxt_par != par:
                    pe.wait_ge(*ring_dve.at(n, FREED_BY_DVE.index(R_XT1) + 1))
                project(n, KVG, nxt_par)
                weigh_v(1)
                turn_p(2)
                project(n, Q0, nxt_par)
                weigh_v(2)
                turn_p(3)
                project(n, Q1, nxt_par)
                weigh_v(3)
                turn_v(n)

            iterations(pe, body)

        for sig in signals:
            if sig is not s_cap:
                sig.checked(4, WSLOTS if sig in (w_high, w_low) else 0)
        for sig in quarterly:
            sig.checked(2)


def phase_b(nc, x, w_out, final_gain, y_dram, out, shared):
    ident, ones, wo_raw, egain, acc_sq, sums = shared
    with ExitStack() as ctx:
        def sb(name, shape, dt=F32):
            return ctx.enter_context(nc.sbuf_tensor(name, shape, dt))

        def sem(name):
            return ctx.enter_context(nc.semaphore(name))

        wo_hi = sb("wo_hi", [P, EC, D], F32R)
        wo_lo = sb("wo_lo", [P, EC, D], F32R)
        y_raw = sb("y_raw", [P, EC, P])
        y_hi = sb("y_hi", [P, 2, EC, P], F32R)
        y_lo = sb("y_lo", [P, 2, EC, P], F32R)
        res = sb("res", [P, 2, D])
        fgain = sb("fgain", [P, D])
        junk = sb("junk_b", [P, D], BF16)
        rms = sb("rms", [P, 2, NTOK])
        stat = sb("stat", [P, 2, 4])
        acc = ctx.enter_context(nc.psum_tensor("acc_b", [P, 2, 2, 2, D // 2], F32))
        stat_ps = acc[:, 1, 0, 0, 0:2 * NBLK]

        signals = []

        def signal(name, per, unit=1):
            s = Signal(ctx, nc, name, per, unit)
            signals.append(s)
            return s

        primed = sem("primed_b")
        fgain_in = sem("fgain_in")
        stat_done = sem("stat_done")
        rms_step = sem("rms_step")
        rms_root = sem("rms_root")
        settled = sem("settled_b")
        wo_in = [signal(f"wo_in{s}", 1, 16) for s in range(WSLOTS)]
        wo_high = signal("wo_high", 1)
        wo_low = signal("wo_low", 1)
        y_in = signal("y_in", 2, 16)
        y_high = signal("y_high", 2)
        y_low = signal("y_low", 2)
        x_in = [signal(f"x_in_b{s}", 1, 16) for s in range(2)]
        product = signal("product", 2)
        added = signal("added", 4)
        sq_done = signal("sq_done", 2)
        mean = signal("mean", 2)
        rooted = signal("rooted", 2)
        recip = signal("recip", 2)
        normed = signal("normed", 2)
        res_free = [signal(f"res_free{s}", 1) for s in range(2)]
        stored = [Signal(ctx, nc, f"stored{s}", 1, 16, lead=0) for s in range(2)]

        f = lambda ap: ap.bitcast(F32)
        STEPS = NTOK // 2
        TURNS = EC // WSLOTS
        at_step = lambda m, s: bass.ds(m * (2 * P) + s * P, P)
        block = ctx.enter_context(nc.Block())

        @block.sync
        def _(sp):
            sp.wait_ge(primed, 1)

            def load_y(m, s):
                sp.wait_ge(*y_low.at(m, s))
                sp.dma_start(y_raw[:, :, :], y_dram[:, :, at_step(m, s)].rearrange("e p t -> p e t")
                             ).then_inc(*y_in.one())

            def load_x(m, s):
                sp.wait_ge(*res_free[s].at(m, 0))
                sp.dma_start(res[:, s, :], x[0, at_step(m, s), :]).then_inc(*x_in[s].one())

            def load_w(i, s):
                sp.wait_ge(*wo_low.at(i * WSLOTS + (s - WSLOTS), 1))
                sp.dma_start(wo_raw[:, s, :], w_out[0, bass.ds(i * (WSLOTS * P) + s * P, P), :]
                             ).then_inc(*wo_in[s].one())

            load_y(0, 0)
            load_y(0, 1)
            with sp.Fori(1, TURNS) as i:
                for s in range(WSLOTS):
                    load_w(i, s)
            for s in range(EC - TURNS * WSLOTS):
                load_w(TURNS, s)
            for s in range(2):
                load_x(0, s)
            sp.dma_start(fgain[:, :], final_gain.rearrange("(o d) -> o d", o=1).broadcast_to([P, D])
                         ).then_inc(fgain_in, 16)
            with sp.Fori(1, STEPS) as m:
                for s in range(2):
                    load_y(m, s)
                    load_x(m, s)
            sp.wait_ge(*y_low.at(STEPS, 0))
            sp.sem_inc(y_in.sem, 16)

        @block.gpsimd
        def _(pool):
            for s in signals:
                pool.sem_inc(s.sem, s.prime)
            pool.sem_inc(primed, 1)
            with pool.Fori(0, STEPS) as m:
                for s in range(2):
                    pool.wait_ge(*normed.at(m, s + 1))
                    pool.sem_inc(settled, 1)
                    pool.dma_start(out[0, at_step(m, s), :], res[:, s, :]).then_inc(*stored[s].one())
                    pool.wait_ge(*stored[s].at(m, 1))
                    pool.sem_inc(res_free[s].sem, 1)

        @block.scalar
        def _(act):
            act.wait_ge(primed, 1)

            def high_y(m, s):
                act.wait_ge(*y_in.at(m, s + 1))
                act.wait_ge(*product.at(m, s - 1))
                nc.scalar.activation(y_hi[:, s, :, :], y_raw[:, :, :], ACT.Copy).then_inc(*y_high.one())

            def high_w(i, s):
                e = i * WSLOTS + s
                act.wait_ge(*wo_in[s].at(i, 0))
                act.sem_inc(settled, 1)
                nc.scalar.activation(wo_hi[:, e, :] if type(e) is int else
                                     wo_hi[:, bass.ds(e, 1), :].rearrange("p o d -> p (o d)"),
                                     wo_raw[:, s, :], ACT.Copy, scale=egain[:, bass.ds(e, 1)]
                                     ).then_inc(*wo_high.one())

            def mean_square(m, s):
                act.wait_ge(*added.at(m, 2 * s + 2))
                nc.scalar.activation(junk[:, :], res[:, s, :], ACT.Square, accum_out=stat[:, s, 0:1]
                                     ).then_inc(*sq_done.one())
                act.wait_ge(*mean.at(m, s + 1))
                nc.scalar.activation(stat[:, s, 2:3], stat[:, s, 1:2], ACT.Sqrt).then_inc(*rooted.one())

            high_y(0, 0)
            for s in range(WSLOTS):
                high_w(0, s)
            high_y(0, 1)
            with act.Fori(1, TURNS) as i:
                for s in range(WSLOTS):
                    high_w(i, s)
            for s in range(EC - TURNS * WSLOTS):
                high_w(TURNS, s)
            act.wait_ge(rms_step, 3)
            nc.scalar.activation(rms[:, :, :], rms[:, :, :], ACT.Sqrt).then_inc(rms_root, 1)
            high_y(1, 0)
            mean_square(0, 0)
            mean_square(0, 1)
            with act.Fori(1, STEPS) as m:
                for s in range(2):
                    high_y(m + s, 1 - s)
                    mean_square(m, s)

        @block.vector
        def _(dve):
            stt = nc.vector.scalar_tensor_tensor
            dve.wait_ge(primed, 1)

            def low_y(m, s):
                dve.wait_ge(*y_high.at(m, s + 1))
                nc.vector.tensor_tensor(y_lo[:, s, :, :], y_raw[:, :, :], f(y_hi[:, s, :, :]), ALU.subtract
                                        ).then_inc(*y_low.one())

            def low_w(i, s):
                e = i * WSLOTS + s
                dve.wait_ge(*wo_high.at(e, 1))
                at = lambda w: w[:, bass.ds(e, 1), :].rearrange("p o d -> p (o d)")
                stt(out=at(wo_lo), in0=wo_raw[:, s, :], scalar=egain[:, bass.ds(e, 1)],
                    in1=f(at(wo_hi)), op0=ALU.mult, op1=ALU.subtract).then_inc(*wo_low.one())

            def finish(m, s):
                dve.wait_ge(*product.at(m, s + 1))
                dve.wait_ge(*x_in[s].at(m, 1))
                r = res[:, s, :].rearrange("p (h c) -> p h c", h=2)
                for g in range(2):
                    if g:
                        dve.wait_ge(*added.at(m, 2 * s + 1))
                    stt(out=r, in0=acc[:, s, g, :, :], scalar=rms[:, g, bass.ds(m * 2 + s, 1)], in1=r,
                        op0=ALU.mult, op1=ALU.add).then_inc(*added.one())
                dve.wait_ge(*sq_done.at(m, s + 1))
                nc.vector.tensor_scalar(stat[:, s, 1:2], stat[:, s, 0:1], 1.0 / D, EPS, ALU.mult, ALU.add
                                        ).then_inc(*mean.one())
                dve.wait_ge(*rooted.at(m, s + 1))
                nc.vector.reciprocal(stat[:, s, 3:4], stat[:, s, 2:3]).then_inc(*recip.one())
                dve.wait_ge(*recip.at(m, s + 1))
                stt(out=res[:, s, :], in0=res[:, s, :], scalar=stat[:, s, 3:4], in1=fgain[:, :],
                    op0=ALU.mult, op1=ALU.mult).then_inc(*normed.one())

            dve.wait_ge(stat_done, 1)
            nc.vector.tensor_scalar(sums[:, :, NTOK:], stat_ps.rearrange("p (g t) -> p g t", g=2), 1.0, None,
                                    ALU.mult).then_inc(rms_step, 1)
            low_y(0, 0)
            for s in range(WSLOTS):
                low_w(0, s)
            low_y(0, 1)
            with dve.Fori(1, TURNS) as i:
                for s in range(WSLOTS):
                    low_w(i, s)
            for s in range(EC - TURNS * WSLOTS):
                low_w(TURNS, s)
            dve.wait_ge(rms_step, 1)
            for g, k in ((0, 4.0), (1, 16.0)):
                nc.vector.tensor_scalar(rms[:, g, :], sums[:, g, NBLK:], 1.0 / 1024, k * EPS, ALU.mult, ALU.add
                                        ).then_inc(rms_step, 1)
            dve.wait_ge(rms_root, 1)
            nc.vector.reciprocal(rms[:, :, :], rms[:, :, :]).then_inc(rms_step, 1)
            dve.wait_ge(rms_step, 4)
            dve.wait_ge(fgain_in, 16)
            low_y(1, 0)
            finish(0, 0)
            finish(0, 1)
            with dve.Fori(1, STEPS) as m:
                for s in range(2):
                    low_y(m + s, 1 - s)
                    finish(m, s)

        @block.tensor
        def _(pe):
            for g in range(2):
                for t in range(NBLK):
                    last = nc.tensor.matmul(stat_ps[:, g * NBLK + t:g * NBLK + t + 1],
                                            acc_sq[:, (NQUART - 1) % 2, g, t * P:(t + 1) * P], ones[:, :],
                                            start=True, stop=True)
            last.then_inc(stat_done, 1)
            pe.wait_ge(primed, 1)

            def chunk(s, e):
                g = e // (EC // 2)
                for j, (y, w) in enumerate(((y_hi, wo_hi), (y_hi, wo_lo), (y_lo, wo_hi))):
                    for h in range(2):
                        last = nc.tensor.matmul(acc[:, s, g, h, :], y[:, s, e, :],
                                                w[:, e, h * (D // 2):(h + 1) * (D // 2)],
                                                start=(e % (EC // 2) == 0 and j == 0),
                                                stop=(e % (EC // 2) == EC // 2 - 1 and j == 2))
                return last

            pe.wait_ge(*y_low.at(0, 1))
            for e in range(EC + LAG):
                if e < EC:
                    pe.wait_ge(*wo_low.at(e, 1))
                    last = chunk(0, e)
                    if e == EC - 1:
                        last.then_inc(*product.one())
                if e == LAG:
                    pe.wait_ge(*y_low.at(0, 2))
                    pe.wait_ge(rms_step, 1)
                if e >= LAG:
                    last = chunk(1, e - LAG)
            last.then_inc(*product.one())
            with pe.Fori(1, STEPS) as m:
                for s in range(2):
                    pe.wait_ge(*y_low.at(m, s + 1))
                    pe.wait_ge(*added.at(m, 2 * s + 2 - 4))
                    for e in range(EC):
                        last = chunk(s, e)
                    last.then_inc(*product.one())


def rope_tables():
    half = ROT // 2
    inv = np.float32(500000.0) ** (-np.arange(0, ROT, 2, dtype=np.float32) / np.float32(ROT))
    ang = np.arange(SEQ, dtype=np.float32)[None, :] * inv.astype(np.float32)[:, None]
    cos, sin = np.cos(ang), np.sin(ang)
    c = np.ones((P, SEQ), np.float32)
    s = np.zeros((P, SEQ), np.float32)
    for head in range(2):
        r = head * HD
        c[r:r + half], c[r + half:r + ROT] = cos, cos
        s[r:r + half], s[r + half:r + ROT] = -sin, sin
    return c, s


_INPUTS = ["x", "ln_gain", "w_in", "sinks", "conv_w", "conv_b", "w_rgate", "b_rgate", "w_igate", "b_igate",
           "lru_lambda", "attn_out_gain", "lru_out_gain", "w_out", "final_gain"]


def constants():
    cos, sin = rope_tables()
    query, key = np.arange(BLK)[:, None], np.arange(BLK)[None, :]
    prev = key > query
    cap = np.full((P, 2, BLK), BIG, np.float32)
    cap[:, 0, :][prev] = NEG
    return {"rope_cos": cos, "rope_sin": sin, "first_cap": cap,
            "identity": np.eye(P, dtype=np.float32)}


def kernel(**inputs):
    import concourse.bacc as bacc
    from concourse.bass_utils import run_bass_kernel_spmd

    nc = bacc.Bacc("TRN2", target_bir_lowering=False, num_devices=1)
    arrays, args = {}, {}
    for name, a in {**{k: inputs[k] for k in _INPUTS}, **constants()}.items():
        a = np.ascontiguousarray(a)
        arrays[name + "_d"] = a
        args[name] = nc.dram_tensor(name + "_d", a.shape, mybir.dt.from_np(a.dtype), kind="ExternalInput").ap()
    out = nc.dram_tensor("out_d", (1, SEQ, D), F32, kind="ExternalOutput").ap()
    hymba_kernel(nc, out=out, **args)
    r = run_bass_kernel_spmd(nc, [arrays], core_ids=[0])
    return r.results[0]["out_d"]
```

```python
from contextlib import ExitStack

import numpy as np

import concourse.bass as bass
from concourse import mybir

F32 = mybir.dt.float32
F32R = mybir.dt.float32r
BF16 = mybir.dt.bfloat16
U8 = mybir.dt.uint8
ALU = mybir.AluOpType
ACT = mybir.ActivationFunctionType
AXX = mybir.AxisListType.X

P = 128
SEQ, D = 2048, 1024
KC = D // P
HD = 64
KV, GQ = 4, 4
BLK = 128
ROT = HD // 4
T = 512
NBLK = T // BLK
NQUART = SEQ // T
NITER = NQUART * KV
LRU_W = 1024
UNITS = LRU_W // P // KV
BW = 64
EPS = 1e-6
MIX = 2048
EC = MIX // P
NTOK = SEQ // P
LAG = 5
CONV = 4
BIG = 3.0e38
NEG = -1.0e30

COL_Q, COL_K, COL_V = 0, 1024, 1024 + KV * HD
COL_GA = COL_V + KV * HD
COL_XL = COL_GA + 1024
COL_GL = COL_XL + LRU_W

XL0, GL0, XL1, GA0, GA1, GL1, KVG, Q0, Q1 = range(9)
NG = 9
WSLOTS = 3
(R_XL0, R_GL0, R_XL1, R_R0, R_I0, R_GA0, R_R1, R_I1, R_GA1, R_XT0, R_XT1, R_GL1, R_KV, R_Q0, R_Q1,
 R_VT) = range(16)
NR = 16
RING = 4
RING_OF_GROUP = [R_XL0, R_GL0, R_XL1, R_GA0, R_GA1, R_GL1, R_KV, R_Q0, R_Q1]
FREED_BY_DVE = [R_GL0, R_GA0, R_GA1, R_XT0, R_XT1, R_GL1]
FREED_BY_ACT = [r for r in range(NR) if r not in FREED_BY_DVE]

(C_W0, C_W1, C_W2, C_W3, C_CB, C_BR, C_BI, C_LAM, C_NEG4SP, C_POS4SP, C_T0, C_T1, C_T2) = range(13)
NPRM = 13


SWAP = [(i + ROT // 2) % ROT if i < ROT else i for i in range(32)]


class Record:
    pass


class Signal:

    def __init__(self, ctx, nc, name, per, unit=1, lead=1, ahead=0):
        self.sem = ctx.enter_context(nc.semaphore(name))
        self.name, self.per, self.unit, self.lead, self.count = name, per, unit, lead, 0
        self.prime = (lead * per - ahead) * unit
        self.ahead = ahead

    def at(self, n, k):
        return self.sem, n * (self.per * self.unit) + (self.lead * self.per + k) * self.unit

    def one(self):
        self.count += 1
        return self.sem, self.unit

    def checked(self, bodies, beyond=0):
        assert self.count == bodies * self.per + self.ahead + beyond, (self.name, self.count, self.per)


def hymba_kernel(nc, x, ln_gain, w_in, sinks, conv_w, conv_b, w_rgate, b_rgate, w_igate, b_igate,
                 lru_lambda, attn_out_gain, lru_out_gain, w_out, final_gain,
                 rope_cos, rope_sin, first_cap, identity, out):
    y_dram = nc.dram_tensor("y_scratch", (EC, P, SEQ), F32, kind="Internal").ap()

    with ExitStack() as top:
        def sb(name, shape, dt=F32):
            return top.enter_context(nc.sbuf_tensor(name, shape, dt))

        both = Record()
        both.ident = sb("ident", [P, P])
        both.ones = sb("ones", [P, 1])
        both.egain = sb("egain", [P, EC])
        both.acc = sb("acc", [P, 2, 2, T])
        both.sums = sb("sums", [P, 2, NTOK + NBLK])
        both.w_raw = sb("w_raw", [P, WSLOTS, D])
        both.w_hi = sb("w_hi", [P, WSLOTS, D], F32R)
        both.w_lo = sb("w_lo", [P, WSLOTS, D], F32R)
        both.rows = sb("rows", [P, 2, D])
        both.split = sb("split", [P, 2, 2, KC * T], F32R)

        signals_b = signals_of_phase_b(nc, top)
        block = top.enter_context(nc.Block())
        done_a = phase_a(nc, top, block, both, signals_b, x, ln_gain, w_in, sinks, conv_w, conv_b, w_rgate,
                         b_rgate, w_igate, b_igate, lru_lambda, attn_out_gain, lru_out_gain, w_out,
                         rope_cos, rope_sin, first_cap, identity, y_dram)
        phase_b(nc, block, both, signals_b, done_a, x, w_out, final_gain, y_dram, out)


def phase_a(nc, top, block, both, signals_b, x, ln_gain, w_in, sinks, conv_w, conv_b, w_rgate,
            b_rgate, w_igate, b_igate, lru_lambda, attn_out_gain, lru_out_gain, w_out,
            rope_cos, rope_sin, first_cap, identity, y_dram):
    ident, ones, egain, acc, sums = both.ident, both.ones, both.egain, both.acc, both.sums
    by_chunk = lambda w: w[:, :, :].rearrange("p s (k c) -> p s k c", k=KC)
    w_raw, w_hi, w_lo = by_chunk(both.w_raw), by_chunk(both.w_hi), by_chunk(both.w_lo)
    xb = both.rows[:, 0, :]
    gain_row = both.rows[:, 1, :]
    h_hi = both.split[:, :, 0, :].rearrange("p q (k t) -> p q k t", k=KC)
    h_lo = both.split[:, :, 1, :].rearrange("p q (k t) -> p q k t", k=KC)
    with ExitStack() as ctx:
        signals = []

        def sb(name, shape, dt=F32):
            return ctx.enter_context(nc.sbuf_tensor(name, shape, dt))

        def sem(name):
            return top.enter_context(nc.semaphore(name))

        def signal(name, per, unit=1, ahead=0):
            s = Signal(top, nc, name, per, unit, lead=2, ahead=ahead)
            signals.append(s)
            return s

        xs = sb("x_stat", [P, 4])
        cosT = sb("cosT", [P, T])
        sinT = sb("sinT", [P, T])
        prev_mask = sb("prev_mask", [P, GQ, BLK], U8)
        cap = sb("cap", [P, 2, BLK])
        sink_all = sb("sink_all", [P, KV * GQ])
        prm = sb("prm", [P, LRU_W // P, NPRM])
        kraw = sb("kraw", [P, T])
        swp = sb("swp", [P, T])
        krot = sb("krot", [HD, BLK + T])
        k_hi = sb("k_hi", [P, BLK + T], F32R)
        k_lo = sb("k_lo", [P, BLK + T], F32R)
        kc_ol = sb("kc_ol", [P, KV, BLK])
        k_carry, o_low = kc_ol[0:HD], kc_ol[HD:]
        vraw = sb("vraw", [P, 1 + NBLK, HD])
        v_hl = sb("v_hl", [P, 1 + NBLK, 2 * HD], F32R)
        dvraw = sb("dvraw", [P, NBLK, HD])
        dv_hl = sb("dv_hl", [P, NBLK, 2 * HD], F32R)
        v_carry = sb("v_carry", [P, KV, HD])
        qraw = sb("qraw", [P, T])
        qrot = sb("qrot", [P, T])
        q_st = sb("q_st", [P, GQ, T], F32R)
        s_sb = sb("s_sb", [P, 2, GQ, BLK])
        smax = sb("smax", [P, 2, 4, GQ])
        sden = sb("sden", [P, 2, 4, GQ])
        p_hi = sb("p_hi", [P, GQ, BLK], F32R)
        p_lo = sb("p_lo", [P, GQ, BLK], F32R)
        p_hi_c = sb("p_hi_c", [P, GQ, BLK], F32R)
        p_lo_c = sb("p_lo_c", [P, GQ, BLK], F32R)
        o_sb = sb("o_sb", [P, 2, BLK])
        ya = sb("ya", [P, 2, T])
        sq = sb("sq", [P, T])
        xl = sb("xl", [P, CONV - 1 + T])
        cu = [sb(f"cu{u}", [P, T]) for u in range(UNITS)]
        u_hi = sb("u_hi", [P, T], F32R)
        u_lo = sb("u_lo", [P, T], F32R)
        ra = [sb(f"ra{u}", [P, T]) for u in range(UNITS)]
        a2 = sb("a2", [P, T])
        ri = [sb(f"ri{u}", [P, T]) for u in range(UNITS)]
        gl = sb("gl", [P, T])
        hs = [sb(f"hs{u}", [P, T]) for u in range(UNITS)]
        x_carry = sb("x_carry", [P, LRU_W // P, CONV - 1])
        h_carry = sb("h_carry", [P, LRU_W // P, 1])
        gw_raw = sb("gw_raw", [P, UNITS, 2, P])
        gw_hi = sb("gw_hi", [P, UNITS, 2, P], F32R)
        gw_lo = sb("gw_lo", [P, UNITS, 2, P], F32R)

        ring = ctx.enter_context(nc.psum_tensor("ring", [P, RING, T], F32))
        ps_s = ctx.enter_context(nc.psum_tensor("ps_s", [P, GQ, 2 * BLK], F32))
        ps_t = ctx.enter_context(nc.psum_tensor("ps_t", [P, GQ, BLK], F32))
        ps_v = ctx.enter_context(nc.psum_tensor("ps_v", [P, GQ, BLK], F32))

        primed = sem("primed")
        consts_in = sem("consts_in")
        zeroed = sem("zeroed")
        prm_step = sem("prm_step")
        prm_act = sem("prm_act")
        pro_x_in = [sem(f"pro_x_in{b}") for b in range(NBLK)]
        early_in = sem("early_in")
        x_early_root = sem("x_early_root")
        pro_sq, pro_ms, pro_root, pro_rs, pro_norm, pro_T, pro_hi, pro_lo = (
            sem("pro_" + s) for s in ("sq", "ms", "root", "rs", "norm", "T", "hi", "lo"))
        masks = sem("masks")
        table_in = sem("table_in")
        settled = sem("settled")

        w_in_dma = [signal(f"w_in_dma{s}", 4 if s == 0 else 3, 16, ahead=2 if s == 0 else 1)
                    for s in range(WSLOTS)]
        W_DMA_AT = {XL0: 1, GL0: 1, XL1: 1, GA0: 2, GA1: 2, GL1: 2, KVG: 4, Q0: 3, Q1: 3}
        w_high = signal("w_high", NG, ahead=3)
        w_low = signal("w_low", NG, ahead=3)
        ring_ready = signal("ring_ready", NR, ahead=4)
        ring_act = signal("ring_act", len(FREED_BY_ACT), ahead=4)
        ring_dve = signal("ring_dve", len(FREED_BY_DVE))
        x_in = signal("x_in", 1, 16)
        x_sq = signal("x_sq", 1)
        x_ms = signal("x_ms", 1)
        x_root = signal("x_root", 1)
        x_rs = signal("x_rs", 1)
        x_norm = signal("x_norm", 1)
        h_high = signal("h_high", 2)
        k_turn = signal("k_turn", 3, ahead=3)
        k_sin = signal("k_sin", 1, ahead=1)
        k_rot = signal("k_rot", 1, ahead=1)
        k_high = signal("k_high", 2, ahead=2)
        k_low = signal("k_low", 3, ahead=3)
        q_turn = signal("q_turn", 4, ahead=4)
        q_sin = signal("q_sin", 2, ahead=2)
        q_rot = signal("q_rot", 2, ahead=2)
        q_high = signal("q_high", 4, ahead=4)
        q_low = signal("q_low", 4, ahead=4)
        v_prev = signal("v_prev", 1, ahead=1)
        v_high = signal("v_high", 1, ahead=1)
        v_low = signal("v_low", 1, ahead=1)
        dv_raw = signal("dv_raw", 1, ahead=1)
        dv_high = signal("dv_high", 1, ahead=1)
        dv_low = signal("dv_low", 1, ahead=1)
        v_kept = signal("v_kept", 1, ahead=1)
        scores = signal("scores", NBLK)
        s_cur = signal("s_cur", NBLK)
        s_sel = signal("s_sel", NBLK)
        s_cap = signal("s_cap", 1)
        s_stat = signal("s_stat", 4 * NBLK)
        p_exp = signal("p_exp", NBLK * (GQ + 1))
        p_den = signal("p_den", 2 * NBLK)
        p_norm = signal("p_norm", NBLK)
        p_T = signal("p_T", NBLK)
        p_high = signal("p_high", NBLK)
        p_low = signal("p_low", NBLK)
        p_cur = signal("p_cur", 2 * NBLK)
        pv = signal("pv", NBLK)
        o_lowdone = signal("o_lowdone", NBLK)
        o_sum = signal("o_sum", 2 * NBLK)
        ga_tanh = signal("ga_tanh", 2)
        ya_done = signal("ya_done", NBLK)
        ya_out = signal("ya_out", 1, 16)
        sq_made = signal("sq_made", 4)
        sq_added = signal("sq_added", 4)
        xl_prev = signal("xl_prev", UNITS)
        xl_in = signal("xl_in", UNITS)
        u_conv = signal("u_conv", 3 * UNITS)
        xl_kept = signal("xl_kept", UNITS)
        u_high = signal("u_high", UNITS)
        u_low = signal("u_low", UNITS)
        gw_dma = signal("gw_dma", 4, 16)
        gw_high = signal("gw_high", 1)
        gw_low = signal("gw_low", 1)
        decay = signal("decay", 3 * UNITS)
        one_minus = signal("one_minus", UNITS)
        root = signal("root", UNITS)
        i_x = signal("i_x", UNITS)
        scan_in = signal("scan_in", UNITS)
        scanned = signal("scanned", UNITS)
        h_kept = signal("h_kept", UNITS)
        gl_tanh = signal("gl_tanh", UNITS)
        yl_done = signal("yl_done", UNITS)
        yl_out = [signal(f"yl_out{u}", 1, 16) for u in range(UNITS)]
        stat_sum = Signal(top, nc, "stat_sum", 1)
        stat_kept = Signal(top, nc, "stat_kept", 1)
        quarterly = [stat_sum, stat_kept]
        acc_zero = sem("acc_zero")

        bank = lambda r: ring[:, r % RING, :]
        f = lambda ap: ap.bitcast(F32)

        pro_x = [xb, ya[:, :, :].rearrange("p j t -> p (j t)"),
                 s_sb[:, :, :, :].rearrange("p s h t -> p (s h t)"),
                 acc[:, 1, :, :].rearrange("p w t -> p (w t)")]
        flat = lambda ap: ap.rearrange("p h t -> p (h t)")
        pro_bank = lambda i: (ring[:, i, :] if i < RING else flat(ps_s[:, 2 * (i - RING):2 * (i - RING) + 2, :])
                              if i < RING + 2 else flat((ps_t, ps_v)[i - RING - 2][:, :, :]))
        pro_stat = smax[:, 0, :, :]

        def bank_free(n, r):
            before = (r - RING) % NR
            late = 0 if r >= RING else 1
            if before in FREED_BY_ACT:
                return ring_act.at(n, FREED_BY_ACT.index(before) + 1 - late * len(FREED_BY_ACT))
            return ring_dve.at(n, FREED_BY_DVE.index(before) + 1 - late * len(FREED_BY_DVE))

        def iterations(eng, body, quarter_start=None):
            with eng.Fori(0, NQUART // 2) as qp:
                for par in range(2):
                    if quarter_start:
                        quarter_start(qp, par)
                    eng.sem_inc(settled, 1)
                    with eng.Fori(0, KV - 1) as g:
                        body(qp * (2 * KV) + (g + par * KV), g, par, qp, g + 1, par)
                    eng.sem_inc(settled, 1)
                    body(qp * (2 * KV) + (KV - 1 + par * KV), KV - 1, par, qp, 0, 1 - par)

        N_CONST = 12

        @block.sync
        def _(sp):
            for b in range(NBLK):
                sp.dma_start(pro_x[b], x[0, b * P:(b + 1) * P, :]).then_inc(pro_x_in[b], 16)
                if b == 0:
                    sp.dma_start(gain_row, ln_gain.broadcast_to([P, D])).then_inc(early_in, 16)
                    sp.dma_start(ident[:, :], identity).then_inc(early_in, 16)

            def load_consts():
                chan = lambda v: v.rearrange("o (u p) -> p (o u)", p=P)
                sp.dma_start(sink_all[:, :], sinks.broadcast_to([P, KV * GQ])).then_inc(consts_in, 16)
                with nc.allow_non_contiguous_dma(reason="per-channel parameters, a few KB once"):
                    for i in range(CONV):
                        sp.dma_start(prm[:, :, C_W0 + i], conv_w[0, i:i + 1, :].rearrange(
                            "o (u p) -> p (o u)", p=P)).then_inc(consts_in, 16)
                    for col, v in ((C_CB, conv_b), (C_BR, b_rgate), (C_BI, b_igate), (C_LAM, lru_lambda)):
                        sp.dma_start(prm[:, :, col], chan(v)).then_inc(consts_in, 16)
                    for i, v in enumerate((attn_out_gain, lru_out_gain)):
                        sp.dma_start(egain[:, i * (EC // 2):(i + 1) * (EC // 2)],
                                     v.rearrange("o (e p) -> p (o e)", p=P)).then_inc(consts_in, 16)
                sp.dma_start(cap[:, :, :], first_cap).then_inc(consts_in, 16)

            def load_group(n, i, col):
                sp.wait_ge(*w_low.at(n, i + 1 - WSLOTS))
                sp.dma_start(w_raw[:, i % WSLOTS, :, :],
                             w_in[0, :, bass.ds(col, P)].rearrange("(k p) c -> p k c", p=P)
                             ).then_inc(*w_in_dma[i % WSLOTS].one())

            def load_next(n, g):
                sp.wait_ge(*w_low.at(n, KVG + 1 - WSLOTS))
                for half, col in ((0, COL_K), (1, COL_V)):
                    sp.dma_start(w_raw[:, 0, :, half * HD:(half + 1) * HD],
                                 w_in[0, :, bass.ds(g * HD + col, HD)].rearrange("(k p) c -> p k c", p=P)
                                 ).then_inc(*w_in_dma[0].one())
                load_group(n, Q0, g * (2 * P) + COL_Q)
                load_group(n, Q1, g * (2 * P) + (COL_Q + P))

            def load_tables(col):
                sp.dma_start(cosT[:, :], rope_cos[:, bass.ds(col, T)]).then_inc(table_in, 16)
                sp.dma_start(sinT[:, :], rope_sin[:, bass.ds(col, T)]).then_inc(table_in, 16)

            sp.wait_ge(primed, 1)
            load_next(-1, 0)
            load_tables(0)
            load_consts()
            sp.wait_ge(zeroed, 6)
            sp.wait_ge(pro_T, 2 * NBLK)

            def body(n, g, par, qp, following, nxt_par):
                load_group(n, XL0, g * (2 * P) + COL_XL)
                load_group(n, GL0, g * (2 * P) + COL_GL)
                sp.wait_ge(*ring_ready.at(n, R_XT1 + 1 - NR))
                first = (qp * (2 * KV) + (g + KV)) if par == 0 else (g + 2 * KV)
                sp.dma_start(xb, x[0, bass.ds(first * P, P), :]).then_inc(*x_in.one())
                load_group(n, XL1, g * (2 * P) + (COL_XL + P))
                sp.wait_ge(*gw_low.at(n, 0))
                for j, w in enumerate((w_rgate, w_igate)):
                    for half in range(2):
                        rows = slice(half * BW, (half + 1) * BW)
                        sp.dma_start(gw_raw[rows, :, j, rows],
                                     w[0, bass.ds(g * (2 * UNITS), 2 * UNITS), :, :].rearrange(
                                         "(u h) c d -> c h u d", h=2)[:, half, :, :]
                                     ).then_inc(*gw_dma.one())
                if nxt_par != par:
                    sp.wait_ge(*q_rot.at(n, 0))
                    load_tables((qp * 2 + 1) * T if par == 0 else 2 * T)
                load_group(n, GA0, g * (2 * P) + COL_GA)
                load_group(n, GA1, g * (2 * P) + (COL_GA + P))
                load_group(n, GL1, g * (2 * P) + (COL_GL + P))
                load_next(n, following)

            iterations(sp, body)
            for s in range(WSLOTS):
                sp.wait_ge(*w_low.at(NITER, s + 1 - WSLOTS))
                sp.dma_start(both.w_raw[:, s, :], w_out[0, s * P:(s + 1) * P, :]).then_inc(w_in_dma[s].sem, 16)

        @block.gpsimd
        def _(pool):
            nc.gpsimd.memset(ones[:, :], 1.0).then_inc(zeroed, 1)
            for s in signals + quarterly + signals_b.all:
                pool.sem_inc(s.sem, s.prime)
            pool.sem_inc(primed, 1)
            for ap in (k_carry, v_carry[:, :, :], x_carry[:, :, :], h_carry[:, :, :], gw_raw[:, :, :, :]):
                nc.gpsimd.memset(ap, 0.0).then_inc(zeroed, 1)

            def quarter_start(qp, par):
                q = qp * 2 + par
                pool.wait_ge(*stat_sum.at(q, 0))
                pool.sem_inc(settled, 1)
                nc.gpsimd.memset(acc[:, par, :, :], 0.0).then_inc(acc_zero, 1)
                pool.wait_ge(acc_zero, q + 1)

            def add_square(n, par, i, y, which, ready):
                pool.wait_ge(*ready)
                pool.wait_ge(*sq_added.at(n, i))
                nc.gpsimd.tensor_tensor(sq[:, :], y, y, ALU.mult).then_inc(*sq_made.one())
                pool.wait_ge(*sq_made.at(n, i + 1))
                nc.gpsimd.tensor_tensor(acc[:, par, which, :], acc[:, par, which, :], sq[:, :], ALU.add
                                        ).then_inc(*sq_added.one())

            def lru_tail(n, u):
                pool.wait_ge(*root.at(n, u + 1))
                pool.wait_ge(*i_x.at(n, u + 1))
                nc.gpsimd.tensor_tensor(ri[u][:, :], ri[u][:, :], hs[u][:, :], ALU.mult
                                        ).then_inc(*scan_in.one())

            def p_current(n, b):
                for k, (src, dst, ready) in enumerate(((p_hi, p_hi_c, p_high), (p_lo, p_lo_c, p_low))):
                    pool.wait_ge(*ready.at(n, b + 1))
                    if k == 0:
                        pool.wait_ge(*pv.at(n, b))
                    pool.sem_inc(settled, 1)
                    nc.gpsimd.affine_select(out=dst[:, :, :], in_=f(src[:, :, :]), compare_op=ALU.is_ge,
                                            fill=0.0, base=0, pattern=[[0, GQ], [1, BLK]],
                                            channel_multiplier=-1).then_inc(*p_cur.one())

            def sine_k(n):
                pool.wait_ge(*k_turn.at(n, 2))
                nc.gpsimd.tensor_tensor(swp[0:HD, :], swp[0:HD, :], sinT[0:HD, :], ALU.mult
                                        ).then_inc(*k_sin.one())

            def sine_q(n, j):
                pool.wait_ge(*q_turn.at(n, 2 * j + 2))
                nc.gpsimd.tensor_tensor(swp[:, :], swp[:, :], sinT[:, :], ALU.mult
                                        ).then_inc(*q_sin.one())

            def split_w(n, i):
                pool.wait_ge(*w_high.at(n, i + 1))
                pool.wait_ge(*w_low.at(n, i))
                nc.gpsimd.tensor_tensor(w_lo[:, i % WSLOTS, :, :], w_raw[:, i % WSLOTS, :, :],
                                        f(w_hi[:, i % WSLOTS, :, :]), ALU.subtract).then_inc(*w_low.one())

            def body(n, g, par, qp, following, nxt_par):
                split_w(n, GA0)
                split_w(n, GA1)
                split_w(n, GL1)
                lru_tail(n, 0)
                lru_tail(n, 1)
                lru_gate(n, par, 0)
                p_current(n, 0)
                p_current(n, 1)
                if nxt_par != par:
                    pool.wait_ge(table_in, (qp * 2 + par + 2) * 32)
                sine_k(n)
                p_current(n, 2)
                lru_gate(n, par, 1)
                sine_q(n, 0)
                p_current(n, 3)
                sine_q(n, 1)
                attention_squares(n, par)

            def attention_squares(n, par):
                pool.wait_ge(*ya_done.at(n, NBLK))
                for j in range(2):
                    add_square(n, par, 2 + j, ya[:, j, :], 0, ya_done.at(n, NBLK))

            def lru_gate(n, par, u):
                pool.wait_ge(*h_kept.at(n, u + 1))
                pool.wait_ge(*ring_dve.at(n, FREED_BY_DVE.index((R_GL0, R_GL1)[u]) + 1))
                nc.gpsimd.tensor_tensor(hs[u][:, :], hs[u][:, :], gl[:, :], ALU.mult
                                        ).then_inc(*yl_done.one())
                add_square(n, par, u, hs[u][:, :], 1, yl_done.at(n, u + 1))

            for i in range(KVG, NG):
                split_w(-1, i)
            pool.wait_ge(table_in, 32)
            sine_k(-1)
            sine_q(-1, 0)
            sine_q(-1, 1)
            iterations(pool, body, quarter_start)

        @block.scalar
        def _(act):
            def split_w(n, i):
                m, i = (n, i) if i < NG else (n + 1, i - NG)
                s = i % WSLOTS
                act.wait_ge(*w_in_dma[s].at(m, W_DMA_AT[i]))
                prev = i - WSLOTS
                act.wait_ge(*ring_ready.at(m, RING_OF_GROUP[prev] + 1 - (NR if prev < 0 else 0)))
                nc.scalar.activation(w_hi[:, s, :, :], w_raw[:, s, :, :], ACT.Copy
                                     ).then_inc(*w_high.one())

            def square_x(n, xin, xsq, free):
                act.wait_ge(*xin)
                act.wait_ge(*free)
                nc.scalar.activation(a2[:, :].bitcast(BF16), xb, ACT.Square, accum_out=xs[:, 0:1]
                                     ).then_inc(*xsq.one())

            def root_x(n, xms, xroot):
                act.wait_ge(*xms)
                nc.scalar.activation(xs[:, 2:3], xs[:, 1:2], ACT.Sqrt).then_inc(*xroot.one())

            def high_x(dst, col, half, ps, ready, done):
                act.wait_ge(*ready)
                act.sem_inc(settled, 1)
                nc.scalar.activation(dst[:, half * 4:half * 4 + 4, bass.ds(col, P)],
                                     ps.rearrange("p (k t) -> p k t", k=4), ACT.Copy).then_inc(*done)

            act.wait_ge(zeroed, 1)
            nc.scalar.activation(xs[:, 2:3], ones[:, :], ACT.Sqrt).then_inc(x_early_root, 1)
            for b in range(NBLK):
                act.wait_ge(pro_x_in[b], 16)
                if b:
                    act.wait_ge(pro_sq, b)
                nc.scalar.activation(a2[:, :].bitcast(BF16), pro_x[b], ACT.Square,
                                     accum_out=pro_stat[:, 0, b:b + 1]).then_inc(pro_sq, 1)
                act.wait_ge(pro_ms, b + 1)
                nc.scalar.activation(pro_stat[:, 2, b:b + 1], pro_stat[:, 1, b:b + 1], ACT.Sqrt
                                     ).then_inc(pro_root, 1)
            act.wait_ge(primed, 1)
            for i in range(2 * NBLK):
                b, half = divmod(i, 2)
                high_x(h_hi[:, 0], b * P, half, pro_bank(i), (pro_T, i + 1), (pro_hi, 1))
                if i in (1, 3, 5):
                    split_w(-1, KVG + i // 2)
            def take_kv(n):
                act.wait_ge(*ring_ready.at(n, R_KV + 1))
                act.wait_ge(*ring_ready.at(n, R_VT + 1 - NR))
                act.wait_ge(*k_rot.at(n, 0))
                nc.scalar.activation(kraw[:, :], bank(R_KV), ACT.Copy).then_inc(*ring_act.one())

            def take_q(n, j):
                act.wait_ge(*ring_ready.at(n, (R_Q0, R_Q1)[j] + 1))
                act.wait_ge(*q_turn.at(n, 2 * j))
                nc.scalar.activation(qraw[:, :], bank((R_Q0, R_Q1)[j]), ACT.Copy).then_inc(*ring_act.one())

            def high_k(n):
                act.wait_ge(*k_rot.at(n, 1))
                act.wait_ge(*scores.at(n, NBLK))
                for half in range(2):
                    nc.scalar.activation(k_hi[half * HD:(half + 1) * HD, :], krot[:, :], ACT.Copy
                                         ).then_inc(*k_high.one())

            def high_q(n, j):
                act.wait_ge(*q_rot.at(n, j + 1))
                act.wait_ge(*scores.at(n, NBLK))
                for half in range(2):
                    rows = slice(half * HD, (half + 1) * HD)
                    nc.scalar.activation(q_st[rows, 2 * j + half, :], qrot[rows, :], ACT.Copy
                                         ).then_inc(*q_high.one())

            def take_v(n):
                act.wait_ge(*ring_ready.at(n, R_VT + 1))
                act.wait_ge(*v_kept.at(n, 0))
                nc.scalar.activation(vraw[:, 1:, :], bank(R_VT).rearrange("p (b c) -> p b c", c=P)[:, :, HD:],
                                     ACT.Copy).then_inc(*ring_act.one())

            def high_v(n):
                act.wait_ge(*v_prev.at(n, 1))
                act.wait_ge(*ring_act.at(n, FREED_BY_ACT.index(R_VT) + 1))
                act.wait_ge(*pv.at(n, NBLK))
                nc.scalar.activation(v_hl[:, :, 0:HD], vraw[:, :, :], ACT.Copy).then_inc(*v_high.one())
                act.wait_ge(*dv_raw.at(n, 1))
                nc.scalar.activation(dv_hl[:, :, 0:HD], dvraw[:, :, :], ACT.Copy).then_inc(*dv_high.one())

            act.wait_ge(consts_in, N_CONST * 16)
            act.wait_ge(prm_step, 1)
            nc.scalar.activation(prm[:, :, C_T1], prm[:, :, C_T0], ACT.Exp).then_inc(prm_act, 1)
            act.wait_ge(prm_step, 2)
            nc.scalar.activation(prm[:, :, C_T2], prm[:, :, C_T0], ACT.Ln).then_inc(prm_act, 1)

            take_kv(-1)
            split_w(-1, NG + XL0)
            take_q(-1, 0)
            high_k(-1)
            split_w(-1, NG + GL0)
            take_q(-1, 1)
            high_q(-1, 0)
            split_w(-1, NG + XL1)
            take_v(-1)
            high_q(-1, 1)
            high_v(-1)

            def body(n, g, par, qp, following, nxt_par):
                def gate_a(j):
                    act.wait_ge(*ring_ready.at(n, (R_GA0, R_GA1)[j] + 1))
                    if j == 0:
                        act.wait_ge(*ya_out.at(n, 0))
                        act.wait_ge(*sq_made.at(n, 0))
                    nc.scalar.activation(ya[:, j, :], bank((R_GA0, R_GA1)[j]), ACT.Tanh, scale=0.5
                                         ).then_inc(*ga_tanh.one())

                def s_copy(b):
                    act.wait_ge(*scores.at(n, b + 1))
                    act.wait_ge(*p_T.at(n, b - 1))
                    nc.scalar.activation(s_sb[:, b % 2], ps_s[:, :, BLK:], ACT.Copy).then_inc(*s_cur.one())

                def s_exp(b):
                    act.wait_ge(*s_stat.at(n, 4 * b + 4))
                    for h in range(GQ):
                        nc.scalar.activation(s_sb[:, b % 2, h, :], s_sb[:, b % 2, h, :], ACT.Exp,
                                             bias=smax[:, b % 2, 2, h:h + 1], scale=HD ** -0.5,
                                             accum_out=sden[:, b % 2, 0, h:h + 1]).then_inc(*p_exp.one())
                    nc.scalar.activation(sden[:, b % 2, 1, :], smax[:, b % 2, 3, :], ACT.Exp
                                         ).then_inc(*p_exp.one())

                def high_p(b):
                    act.wait_ge(*p_T.at(n, b + 1))
                    act.wait_ge(*pv.at(n, b))
                    act.wait_ge(*p_cur.at(n, 2 * b))
                    nc.scalar.activation(p_hi[:, :, :], ps_t[:, :, :], ACT.Copy).then_inc(*p_high.one())

                def low_o(b):
                    act.wait_ge(*pv.at(n, b + 1))
                    act.wait_ge(*o_sum.at(n, 2 * b))
                    nc.scalar.activation(o_low, ps_v[HD:, :, :], ACT.Copy
                                         ).then_inc(*o_lowdone.one())

                def lru_in(u):
                    r = (R_XL0, R_XL1)[u]
                    G = g * UNITS + u
                    act.wait_ge(*ring_ready.at(n, r + 1))
                    act.wait_ge(*xl_kept.at(n, u))
                    act.wait_ge(*i_x.at(n, u + 1 - UNITS))
                    nc.scalar.activation(xl[:, CONV - 1:], bank(r), ACT.Copy).then_inc(*xl_in.one())
                    act.sem_inc(settled, 1)
                    nc.scalar.activation(cu[u][:, :], bank(r), ACT.Identity,
                                         scale=prm[:, G, C_W3:C_W3 + 1], bias=prm[:, G, C_CB:C_CB + 1]
                                         ).then_inc(*ring_act.one())

                def high_u(u):
                    act.wait_ge(*u_conv.at(n, 3 * u + 3))
                    act.wait_ge(*ring_ready.at(n, R_I0 + 1 if u else R_I1 + 1 - NR))
                    nc.scalar.activation(u_hi[:, :], cu[u][:, :], ACT.Copy).then_inc(*u_high.one())

                def gate_l(u):
                    act.wait_ge(*ring_ready.at(n, (R_GL0, R_GL1)[u] + 1))
                    act.wait_ge(*yl_done.at(n, u))
                    nc.scalar.activation(gl[:, :], bank((R_GL0, R_GL1)[u]), ACT.Tanh, scale=0.5
                                         ).then_inc(*gl_tanh.one())

                def decays(u):
                    G = g * UNITS + u
                    act.wait_ge(*ring_ready.at(n, (R_R0, R_R1)[u] + 1))
                    act.wait_ge(*scanned.at(n, u + 1 - UNITS))
                    act.sem_inc(settled, 1)
                    nc.scalar.activation(ra[u][:, :], bank((R_R0, R_R1)[u]), ACT.Tanh, scale=0.5,
                                         bias=prm[:, G, C_BR:C_BR + 1]).then_inc(*ring_act.one())
                    act.wait_ge(*ring_act.at(n, FREED_BY_ACT.index((R_R0, R_R1)[u]) + 1))
                    act.wait_ge(*sq_made.at(n, u + 1 - 4))
                    act.wait_ge(*yl_out[u].at(n, 0))
                    act.sem_inc(settled, 1)
                    nc.scalar.activation(hs[u][:, :], ra[u][:, :], ACT.Tanh, scale=prm[:, G, C_POS4SP:C_POS4SP + 1],
                                         bias=prm[:, G, C_POS4SP:C_POS4SP + 1]).then_inc(*decay.one())
                    nc.scalar.activation(ra[u][:, :], ra[u][:, :], ACT.Exp, scale=prm[:, G, C_NEG4SP:C_NEG4SP + 1],
                                         bias=prm[:, G, C_NEG4SP:C_NEG4SP + 1]).then_inc(*decay.one())
                    act.wait_ge(*decay.at(n, 3 * u + 2))
                    act.wait_ge(*one_minus.at(n, u))
                    act.wait_ge(*x_sq.at(n, 1))
                    nc.scalar.activation(a2[:, :], ra[u][:, :], ACT.Square).then_inc(*decay.one())
                    act.wait_ge(*ring_ready.at(n, (R_I0, R_I1)[u] + 1))
                    act.sem_inc(settled, 1)
                    nc.scalar.activation(ri[u][:, :], bank((R_I0, R_I1)[u]), ACT.Tanh, scale=0.5,
                                         bias=prm[:, G, C_BI:C_BI + 1]).then_inc(*ring_act.one())

                def lru_root(u):
                    act.wait_ge(*one_minus.at(n, u + 1))
                    nc.scalar.activation(hs[u][:, :], hs[u][:, :], ACT.Sqrt).then_inc(*root.one())

                lru_in(0)
                act.wait_ge(*gw_dma.at(n, 4))
                act.wait_ge(*ring_ready.at(n, R_I1 + 1 - NR))
                nc.scalar.activation(gw_hi[:, :, :, :], gw_raw[:, :, :, :], ACT.Copy).then_inc(*gw_high.one())
                split_w(n, GA0)
                high_u(0)
                gate_l(0)
                split_w(n, GA1)
                act.wait_ge(*one_minus.at(n, 0))
                square_x(n, x_in.at(n, 1), x_sq, x_norm.at(n, 0))
                lru_in(1)
                s_copy(0)
                decays(0)
                high_u(1)
                split_w(n, GL1)
                s_exp(0)
                gate_a(0)
                decays(1)
                s_copy(1)
                root_x(n, x_ms.at(n, 1), x_root)
                lru_root(0)
                lru_root(1)
                split_w(n, KVG)
                s_exp(1)
                gate_a(1)
                high_p(0)
                s_copy(2)
                for half in range(2):
                    high_x(h_hi[:, 1 - par], g * P, half, bank(R_XT0 + half),
                           ring_ready.at(n, R_XT0 + half + 1), h_high.one())
                split_w(n, Q0)
                s_exp(2)
                gate_l(1)
                low_o(0)
                high_p(1)
                s_copy(3)
                split_w(n, Q1)
                s_exp(3)
                take_kv(n)
                low_o(1)
                high_p(2)
                split_w(n, NG + XL0)
                take_q(n, 0)
                high_k(n)
                low_o(2)
                high_p(3)
                split_w(n, NG + GL0)
                high_q(n, 0)
                take_q(n, 1)
                low_o(3)
                take_v(n)
                split_w(n, NG + XL1)
                write_out(n, g, par, qp)
                high_q(n, 1)
                high_v(n)

            def write_out(n, g, par, qp):
                q = qp * 2 + par
                act.wait_ge(*ya_done.at(n, NBLK))
                for_dst = y_dram[bass.ds(g * 2, 2), :, bass.ds(q * T, T)].rearrange("e p t -> p e t")
                act.dma_start(for_dst, ya[:, :, :]).then_inc(*ya_out.one())
                for u in range(UNITS):
                    act.wait_ge(*yl_done.at(n, u + 1))
                    act.dma_start(y_dram[bass.ds(g * UNITS + (EC // 2 + u), 1), :, bass.ds(q * T, T)].rearrange(
                        "e p t -> p (e t)"), hs[u][:, :]).then_inc(*yl_out[u].one())

            iterations(act, body)

        @block.vector
        def _(dve):
            stt = nc.vector.scalar_tensor_tensor

            def split_w(n, i):
                m, i = (n, i) if i < NG else (n + 1, i - NG)
                s = i % WSLOTS
                dve.wait_ge(*w_high.at(m, i + 1))
                dve.wait_ge(*w_low.at(m, i))
                nc.vector.tensor_tensor(w_lo[:, s, :, :], w_raw[:, s, :, :], f(w_hi[:, s, :, :]),
                                        ALU.subtract).then_inc(*w_low.one())

            dve.wait_ge(primed, 1)

            def stat_x(sq_in, xms):
                dve.wait_ge(*sq_in)
                nc.vector.tensor_scalar(xs[:, 1:2], xs[:, 0:1], 1.0 / D, EPS, ALU.mult, ALU.add
                                        ).then_inc(*xms.one())

            def norm_x(n, root_in, xrs, xnorm):
                dve.wait_ge(*root_in)
                nc.vector.reciprocal(xs[:, 3:4], xs[:, 2:3]).then_inc(*xrs.one())
                dve.wait_ge(*xrs.at(n, 1))
                stt(out=xb, in0=xb, scalar=xs[:, 3:4], in1=gain_row, op0=ALU.mult,
                    op1=ALU.mult).then_inc(*xnorm.one())

            def low_x(dst, hi, col, half, ps, ready, done):
                dve.wait_ge(*ready)
                at = (slice(None), slice(half * 4, half * 4 + 4), bass.ds(col, P))
                nc.vector.tensor_tensor(dst[at], ps.rearrange("p (k t) -> p k t", k=4), f(hi[at]),
                                        ALU.subtract).then_inc(*done)

            dve.wait_ge(early_in, 32)

            def low_first(i):
                b, half = divmod(i, 2)
                low_x(h_lo[:, 0], h_hi[:, 0], b * P, half, pro_bank(i), (pro_hi, i + 1), (pro_lo, 1))

            for b in range(NBLK):
                dve.wait_ge(pro_sq, b + 1)
                nc.vector.tensor_scalar(pro_stat[:, 1, b:b + 1], pro_stat[:, 0, b:b + 1], 1.0 / D, EPS,
                                        ALU.mult, ALU.add).then_inc(pro_ms, 1)
                dve.wait_ge(pro_root, b + 1)
                nc.vector.reciprocal(pro_stat[:, 3, b:b + 1], pro_stat[:, 2, b:b + 1]).then_inc(pro_rs, 1)
                dve.wait_ge(pro_rs, b + 1)
                stt(out=pro_x[b], in0=pro_x[b], scalar=pro_stat[:, 3, b:b + 1], in1=gain_row,
                    op0=ALU.mult, op1=ALU.mult).then_inc(pro_norm, 1)
            for i in range(2 * NBLK):
                low_first(i)

            def turn_k(n, g):
                dve.wait_ge(*k_high.at(n, 0))
                dve.wait_ge(*k_low.at(n, 0))
                nc.vector.tensor_scalar(krot[:, 0:BLK], k_carry[:, g, :], 1.0, None, ALU.mult
                                        ).then_inc(*k_turn.one())
                dve.wait_ge(*ring_act.at(n, FREED_BY_ACT.index(R_KV) + 1))
                dve.wait_ge(*q_rot.at(n, 0))
                dve.sem_inc(settled, 1)
                nc.vector.stream_shuffle(swp[0:HD, :], kraw[0:HD, :], SWAP).then_inc(*k_turn.one())
                nc.vector.tensor_tensor(krot[:, BLK:], kraw[0:HD, :], cosT[0:HD, :], ALU.mult
                                        ).then_inc(*k_turn.one())

            def add_k(n):
                dve.wait_ge(*k_turn.at(n, 3))
                dve.wait_ge(*k_sin.at(n, 1))
                nc.vector.tensor_tensor(krot[:, BLK:], krot[:, BLK:], swp[0:HD, :], ALU.add
                                        ).then_inc(*k_rot.one())

            def low_k(n, g):
                dve.wait_ge(*k_high.at(n, 2))
                nc.vector.tensor_tensor(k_lo[0:HD, :], krot[:, :], f(k_hi[0:HD, :]), ALU.subtract
                                        ).then_inc(*k_low.one())
                dve.wait_ge(*k_low.at(n, 1))
                nc.vector.tensor_copy(k_lo[HD:, :], k_lo[0:HD, :]).then_inc(*k_low.one())
                nc.vector.tensor_scalar(k_carry[:, g, :], krot[:, T:], 1.0, None, ALU.mult
                                        ).then_inc(*k_low.one())

            def turn_q(n, j):
                dve.wait_ge(*ring_act.at(n, FREED_BY_ACT.index((R_Q0, R_Q1)[j]) + 1))
                dve.wait_ge(*q_low.at(n, 2 * j))
                dve.wait_ge(*q_high.at(n, 2 * j))
                dve.wait_ge(*(q_rot.at(n, j) if j else k_rot.at(n, 1)))
                nc.vector.tensor_tensor(qrot[:, :], qraw[:, :], cosT[:, :], ALU.mult
                                        ).then_inc(*q_turn.one())
                nc.vector.stream_shuffle(swp[:, :], qraw[:, :], SWAP).then_inc(*q_turn.one())

            def add_q(n, j):
                dve.wait_ge(*q_turn.at(n, 2 * j + 1))
                dve.wait_ge(*q_sin.at(n, j + 1))
                nc.vector.tensor_tensor(qrot[:, :], qrot[:, :], swp[:, :], ALU.add
                                        ).then_inc(*q_rot.one())

            def low_q(n, j):
                for half in range(2):
                    rows = slice(half * HD, (half + 1) * HD)
                    other = slice((1 - half) * HD, (2 - half) * HD)
                    dve.wait_ge(*q_high.at(n, 2 * j + half + 1))
                    nc.vector.tensor_tensor(q_st[other, 2 * j + half, :], qrot[rows, :],
                                            f(q_st[rows, 2 * j + half, :]), ALU.subtract
                                            ).then_inc(*q_low.one())

            def previous_v(n, g):
                dve.wait_ge(*v_high.at(n, 0))
                dve.wait_ge(*v_kept.at(n, 0))
                nc.vector.tensor_scalar(vraw[:, 0, :], v_carry[:, g, :], 1.0, None, ALU.mult
                                        ).then_inc(*v_prev.one())

            def differ_v(n):
                dve.wait_ge(*v_prev.at(n, 1))
                dve.wait_ge(*ring_act.at(n, FREED_BY_ACT.index(R_VT) + 1))
                dve.wait_ge(*dv_low.at(n, 0))
                nc.vector.tensor_tensor(dvraw[:, :, :], vraw[:, 1:, :], vraw[:, :NBLK, :], ALU.subtract
                                        ).then_inc(*dv_raw.one())

            def low_v(n, g):
                dve.wait_ge(*v_high.at(n, 1))
                nc.vector.tensor_tensor(v_hl[:, :, HD:], vraw[:, :, :], f(v_hl[:, :, 0:HD]), ALU.subtract
                                        ).then_inc(*v_low.one())
                nc.vector.tensor_scalar(v_carry[:, g, :], vraw[:, NBLK, :], 1.0, None, ALU.mult
                                        ).then_inc(*v_kept.one())
                dve.wait_ge(*dv_high.at(n, 1))
                nc.vector.tensor_tensor(dv_hl[:, :, HD:], dvraw[:, :, :], f(dv_hl[:, :, 0:HD]),
                                        ALU.subtract).then_inc(*dv_low.one())

            dve.wait_ge(consts_in, N_CONST * 16)
            col = lambda c: prm[:, :, c]
            step = [0]

            def done(ins):
                step[0] += 1
                ins.then_inc(prm_step, 1)
                dve.wait_ge(prm_step, step[0])

            nc.vector.tensor_scalar(prev_mask[:, :, :], cap[:, 0, :].unsqueeze(1).broadcast_to([P, GQ, BLK]),
                                    0.0, None, ALU.is_lt).then_inc(masks, 1)
            nc.vector.tensor_scalar(col(C_T1), col(C_LAM), -1.0, None, ALU.mult).then_inc(masks, 1)
            dve.wait_ge(masks, 2)
            done(nc.vector.tensor_tensor(col(C_T0), col(C_LAM), col(C_T1), ALU.min))
            dve.wait_ge(prm_act, 1)
            done(nc.vector.tensor_scalar(col(C_T0), col(C_T1), 1.0, None, ALU.add))
            dve.wait_ge(prm_act, 2)
            done(nc.vector.tensor_scalar(col(C_POS4SP), col(C_T0), 1.0, None, ALU.is_equal))
            done(nc.vector.tensor_scalar(col(C_T0), col(C_T0), -1.0, None, ALU.add))
            done(nc.vector.tensor_tensor(col(C_T0), col(C_T0), col(C_POS4SP), ALU.add))
            done(nc.vector.reciprocal(col(C_NEG4SP), col(C_T0)))
            done(nc.vector.tensor_tensor(col(C_T2), col(C_T2), col(C_NEG4SP), ALU.mult))
            done(nc.vector.tensor_tensor(col(C_T2), col(C_T2), col(C_POS4SP), ALU.add))
            done(nc.vector.tensor_tensor(col(C_T2), col(C_T2), col(C_T1), ALU.mult))
            done(nc.vector.tensor_scalar(col(C_T0), col(C_LAM), -1.0, 0.0, ALU.mult, ALU.max))
            done(nc.vector.tensor_tensor(col(C_T2), col(C_T2), col(C_T0), ALU.add))
            done(nc.vector.tensor_scalar(col(C_POS4SP), col(C_T2), 4.0, None, ALU.mult))
            done(nc.vector.tensor_scalar(col(C_NEG4SP), col(C_T2), -4.0, None, ALU.mult))
            done(nc.vector.tensor_scalar(col(C_BR), col(C_BR), 0.5, None, ALU.mult))
            done(nc.vector.tensor_scalar(col(C_BI), col(C_BI), 0.5, None, ALU.mult))

            dve.wait_ge(table_in, 32)
            dve.wait_ge(zeroed, 6)
            turn_k(-1, 0)
            dve.wait_ge(*w_low.at(-1, NG))
            split_w(-1, NG + XL0)
            add_k(-1)
            low_k(-1, 0)
            turn_q(-1, 0)
            split_w(-1, NG + GL0)
            add_q(-1, 0)
            low_q(-1, 0)
            turn_q(-1, 1)
            previous_v(-1, 0)
            split_w(-1, NG + XL1)
            add_q(-1, 1)
            low_q(-1, 1)
            differ_v(-1)
            low_v(-1, 0)

            def body(n, g, par, qp, following, nxt_par):
                def silu_a(j):
                    dve.wait_ge(*ga_tanh.at(n, j + 1))
                    stt(out=ya[:, j, :], in0=ya[:, j, :], scalar=1.0, in1=bank((R_GA0, R_GA1)[j]),
                        op0=ALU.add, op1=ALU.mult).then_inc(*ring_dve.one())

                def softmax_a(b):
                    s, t = s_sb[:, b % 2], smax[:, b % 2]
                    dve.wait_ge(*s_cur.at(n, b + 1))
                    dve.sem_inc(settled, 1)
                    nc.vector.copy_predicated(s, prev_mask[:, :, :], ps_s[:, :, 0:BLK]
                                              ).then_inc(*s_sel.one())
                    dve.wait_ge(*s_sel.at(n, b + 1))
                    if b == 0:
                        if par == 0:
                            nc.vector.tensor_tensor(s, s, cap[:, qp, :].unsqueeze(1).broadcast_to([P, GQ, BLK]), ALU.min).then_inc(*s_cap.one())
                        else:
                            dve.sem_inc(s_cap.sem, 1)
                        dve.wait_ge(*s_cap.at(n, 1))
                    nc.vector.tensor_reduce(out=t[:, 0, :], in_=s, op=ALU.max, axis=AXX
                                            ).then_inc(*s_stat.one())
                    dve.wait_ge(*s_stat.at(n, 4 * b + 1))
                    sink = sink_all[:, bass.ds(g * GQ, GQ)]
                    stt(out=t[:, 1, :], in0=t[:, 0, :], scalar=HD ** -0.5, in1=sink, op0=ALU.mult,
                        op1=ALU.max).then_inc(*s_stat.one())
                    dve.wait_ge(*s_stat.at(n, 4 * b + 2))
                    nc.vector.tensor_scalar(t[:, 2, :], t[:, 1, :], -1.0, None, ALU.mult
                                            ).then_inc(*s_stat.one())
                    nc.vector.tensor_tensor(t[:, 3, :], sink, t[:, 1, :], ALU.subtract
                                            ).then_inc(*s_stat.one())

                def softmax_b(b):
                    d = sden[:, b % 2]
                    dve.wait_ge(*p_exp.at(n, (GQ + 1) * (b + 1)))
                    nc.vector.tensor_tensor(d[:, 2, :], d[:, 0, :], d[:, 1, :], ALU.add
                                            ).then_inc(*p_den.one())
                    dve.wait_ge(*p_den.at(n, 2 * b + 1))
                    nc.vector.reciprocal(d[:, 3, :], d[:, 2, :]).then_inc(*p_den.one())
                    dve.wait_ge(*p_den.at(n, 2 * b + 2))
                    nc.vector.tensor_tensor(s_sb[:, b % 2], s_sb[:, b % 2],
                                            d[:, 3, :].unsqueeze(2).broadcast_to([P, GQ, BLK]), ALU.mult
                                            ).then_inc(*p_norm.one())

                def low_p(b):
                    dve.wait_ge(*p_high.at(n, b + 1))
                    nc.vector.tensor_tensor(p_lo[:, :, :], ps_t[:, :, :], f(p_hi[:, :, :]), ALU.subtract
                                            ).then_inc(*p_low.one())

                def gather_o(b):
                    dve.wait_ge(*o_lowdone.at(n, b + 1))
                    dve.wait_ge(*ya_done.at(n, b))
                    pair = lambda ap, s: ap.rearrange("p (j s) t -> p s j t", s=2)[:, s]
                    for s in range(2):
                        nc.vector.tensor_tensor(o_sb[s * HD:(s + 1) * HD, :, :], pair(ps_v[0:HD], s),
                                                pair(o_low, s), ALU.add).then_inc(*o_sum.one())
                    dve.wait_ge(*o_sum.at(n, 2 * b + 2))
                    if b == 0:
                        dve.wait_ge(*ring_dve.at(n, FREED_BY_DVE.index(R_GA1) + 1))
                    y = ya[:, :, b * BLK:(b + 1) * BLK]
                    nc.vector.tensor_tensor(y, y, o_sb[:, :, :], ALU.mult).then_inc(*ya_done.one())

                def conv(u):
                    G = g * UNITS + u
                    dve.wait_ge(*u_conv.at(n, 3 * u))
                    dve.wait_ge(*xl_kept.at(n, u))
                    nc.vector.tensor_scalar(xl[:, 0:CONV - 1], x_carry[:, G, :], 1.0, None, ALU.mult
                                            ).then_inc(*xl_prev.one())
                    dve.wait_ge(*xl_prev.at(n, u + 1))
                    dve.wait_ge(*ring_act.at(n, FREED_BY_ACT.index((R_XL0, R_XL1)[u]) + 1))
                    for i in range(3):
                        tap = 2 - i
                        if i:
                            dve.wait_ge(*u_conv.at(n, 3 * u + i))
                        stt(out=cu[u][:, :], in0=xl[:, tap:tap + T],
                            scalar=prm[:, G, C_W0 + tap:C_W0 + tap + 1], in1=cu[u][:, :], op0=ALU.mult,
                            op1=ALU.add).then_inc(*u_conv.one())
                    nc.vector.tensor_scalar(x_carry[:, G, :], xl[:, T:], 1.0, None, ALU.mult
                                            ).then_inc(*xl_kept.one())

                def low_u(u):
                    dve.wait_ge(*u_high.at(n, u + 1))
                    nc.vector.tensor_tensor(u_lo[:, :], cu[u][:, :], f(u_hi[:, :]), ALU.subtract
                                            ).then_inc(*u_low.one())

                def silu_l(u):
                    dve.wait_ge(*gl_tanh.at(n, u + 1))
                    stt(out=gl[:, :], in0=gl[:, :], scalar=1.0, in1=bank((R_GL0, R_GL1)[u]),
                        op0=ALU.add, op1=ALU.mult).then_inc(*ring_dve.one())

                def lru_mid(u):
                    dve.wait_ge(*decay.at(n, 3 * u + 3))
                    stt(out=hs[u][:, :], in0=a2[:, :], scalar=1.0, in1=hs[u][:, :], op0=ALU.add,
                        op1=ALU.mult).then_inc(*one_minus.one())
                    dve.wait_ge(*ring_act.at(n, FREED_BY_ACT.index((R_I0, R_I1)[u]) + 1))
                    stt(out=ri[u][:, :], in0=ri[u][:, :], scalar=1.0, in1=cu[u][:, :], op0=ALU.add,
                        op1=ALU.mult).then_inc(*i_x.one())

                def lru_scan(u):
                    G = g * UNITS + u
                    dve.wait_ge(*scan_in.at(n, u + 1))
                    dve.wait_ge(*h_kept.at(n, u))
                    dve.wait_ge(*one_minus.at(n, u + 1))
                    nc.vector.tensor_tensor_scan(hs[u][:, :], ra[u][:, :], ri[u][:, :], h_carry[:, G, :],
                                                 ALU.mult, ALU.add).then_inc(*scanned.one())
                    dve.wait_ge(*scanned.at(n, u + 1))
                    nc.vector.tensor_scalar(h_carry[:, G, :], hs[u][:, T - 1:], 1.0, None, ALU.mult
                                            ).then_inc(*h_kept.one())

                conv(0)
                dve.wait_ge(*gw_high.at(n, 1))
                nc.vector.tensor_tensor(gw_lo[:, :, :, :], gw_raw[:, :, :, :], f(gw_hi[:, :, :, :]),
                                        ALU.subtract).then_inc(*gw_low.one())
                silu_l(0)
                low_u(0)
                stat_x(x_sq.at(n, 1), x_ms)
                conv(1)
                softmax_a(0)
                if nxt_par != par:
                    q = qp * 2 + par
                    dve.wait_ge(*stat_sum.at(q, 1))
                    dve.sem_inc(settled, 1)
                    nc.vector.tensor_scalar(sums[:, :, bass.ds(q * NBLK, NBLK)],
                                            ps_t[:, 0, 0:2 * NBLK].rearrange("p (w b) -> p w b", w=2), 1.0, None,
                                            ALU.mult).then_inc(*stat_kept.one())
                low_u(1)
                lru_mid(0)
                softmax_b(0)
                silu_a(0)
                lru_mid(1)
                softmax_a(1)
                norm_x(n, x_root.at(n, 1), x_rs, x_norm)
                lru_scan(0)
                split_w(n, KVG)
                lru_scan(1)
                softmax_b(1)
                silu_a(1)
                low_p(0)
                softmax_a(2)
                for half in range(2):
                    low_x(h_lo[:, 1 - par], h_hi[:, 1 - par], g * P, half, bank(R_XT0 + half),
                          h_high.at(n, half + 1), ring_dve.one())
                split_w(n, Q0)
                softmax_b(2)
                gather_o(0)
                low_p(1)
                softmax_a(3)
                split_w(n, Q1)
                silu_l(1)
                softmax_b(3)
                if nxt_par != par:
                    dve.wait_ge(table_in, (qp * 2 + par + 2) * 32)
                turn_k(n, following)
                low_p(2)
                gather_o(1)
                add_k(n)
                split_w(n, NG + XL0)
                turn_q(n, 0)
                low_p(3)
                gather_o(2)
                low_k(n, following)
                add_q(n, 0)
                split_w(n, NG + GL0)
                low_q(n, 0)
                turn_q(n, 1)
                previous_v(n, following)
                gather_o(3)
                differ_v(n)
                add_q(n, 1)
                split_w(n, NG + XL1)
                low_q(n, 1)
                low_v(n, following)

            iterations(dve, body)

        @block.tensor
        def _(pe):
            mm = nc.tensor.matmul
            passes = ((w_hi, h_hi), (w_hi, h_lo), (w_lo, h_hi))
            pe.wait_ge(early_in, 32)
            for i in range(2 * NBLK):
                b, half = divmod(i, 2)
                pe.wait_ge(pro_norm, b + 1)
                for k in range(4):
                    c = half * 4 + k
                    last = nc.tensor.transpose(pro_bank(i)[:, k * P:(k + 1) * P],
                                               pro_x[b][:, c * P:(c + 1) * P], ident[:, :])
                last.then_inc(pro_T, 1)
            pe.wait_ge(pro_lo, 2 * NBLK)

            def project(n, i, par):
                r = RING_OF_GROUP[i]
                pe.wait_ge(*w_low.at(n, i + 1))
                pe.wait_ge(*bank_free(n, r))
                for k in range(KC):
                    for j, (w, h) in enumerate(passes):
                        last = mm(bank(r), w[:, i % WSLOTS, k, :], h[:, par, k, :],
                                  start=(k == 0 and j == 0), stop=(k == KC - 1 and j == 2))
                last.then_inc(*ring_ready.one())

            def turn_v(n):
                pe.wait_ge(*ring_act.at(n, FREED_BY_ACT.index(R_KV) + 1))
                pe.wait_ge(*bank_free(n, R_VT))
                for b in range(NBLK):
                    last = nc.tensor.transpose(bank(R_VT)[:, b * P:(b + 1) * P],
                                               kraw[:, b * P:(b + 1) * P], ident[:, :])
                last.then_inc(*ring_ready.one())

            for i in range(KVG, NG):
                project(-1, i, 0)
            turn_v(-1)

            def body(n, g, par, qp, following, nxt_par):
                def score(b):
                    if b == 0:
                        pe.wait_ge(*q_low.at(n, 0))
                        pe.wait_ge(*k_low.at(n, 0))
                    pe.wait_ge(*s_sel.at(n, b))
                    for h in range(GQ):
                        for k, st, sp_ in ((k_hi, True, False), (k_lo, False, True)):
                            last = mm(ps_s[:, h, :], q_st[:, h, b * BLK:(b + 1) * BLK],
                                      k[:, b * BLK:(b + 2) * BLK], start=st, stop=sp_)
                    last.then_inc(*scores.one())

                def sum_squares():
                    pe.wait_ge(*sq_added.at(n, 0))
                    pe.wait_ge(*p_low.at(n, 0))
                    for which in range(2):
                        for b in range(NBLK):
                            i = which * NBLK + b
                            last = mm(ps_t[:, 0, i:i + 1], acc[:, 1 - par, which, b * BLK:(b + 1) * BLK],
                                      ones[:, :], start=True, stop=True)
                    last.then_inc(*stat_sum.one())

                def turn_p(b):
                    pe.wait_ge(*p_norm.at(n, b + 1))
                    if b == 0 and nxt_par != par:
                        pe.wait_ge(*stat_kept.at(qp * 2 + par, 1))
                    pe.wait_ge(*p_low.at(n, b))
                    for h in range(GQ):
                        last = nc.tensor.transpose(ps_t[:, h, :], s_sb[:, b % 2, h, :], ident[:, :])
                    last.then_inc(*p_T.one())

                def weigh_v(b):
                    if b == 0:
                        pe.wait_ge(*v_low.at(n, 0))
                        pe.wait_ge(*dv_low.at(n, 0))
                    pe.wait_ge(*p_low.at(n, b + 1))
                    pe.wait_ge(*o_sum.at(n, 2 * b))
                    terms = ((v_hl, p_hi), (v_hl, p_lo), (dv_hl, p_hi_c), (dv_hl, p_lo_c))
                    for i, (v, p) in enumerate(terms):
                        if i >= 2:
                            pe.wait_ge(*p_cur.at(n, 2 * b + i - 1))
                        last = mm(ps_v[:, :, :], v[:, b, :], p[:, :, :], start=(i == 0), stop=(i == 3))
                    last.then_inc(*pv.one())

                def gates(u):
                    pe.wait_ge(*u_low.at(n, u + 1))
                    if u == 0:
                        pe.wait_ge(*gw_low.at(n, 1))
                    for j in range(2):
                        r = ((R_R0, R_I0), (R_R1, R_I1))[u][j]
                        pe.wait_ge(*bank_free(n, r))
                        for i, (w, v) in enumerate(((gw_hi, u_hi), (gw_hi, u_lo), (gw_lo, u_hi))):
                            last = mm(bank(r), w[:, u, j, :], v[:, :], start=(i == 0), stop=(i == 2))
                        last.then_inc(*ring_ready.one())

                def turn_x():
                    pe.wait_ge(*x_norm.at(n, 1))
                    for half in range(2):
                        pe.wait_ge(*bank_free(n, R_XT0 + half))
                        for k in range(4):
                            c = half * 4 + k
                            last = nc.tensor.transpose(bank(R_XT0 + half)[:, k * P:(k + 1) * P],
                                                       xb[:, c * P:(c + 1) * P], ident[:, :])
                        last.then_inc(*ring_ready.one())

                project(n, XL0, par)
                project(n, GL0, par)
                project(n, XL1, par)
                score(0)
                if nxt_par != par:
                    sum_squares()
                gates(0)
                project(n, GA0, par)
                gates(1)
                score(1)
                project(n, GA1, par)
                turn_p(0)
                score(2)
                turn_x()
                project(n, GL1, par)
                weigh_v(0)
                turn_p(1)
                score(3)
                if nxt_par != par:
                    pe.wait_ge(*ring_dve.at(n, FREED_BY_DVE.index(R_XT1) + 1))
                project(n, KVG, nxt_par)
                weigh_v(1)
                turn_p(2)
                project(n, Q0, nxt_par)
                weigh_v(2)
                turn_p(3)
                project(n, Q1, nxt_par)
                weigh_v(3)
                turn_v(n)

            iterations(pe, body)

        for sig in signals:
            if sig is not s_cap:
                sig.checked(4, WSLOTS if sig in (w_high, w_low) else 0)
        for sig in quarterly:
            sig.checked(2)
        done = Record()
        done.w_in_dma = w_in_dma
        done.w_low = w_low
        done.ring_ready = ring_ready
        done.ring_act = ring_act
        done.ring_dve = ring_dve
        done.x_norm = x_norm
        done.v_kept = v_kept
        done.dv_low = dv_low
        done.dv_high = dv_high
        done.sq_added = sq_added
        done.s_sel = s_sel
        done.p_low = p_low
        done.o_sum = o_sum
        done.stat_sum = stat_sum
        done.ya_out = ya_out
        done.yl_out = yl_out
        done.zeroed = zeroed
        return done


def signals_of_phase_b(nc, top):
    b = Record()
    b.all = []

    def signal(name, per, unit=1):
        s = Signal(top, nc, name, per, unit)
        b.all.append(s)
        return s

    b.wo_in = [signal(f"wo_in{s}", 1, 16) for s in range(WSLOTS)]
    b.wo_high = signal("wo_high", 1)
    b.wo_low = signal("wo_low", 1)
    b.y_in = signal("y_in", 2, 16)
    b.y_high = signal("y_high", 2)
    b.y_low = signal("y_low", 2)
    b.x_in = [signal(f"x_in_b{s}", 1, 16) for s in range(2)]
    b.product = [signal(f"product{s}", 2) for s in range(2)]
    b.added = signal("added", 4)
    b.sq_done = signal("sq_done", 2)
    b.mean = signal("mean", 2)
    b.rooted = signal("rooted", 2)
    b.recip = signal("recip", 2)
    b.normed = signal("normed", 2)
    b.res_free = [signal(f"res_free{s}", 1) for s in range(2)]
    b.stored = [Signal(top, nc, f"stored{s}", 1, 16, lead=0) for s in range(2)]
    sem = lambda name: top.enter_context(nc.semaphore(name))
    b.over, b.fgain_in, b.stat_done = sem("phase_a_over"), sem("fgain_in"), sem("stat_done")
    b.rms_step, b.rms_root, b.settled = sem("rms_step"), sem("rms_root"), sem("settled_b")
    return b


def phase_b(nc, block, both, b, a, x, w_out, final_gain, y_dram, out):
    ones, wo_raw, egain, acc_sq, sums = both.ones, both.w_raw, both.egain, both.acc, both.sums
    with ExitStack() as ctx:
        def sb(name, shape, dt=F32):
            return ctx.enter_context(nc.sbuf_tensor(name, shape, dt))

        f = lambda ap: ap.bitcast(F32)
        wo_rest = sb("wo_rest", [P, EC // 2, 2, D], F32R)
        y_odd = sb("y_odd", [P, 2, EC, P], F32R)
        res = sb("res", [P, 2, D])
        rms = sb("rms", [P, 2, NTOK])
        stat = sb("stat", [P, 2, 4])
        acc = ctx.enter_context(nc.psum_tensor("acc_b", [P, 2, 2, 2, D // 2], F32))
        stat_ps = acc[:, 1, 0, 0, 0:2 * NBLK]
        blocks = lambda ap: ap.rearrange("p s d -> p (s d)").rearrange("p (e t) -> p e t", e=EC)
        y_raw = blocks(both.rows[:, :, :])
        y_hi = [blocks(both.w_hi[:, 0:2, :]), y_odd[:, 0, :, :]]
        y_lo = [blocks(both.w_lo[:, 0:2, :]), y_odd[:, 1, :, :]]
        junk = both.w_hi[:, 2, :]
        fgain = both.acc[:, 0, :, :].rearrange("p w t -> p (w t)")

        early = both.split[:, :, :, :].rearrange("p q w (c d) -> p q w c d", c=4)

        def wo(e, low):
            return wo_rest[:, e - EC // 2, low, :] if e >= EC // 2 else early[:, 1 - e // 4, low, e % 4, :]

        STEPS = NTOK // 2
        at_step = lambda m, s: bass.ds(m * (2 * P) + s * P, P)

        @block.sync
        def _(sp):
            def load_y(m, s):
                sp.wait_ge(*b.y_low.at(m, s))
                sp.dma_start(y_raw[:, :, :], y_dram[:, :, at_step(m, s)].rearrange("e p t -> p e t")
                             ).then_inc(*b.y_in.one())

            def load_x(m, s):
                sp.wait_ge(*b.res_free[s].at(m, 0))
                sp.dma_start(res[:, s, :], x[0, at_step(m, s), :]).then_inc(*b.x_in[s].one())

            def load_w(e):
                sp.wait_ge(*b.wo_low.at(e - WSLOTS, 1))
                sp.dma_start(wo_raw[:, e % WSLOTS, :], w_out[0, e * P:(e + 1) * P, :]
                             ).then_inc(*b.wo_in[e % WSLOTS].one())

            sp.wait_ge(*a.ring_ready.at(NITER - 1, R_XT1 + 1))
            sp.wait_ge(*a.ya_out.at(KV, 0))
            for u in range(UNITS):
                sp.wait_ge(*a.yl_out[u].at(KV, 0))
            load_y(0, 0)
            for e in range(WSLOTS, 2 * WSLOTS):
                load_w(e)
            load_y(0, 1)
            for e in range(2 * WSLOTS, EC):
                load_w(e)
            sp.wait_ge(b.over, 1)
            for s in range(2):
                load_x(0, s)
            sp.wait_ge(*a.stat_sum.at(NQUART - 1, 1))
            sp.dma_start(fgain, final_gain.rearrange("(o d) -> o d", o=1).broadcast_to([P, D])
                         ).then_inc(b.fgain_in, 16)
            with sp.Fori(1, STEPS) as m:
                for s in range(2):
                    load_y(m, s)
                    load_x(m, s)
            sp.wait_ge(*b.y_low.at(STEPS, 0))
            sp.sem_inc(b.y_in.sem, 16)

        @block.gpsimd
        def _(pool):
            with pool.Fori(0, STEPS) as m:
                for s in range(2):
                    pool.wait_ge(*b.normed.at(m, s + 1))
                    pool.sem_inc(b.settled, 1)
                    pool.dma_start(out[0, at_step(m, s), :], res[:, s, :]).then_inc(*b.stored[s].one())
                    pool.wait_ge(*b.stored[s].at(m, 1))
                    pool.sem_inc(b.res_free[s].sem, 1)

        @block.scalar
        def _(act):
            def high_y(m, s):
                act.wait_ge(*b.y_in.at(m, s + 1))
                act.wait_ge(*b.product[s].at(m, 0))
                nc.scalar.activation(y_hi[s], y_raw, ACT.Copy).then_inc(*b.y_high.one())

            def high_w(e):
                s = e % WSLOTS
                if e < WSLOTS:
                    act.wait_ge(*a.w_in_dma[s].at(NITER, 1))
                else:
                    act.wait_ge(*b.wo_in[s].at(e // WSLOTS, 0))
                nc.scalar.activation(wo(e, 0), wo_raw[:, s, :], ACT.Copy, scale=egain[:, e:e + 1]
                                     ).then_inc(*b.wo_high.one())

            def mean_square(m, s):
                act.wait_ge(*b.added.at(m, 2 * s + 2))
                nc.scalar.activation(junk, res[:, s, :], ACT.Square, accum_out=stat[:, s, 0:1]
                                     ).then_inc(*b.sq_done.one())
                act.wait_ge(*b.mean.at(m, s + 1))
                nc.scalar.activation(stat[:, s, 2:3], stat[:, s, 1:2], ACT.Sqrt).then_inc(*b.rooted.one())

            act.wait_ge(*a.w_low.at(NITER, WSLOTS))
            act.wait_ge(*a.ring_ready.at(NITER, 0))
            high_y(0, 0)
            for e in range(WSLOTS):
                high_w(e)
            act.wait_ge(*a.dv_low.at(NITER, 0))
            act.wait_ge(*a.sq_added.at(NITER, 0))
            act.wait_ge(*a.ya_out.at(NITER, 0))
            for u in range(UNITS):
                act.wait_ge(*a.yl_out[u].at(NITER, 0))
            act.sem_inc(b.over, 1)
            for e in range(WSLOTS, 2 * WSLOTS):
                high_w(e)
            high_y(0, 1)
            for e in range(2 * WSLOTS, EC):
                high_w(e)
            act.wait_ge(b.rms_step, 3)
            nc.scalar.activation(rms[:, :, :], rms[:, :, :], ACT.Sqrt).then_inc(b.rms_root, 1)
            high_y(1, 0)
            mean_square(0, 0)
            mean_square(0, 1)
            with act.Fori(1, STEPS) as m:
                for s in range(2):
                    high_y(m + s, 1 - s)
                    mean_square(m, s)

        @block.vector
        def _(dve):
            stt = nc.vector.scalar_tensor_tensor

            def low_y(m, s):
                dve.wait_ge(*b.y_high.at(m, s + 1))
                nc.vector.tensor_tensor(y_lo[s], y_raw, f(y_hi[s]), ALU.subtract
                                        ).then_inc(*b.y_low.one())

            def low_w(e):
                dve.wait_ge(*b.wo_high.at(e, 1))
                stt(out=wo(e, 1), in0=wo_raw[:, e % WSLOTS, :], scalar=egain[:, e:e + 1],
                    in1=f(wo(e, 0)), op0=ALU.mult, op1=ALU.subtract).then_inc(*b.wo_low.one())

            def finish(m, s):
                dve.wait_ge(*b.x_in[s].at(m, 1))
                r = res[:, s, :].rearrange("p (h c) -> p h c", h=2)
                for g in range(2):
                    dve.wait_ge(*b.product[s].at(m, g + 1))
                    if g:
                        dve.wait_ge(*b.added.at(m, 2 * s + 1))
                    stt(out=r, in0=acc[:, s, g, :, :], scalar=rms[:, g, bass.ds(m * 2 + s, 1)], in1=r,
                        op0=ALU.mult, op1=ALU.add).then_inc(*b.added.one())
                dve.wait_ge(*b.sq_done.at(m, s + 1))
                nc.vector.tensor_scalar(stat[:, s, 1:2], stat[:, s, 0:1], 1.0 / D, EPS, ALU.mult, ALU.add
                                        ).then_inc(*b.mean.one())
                dve.wait_ge(*b.rooted.at(m, s + 1))
                nc.vector.reciprocal(stat[:, s, 3:4], stat[:, s, 2:3]).then_inc(*b.recip.one())
                dve.wait_ge(*b.recip.at(m, s + 1))
                stt(out=res[:, s, :], in0=res[:, s, :], scalar=stat[:, s, 3:4], in1=fgain,
                    op0=ALU.mult, op1=ALU.mult).then_inc(*b.normed.one())

            low_y(0, 0)
            for e in range(WSLOTS):
                low_w(e)
            dve.wait_ge(b.stat_done, 1)
            nc.vector.tensor_scalar(sums[:, :, NTOK:], stat_ps.rearrange("p (g t) -> p g t", g=2), 1.0, None,
                                    ALU.mult).then_inc(b.rms_step, 1)
            for e in range(WSLOTS, 2 * WSLOTS):
                low_w(e)
            low_y(0, 1)
            for e in range(2 * WSLOTS, EC):
                low_w(e)
            dve.wait_ge(b.rms_step, 1)
            for g, k in ((0, 4.0), (1, 16.0)):
                nc.vector.tensor_scalar(rms[:, g, :], sums[:, g, NBLK:], 1.0 / 1024, k * EPS, ALU.mult, ALU.add
                                        ).then_inc(b.rms_step, 1)
            dve.wait_ge(b.rms_root, 1)
            nc.vector.reciprocal(rms[:, :, :], rms[:, :, :]).then_inc(b.rms_step, 1)
            dve.wait_ge(b.rms_step, 4)
            dve.wait_ge(b.fgain_in, 16)
            low_y(1, 0)
            finish(0, 0)
            finish(0, 1)
            with dve.Fori(1, STEPS) as m:
                for s in range(2):
                    low_y(m + s, 1 - s)
                    finish(m, s)

        @block.tensor
        def _(pe):
            def sum_squares():
                pe.wait_ge(*a.sq_added.at(NITER, 0))
                pe.wait_ge(*a.s_sel.at(NITER, 0))
                for g in range(2):
                    for t in range(NBLK):
                        last = nc.tensor.matmul(stat_ps[:, g * NBLK + t:g * NBLK + t + 1],
                                                acc_sq[:, (NQUART - 1) % 2, g, t * P:(t + 1) * P],
                                                ones[:, :], start=True, stop=True)
                last.then_inc(b.stat_done, 1)

            def chunk(s, e):
                g = e // (EC // 2)
                for j, (y, low) in enumerate(((y_hi, 0), (y_hi, 1), (y_lo, 0))):
                    for h in range(2):
                        last = nc.tensor.matmul(acc[:, s, g, h, :], y[s][:, e, :],
                                                wo(e, low)[:, h * (D // 2):(h + 1) * (D // 2)],
                                                start=(e % (EC // 2) == 0 and j == 0),
                                                stop=(e % (EC // 2) == EC // 2 - 1 and j == 2))
                if (e + 1) % (EC // 2) == 0:
                    last.then_inc(*b.product[s].one())

            pe.wait_ge(*b.y_low.at(0, 1))
            pe.wait_ge(*a.ring_act.at(NITER, 0))
            pe.wait_ge(*a.ring_dve.at(NITER, 0))
            for e in range(EC + LAG):
                if e == WSLOTS:
                    sum_squares()
                if e < EC:
                    pe.wait_ge(*b.wo_low.at(e, 1))
                    chunk(0, e)
                if e == LAG:
                    pe.wait_ge(*b.y_low.at(0, 2))
                    pe.wait_ge(b.rms_step, 1)
                    pe.wait_ge(*a.p_low.at(NITER, 0))
                    pe.wait_ge(*a.o_sum.at(NITER, 0))
                if e >= LAG:
                    chunk(1, e - LAG)
            with pe.Fori(1, STEPS) as m:
                for s in range(2):
                    pe.wait_ge(*b.y_low.at(m, s + 1))
                    pe.wait_ge(*b.added.at(m, 2 * s + 2 - 4))
                    for e in range(EC):
                        chunk(s, e)


def rope_tables():
    half = ROT // 2
    inv = np.float32(500000.0) ** (-np.arange(0, ROT, 2, dtype=np.float32) / np.float32(ROT))
    ang = np.arange(SEQ, dtype=np.float32)[None, :] * inv.astype(np.float32)[:, None]
    cos, sin = np.cos(ang), np.sin(ang)
    c = np.ones((P, SEQ), np.float32)
    s = np.zeros((P, SEQ), np.float32)
    for head in range(2):
        r = head * HD
        c[r:r + half], c[r + half:r + ROT] = cos, cos
        s[r:r + half], s[r + half:r + ROT] = -sin, sin
    return c, s


_INPUTS = ["x", "ln_gain", "w_in", "sinks", "conv_w", "conv_b", "w_rgate", "b_rgate", "w_igate", "b_igate",
           "lru_lambda", "attn_out_gain", "lru_out_gain", "w_out", "final_gain"]


def constants():
    cos, sin = rope_tables()
    query, key = np.arange(BLK)[:, None], np.arange(BLK)[None, :]
    prev = key > query
    cap = np.full((P, 2, BLK), BIG, np.float32)
    cap[:, 0, :][prev] = NEG
    return {"rope_cos": cos, "rope_sin": sin, "first_cap": cap,
            "identity": np.eye(P, dtype=np.float32)}


def kernel(**inputs):
    import concourse.bacc as bacc
    from concourse.bass_utils import run_bass_kernel_spmd

    nc = bacc.Bacc("TRN2", target_bir_lowering=False, num_devices=1)
    arrays, args = {}, {}
    for name, a in {**{k: inputs[k] for k in _INPUTS}, **constants()}.items():
        a = np.ascontiguousarray(a)
        arrays[name + "_d"] = a
        args[name] = nc.dram_tensor(name + "_d", a.shape, mybir.dt.from_np(a.dtype), kind="ExternalInput").ap()
    out = nc.dram_tensor("out_d", (1, SEQ, D), F32, kind="ExternalOutput").ap()
    hymba_kernel(nc, out=out, **args)
    r = run_bass_kernel_spmd(nc, [arrays], core_ids=[0])
    return r.results[0]["out_d"]
```
